# Optimizing a Trainium2 kernel written in Bass

```python
import jax, jax.numpy as jnp
from jax import lax
import numpy as np

D_MODEL = 1024
BATCH = 1
SEQ = 512
DEPTH = 2

HEAD_DIM = 64
ROPE_THETA = 10000.0
Q_BLOCK = 128
A_HEADS = 8
A_KV_HEADS = 2
A_WINDOW = 128
B_HEADS = 4
IDX_HEADS = 4
IDX_DIM = 64
IDX_TOPK_MAX = 256
IDX_W_SCALE = (IDX_HEADS * IDX_DIM) ** -0.5
C_HEADS = 4
C_NOPE = 64
C_ROPE = 32
C_V = 64
C_Q_RANK = 256
C_KV_RANK = 128
A_Q = A_HEADS * HEAD_DIM
A_KV = A_KV_HEADS * HEAD_DIM
B_Q = B_HEADS * HEAD_DIM
B_KV = HEAD_DIM
IDX_Q = IDX_HEADS * IDX_DIM
IN_SPLITS = (A_Q, A_KV, A_KV, B_Q, B_KV, B_KV, IDX_Q, IDX_DIM, IDX_HEADS, C_Q_RANK, C_KV_RANK, C_ROPE)
IN_COLS = A_Q + 2 * A_KV + B_Q + 2 * B_KV + IDX_Q + IDX_DIM + IDX_HEADS + C_Q_RANK + C_KV_RANK + C_ROPE
MIX_WIDTH = A_HEADS * HEAD_DIM + B_HEADS * HEAD_DIM + C_HEADS * C_V
N_EXPERTS = 16
N_GROUPS = 4
EXPERTS_PER_GROUP = N_EXPERTS // N_GROUPS
TOP_K = 2
D_EXPERT = 256
DEEPNORM_ALPHA = (2 * DEPTH) ** 0.25
DEEPNORM_BETA = (8 * DEPTH) ** -0.25
LN_EPS = 1e-5
RMS_EPS = 1e-6


def rope_tables(pos, dim):
    inv = 1.0 / (ROPE_THETA ** (jnp.arange(0, dim, 2, dtype=jnp.float32) / dim))
    ang = pos.astype(jnp.float32)[:, None] * inv[None, :]
    return jnp.cos(ang), jnp.sin(ang)

def apply_rope(x, cos, sin):
    d2 = x.shape[-1] // 2
    shape = (1, cos.shape[0]) + (1,) * (x.ndim - 3) + (d2,)
    c = cos.reshape(shape)
    s = sin.reshape(shape)
    xf = x.astype(jnp.float32)
    x1, x2 = xf[..., :d2], xf[..., d2:]
    return jnp.concatenate([x1 * c - x2 * s, x2 * c + x1 * s], axis=-1).astype(x.dtype)

def layer_norm(x, g, b):
    xf = x.astype(jnp.float32)
    mu = jnp.mean(xf, axis=-1, keepdims=True)
    var = jnp.mean(jnp.square(xf - mu), axis=-1, keepdims=True)
    return ((xf - mu) * lax.rsqrt(var + LN_EPS) * g.astype(jnp.float32) + b.astype(jnp.float32)).astype(x.dtype)

def rms_norm(x, g):
    xf = x.astype(jnp.float32)
    return (xf * lax.rsqrt(jnp.mean(jnp.square(xf), axis=-1, keepdims=True) + RMS_EPS) * g.astype(jnp.float32)).astype(x.dtype)

def split_cols(h):
    offs = np.cumsum(IN_SPLITS)[:-1].tolist()
    return jnp.split(h, offs, axis=-1)

def to_blocks(t):
    b, s = t.shape[0], t.shape[1]
    return jnp.moveaxis(t.reshape((b, s // Q_BLOCK, Q_BLOCK) + t.shape[2:]), 1, 0)

def sliding_window_sink_attn(q, k, v, sinks):
    B, S, Hq, D = q.shape
    Hkv = k.shape[2]
    G = Hq // Hkv
    W = A_WINDOW
    nb = S // W
    qb = q.reshape(B, nb, W, Hkv, G, D)

    def band(t):
        tb = t.reshape(B, nb, W, Hkv, D)
        prev = jnp.pad(tb[:, :-1], ((0, 0), (1, 0), (0, 0), (0, 0), (0, 0)))
        return jnp.concatenate([prev, tb], axis=2)

    kb, vb = band(k), band(v)
    s = jnp.einsum('bnqhgd,bnkhd->bnhgqk', qb, kb).astype(jnp.float32) * (D ** -0.5)
    qi = jnp.arange(W)[:, None]
    kj = jnp.arange(2 * W)[None, :]
    diff = qi + W - kj
    in_window = (diff >= 0) & (diff < W)
    not_pad = (jnp.arange(nb)[:, None, None] > 0) | (kj[None] >= W)
    mask = (in_window[None] & not_pad)[None, :, None, None]
    s = jnp.where(mask, s, -jnp.inf)
    sink = jnp.broadcast_to(sinks.astype(jnp.float32).reshape(1, 1, Hkv, G, 1, 1), s.shape[:-1] + (1,))
    p = jax.nn.softmax(jnp.concatenate([s, sink], axis=-1), axis=-1)[..., :-1]
    o = jnp.einsum('bnhgqk,bnkhd->bnqhgd', p.astype(v.dtype), vb)
    return o.reshape(B, S, Hq * D)

def indexer_sparse_attn(q, k, v, q_idx, k_idx, w_idx):
    B, S, H, D = q.shape
    topk = min(IDX_TOPK_MAX, S // 4)
    nb = S // Q_BLOCK
    key_pos = jnp.arange(S)
    bidx = jnp.arange(B)[:, None]

    def block_fn(args):
        qb, qib, wb, t0 = args
        tpos = t0 + jnp.arange(Q_BLOCK)
        logits = jnp.einsum('bthd,bsd->bths', qib, k_idx).astype(jnp.float32)
        score = jnp.einsum('bth,bths->bts', wb.astype(jnp.float32), jax.nn.relu(logits))
        causal = key_pos[None, :] <= tpos[:, None]
        score = jnp.where(causal[None], score, -jnp.inf)
        _, idx = lax.top_k(score, topk)
        flat = idx.reshape(B, Q_BLOCK * topk)
        kg = k[bidx, flat].reshape(B, Q_BLOCK, topk, D)
        vg = v[bidx, flat].reshape(B, Q_BLOCK, topk, D)
        valid = idx <= tpos[None, :, None]
        s = jnp.einsum('bthd,btkd->bthk', qb, kg).astype(jnp.float32) * (D ** -0.5)
        s = jnp.where(valid[:, :, None, :], s, -jnp.inf)
        p = jax.nn.softmax(s, axis=-1)
        return jnp.einsum('bthk,btkd->bthd', p.astype(vg.dtype), vg)

    t0s = jnp.arange(nb, dtype=jnp.int32) * Q_BLOCK
    out = lax.map(block_fn, (to_blocks(q), to_blocks(q_idx), to_blocks(w_idx), t0s))
    return jnp.moveaxis(out, 0, 1).reshape(B, S, H * D)

def mla_attn(q_nope, q_rope, k_nope, k_rope, v):
    B, S, H, Dv = v.shape
    scale = (q_nope.shape[-1] + q_rope.shape[-1]) ** -0.5
    nb = S // Q_BLOCK
    key_pos = jnp.arange(S)

    def block_fn(args):
        qn, qr, t0 = args
        tpos = t0 + jnp.arange(Q_BLOCK)
        s = (jnp.einsum('bthd,bshd->bhts', qn, k_nope) + jnp.einsum('bthd,bsd->bhts', qr, k_rope)).astype(jnp.float32) * scale
        causal = key_pos[None, :] <= tpos[:, None]
        s = jnp.where(causal[None, None], s, -jnp.inf)
        p = jax.nn.softmax(s, axis=-1)
        return jnp.einsum('bhts,bshd->bthd', p.astype(v.dtype), v)

    t0s = jnp.arange(nb, dtype=jnp.int32) * Q_BLOCK
    out = lax.map(block_fn, (to_blocks(q_nope), to_blocks(q_rope), t0s))
    return jnp.moveaxis(out, 0, 1).reshape(B, S, H * Dv)

def moe_ffn(x, w_router, router_bias, w_gate, w_up, w_down):
    B, S, D = x.shape
    N = B * S
    xt = x.reshape(N, D)
    scores = jax.nn.sigmoid(jnp.dot(xt, w_router).astype(jnp.float32))
    biased = (scores + router_bias.astype(jnp.float32)).reshape(N, N_GROUPS, EXPERTS_PER_GROUP)
    group_score = jnp.sum(lax.top_k(biased, TOP_K)[0], axis=-1)
    g_sel = jnp.argmax(group_score, axis=-1)
    in_group = jnp.take_along_axis(biased, g_sel[:, None, None], axis=1)[:, 0]
    _, local = lax.top_k(in_group, TOP_K)
    expert_idx = g_sel[:, None] * EXPERTS_PER_GROUP + local
    w = jnp.take_along_axis(scores, expert_idx, axis=1)
    w = w / jnp.sum(w, axis=-1, keepdims=True)
    gates = jnp.sum(jax.nn.one_hot(expert_idx, N_EXPERTS, dtype=jnp.float32) * w[..., None], axis=1)
    h = jax.nn.silu(jnp.einsum('nd,edf->enf', xt, w_gate)) * jnp.einsum('nd,edf->enf', xt, w_up)
    h = h * gates.T.astype(h.dtype)[:, :, None]
    y = jnp.einsum('enf,efd->nd', h, w_down)
    return y.reshape(B, S, D)

def first_inputs(seed: int = 0) -> dict:
    key = jax.random.key(seed)
    ks = jax.random.split(key, 20)
    f32 = jnp.float32
    nrm = lambda k, shape, scale: jax.random.normal(k, shape, f32) * scale
    return {
        'x': nrm(ks[0], (BATCH, SEQ, D_MODEL), 1.0),
        'w_in': nrm(ks[1], (DEPTH, D_MODEL, IN_COLS), D_MODEL ** -0.5),
        'attn_sinks': nrm(ks[2], (DEPTH, A_HEADS), 0.5),
        'c_q_norm_g': 1.0 + nrm(ks[3], (DEPTH, C_Q_RANK), 0.02),
        'c_kv_norm_g': 1.0 + nrm(ks[4], (DEPTH, C_KV_RANK), 0.02),
        'w_uq': nrm(ks[5], (DEPTH, C_Q_RANK, C_HEADS * (C_NOPE + C_ROPE)), C_Q_RANK ** -0.5),
        'w_ukv': nrm(ks[6], (DEPTH, C_KV_RANK, C_HEADS * (C_NOPE + C_V)), C_KV_RANK ** -0.5),
        'w_out': nrm(ks[7], (DEPTH, MIX_WIDTH, D_MODEL), DEEPNORM_BETA * MIX_WIDTH ** -0.5),
        'ln1_g': 1.0 + nrm(ks[8], (DEPTH, D_MODEL), 0.02),
        'ln1_b': nrm(ks[9], (DEPTH, D_MODEL), 0.02),
        'w_router': nrm(ks[10], (D_MODEL, N_EXPERTS), D_MODEL ** -0.5),
        'router_bias': nrm(ks[11], (N_EXPERTS,), 0.01),
        'w_gate': nrm(ks[12], (DEPTH, N_EXPERTS, D_MODEL, D_EXPERT), D_MODEL ** -0.5),
        'w_up': nrm(ks[13], (DEPTH, N_EXPERTS, D_MODEL, D_EXPERT), D_MODEL ** -0.5),
        'w_down': nrm(ks[14], (DEPTH, N_EXPERTS, D_EXPERT, D_MODEL), DEEPNORM_BETA * D_EXPERT ** -0.5),
        'ln2_g': 1.0 + nrm(ks[15], (DEPTH, D_MODEL), 0.02),
        'ln2_b': nrm(ks[16], (DEPTH, D_MODEL), 0.02),
    }

def first_block(x, w_in, attn_sinks, c_q_norm_g, c_kv_norm_g, w_uq, w_ukv, w_out, ln1_g, ln1_b, w_router, router_bias, w_gate, w_up, w_down, ln2_g, ln2_b):
    B, S, _ = x.shape
    pos = jnp.arange(S)
    cos_h, sin_h = rope_tables(pos, HEAD_DIM)
    cos_r, sin_r = rope_tables(pos, C_ROPE)
    for l in range(DEPTH):
        h = jnp.einsum('bsd,dc->bsc', x, w_in[l])
        a_q, a_k, a_v, b_q, b_k, b_v, i_q, i_k, i_w, c_q, c_kv, c_kr = split_cols(h)
        o_a = sliding_window_sink_attn(
            apply_rope(a_q.reshape(B, S, A_HEADS, HEAD_DIM), cos_h, sin_h),
            apply_rope(a_k.reshape(B, S, A_KV_HEADS, HEAD_DIM), cos_h, sin_h),
            a_v.reshape(B, S, A_KV_HEADS, HEAD_DIM), attn_sinks[l])
        o_b = indexer_sparse_attn(
            apply_rope(b_q.reshape(B, S, B_HEADS, HEAD_DIM), cos_h, sin_h),
            apply_rope(b_k, cos_h, sin_h), b_v,
            apply_rope(i_q.reshape(B, S, IDX_HEADS, IDX_DIM), cos_h, sin_h),
            apply_rope(i_k, cos_h, sin_h), i_w * IDX_W_SCALE)
        q_c = jnp.einsum('bsr,rc->bsc', rms_norm(c_q, c_q_norm_g[l]), w_uq[l]).reshape(B, S, C_HEADS, C_NOPE + C_ROPE)
        kv_c = jnp.einsum('bsr,rc->bsc', rms_norm(c_kv, c_kv_norm_g[l]), w_ukv[l]).reshape(B, S, C_HEADS, C_NOPE + C_V)
        o_c = mla_attn(q_c[..., :C_NOPE], apply_rope(q_c[..., C_NOPE:], cos_r, sin_r),
                       kv_c[..., :C_NOPE], apply_rope(c_kr, cos_r, sin_r), kv_c[..., C_NOPE:])
        mix = jnp.concatenate([o_a, o_b, o_c], axis=-1)
        x = layer_norm(DEEPNORM_ALPHA * x + jnp.einsum('bsm,md->bsd', mix, w_out[l]), ln1_g[l], ln1_b[l])
        x = layer_norm(DEEPNORM_ALPHA * x + moe_ffn(x, w_router, router_bias, w_gate[l], w_up[l], w_down[l]), ln2_g[l], ln2_b[l])
    return x


N_A_LAYERS = DEPTH // 2
N_B_LAYERS = DEPTH - N_A_LAYERS

D_FF = ((8 * D_MODEL // 3 + 255) // 256) * 256
N_FFN_PER_LAYER = 2

POOL_WINDOWS = (2, 4, 8, 16)
POOL_GROUPS = len(POOL_WINDOWS)
POOL_GROUP_DIM = D_MODEL // POOL_GROUPS

ATTN_GROUPS = ((128, 1), (512, 4), (2048, 16))
N_ATTN_GROUPS = len(ATTN_GROUPS)
HEADS_PER_GROUP = D_MODEL // (2 * HEAD_DIM)
QKV_WIDTH = N_ATTN_GROUPS * HEADS_PER_GROUP * HEAD_DIM
O_WIDTH = HEADS_PER_GROUP * HEAD_DIM

N_NORMS_PER_LAYER = 6
NEG_BIG = -1e30


def rms_norm_2(x, gain):
    x32 = x.astype(jnp.float32)
    y = x32 * lax.rsqrt(jnp.mean(x32 * x32, axis=-1, keepdims=True) + RMS_EPS) * gain.astype(jnp.float32)
    return y.astype(x.dtype)

def swiglu(h, w_gate, w_up, w_down):
    return (jax.nn.silu(h @ w_gate) * (h @ w_up)) @ w_down

def rope_tables_2(positions):
    inv_freq = ROPE_THETA ** (-jnp.arange(0, HEAD_DIM, 2, dtype=jnp.float32) / HEAD_DIM)
    ang = positions.astype(jnp.float32)[..., None] * inv_freq
    return jnp.cos(ang), jnp.sin(ang)

def apply_rope_2(x, cos, sin):
    extra = x.ndim - 3
    shape = cos.shape[:2] + (1,) * extra + cos.shape[-1:]
    c = cos.reshape(shape)
    s = sin.reshape(shape)
    x32 = x.astype(jnp.float32)
    x1, x2 = jnp.split(x32, 2, axis=-1)
    out = jnp.concatenate([x1 * c - x2 * s, x2 * c + x1 * s], axis=-1)
    return out.astype(x.dtype)

def pool_mixer(h, w_in, w_group, scale, w_out):
    B, S, _ = h.shape
    u = h @ w_in
    u32 = u.astype(jnp.float32)
    csum = jnp.cumsum(u32, axis=1)
    t = jnp.arange(S)
    pooled = []
    for g, w in enumerate(POOL_WINDOWS):
        lo, hi = g * POOL_GROUP_DIM, (g + 1) * POOL_GROUP_DIM
        c = csum[..., lo:hi]
        c_prev = jnp.pad(c, ((0, 0), (w, 0), (0, 0)))[:, :S]
        count = jnp.minimum(t + 1, w).astype(jnp.float32)[None, :, None]
        pooled.append((c - c_prev) / count - u32[..., lo:hi])
    p = jnp.stack(pooled, axis=2).astype(u.dtype)
    y = jnp.einsum('bsgc,gcd->bsgd', p, w_group).reshape(B, S, D_MODEL) * scale
    return y @ w_out

def dilated_window_attention(q, k, v, window, dilation):
    B, S, H, Dh = q.shape
    blk = window // dilation
    span = blk * dilation
    s_pad = -(-S // span) * span
    nb = s_pad // span

    def split(a):
        a = jnp.pad(a, ((0, 0), (0, s_pad - S), (0, 0), (0, 0)))
        return a.reshape(B, nb, blk, dilation, H, Dh)

    def with_prev(a):
        prev = jnp.pad(a[:, :-1], ((0, 0), (1, 0), (0, 0), (0, 0), (0, 0), (0, 0)))
        return jnp.concatenate([prev, a], axis=2)

    qb = split(q)
    kc = with_prev(split(k))
    vc = with_prev(split(v))
    s = jnp.einsum('bnqrhd,bnkrhd->bnrhqk', qb, kc, preferred_element_type=jnp.float32) * (Dh ** -0.5)
    qi = jnp.arange(blk)[:, None]
    kj = jnp.arange(2 * blk)[None, :]
    band = (kj >= qi) & (kj <= qi + blk)
    valid_prev = (jnp.arange(nb)[:, None, None] > 0) | (kj[None] >= blk)
    mask = band[None] & valid_prev
    s = jnp.where(mask[None, :, None, None], s, NEG_BIG)
    m = jnp.max(s, axis=-1, keepdims=True)
    p = jnp.exp(s - m)
    den = jnp.sum(p, axis=-1, keepdims=True)
    o = jnp.einsum('bnrhqk,bnkrhd->bnqrhd', (p / den).astype(v.dtype), vc)
    lse = (m + jnp.log(den))[..., 0]
    o = o.reshape(B, s_pad, H, Dh)[:, :S]
    lse = lse.transpose(0, 1, 4, 2, 3).reshape(B, s_pad, H)[:, :S]
    return o, lse

def shared_kv(h, kv_gain, w_k, w_v, cos, sin):
    B, S, _ = h.shape
    hk = rms_norm_2(h, kv_gain)
    k = (hk @ w_k).reshape(B, S, N_ATTN_GROUPS, HEADS_PER_GROUP, HEAD_DIM)
    v = (hk @ w_v).reshape(B, S, N_ATTN_GROUPS, HEADS_PER_GROUP, HEAD_DIM)
    return apply_rope_2(k, cos, sin), v

def dilated_mixer(h, cos, sin, w_q, k_sh, v_sh, w_o):
    B, S, _ = h.shape
    q = (h @ w_q).reshape(B, S, N_ATTN_GROUPS, HEADS_PER_GROUP, HEAD_DIM)
    q = apply_rope_2(q, cos, sin)
    outs, lses = [], []
    for g, (window, dilation) in enumerate(ATTN_GROUPS):
        o, l = dilated_window_attention(q[:, :, g], k_sh[:, :, g], v_sh[:, :, g], window, dilation)
        outs.append(o)
        lses.append(l)
    wts = jax.nn.softmax(jnp.stack(lses, axis=0), axis=0)
    o = jnp.sum(wts[..., None] * jnp.stack(outs, axis=0).astype(jnp.float32), axis=0).astype(h.dtype)
    return o.reshape(B, S, O_WIDTH) @ w_o

def second_inputs(seed: int = 0) -> dict:
    key = jax.random.key(seed)
    ks = jax.random.split(key, 16)
    f32 = jnp.float32

    def w(k, shape, fan_in):
        return jax.random.normal(k, shape, f32) * (fan_in ** -0.5)

    x = jax.random.normal(ks[0], (BATCH, SEQ, D_MODEL), f32)
    offset = jax.random.randint(ks[1], (BATCH, 1), 0, 1024, dtype=jnp.int32)
    positions = (jnp.arange(SEQ, dtype=jnp.int32)[None, :] + offset).astype(jnp.int32)
    norm_gain = 1.0 + 0.05 * jax.random.normal(ks[2], (DEPTH, N_NORMS_PER_LAYER, D_MODEL), f32)
    ffn_w_gate = w(ks[3], (DEPTH, N_FFN_PER_LAYER, D_MODEL, D_FF), D_MODEL)
    ffn_w_up = w(ks[4], (DEPTH, N_FFN_PER_LAYER, D_MODEL, D_FF), D_MODEL)
    ffn_w_down = w(ks[5], (DEPTH, N_FFN_PER_LAYER, D_FF, D_MODEL), D_FF)
    pool_w_in = w(ks[6], (N_A_LAYERS, D_MODEL, D_MODEL), D_MODEL)
    pool_w_group = w(ks[7], (N_A_LAYERS, POOL_GROUPS, POOL_GROUP_DIM, POOL_GROUP_DIM), POOL_GROUP_DIM)
    pool_scale = 1.0 + 0.1 * jax.random.normal(ks[8], (N_A_LAYERS, D_MODEL), f32)
    pool_w_out = w(ks[9], (N_A_LAYERS, D_MODEL, D_MODEL), D_MODEL)
    kv_norm_gain = 1.0 + 0.05 * jax.random.normal(ks[10], (D_MODEL,), f32)
    w_k = w(ks[11], (D_MODEL, QKV_WIDTH), D_MODEL)
    w_v = w(ks[12], (D_MODEL, QKV_WIDTH), D_MODEL)
    attn_w_q = w(ks[13], (N_B_LAYERS, D_MODEL, QKV_WIDTH), D_MODEL)
    attn_w_o = w(ks[14], (N_B_LAYERS, O_WIDTH, D_MODEL), O_WIDTH)
    return {
        "x": x, "positions": positions, "norm_gain": norm_gain,
        "ffn_w_gate": ffn_w_gate, "ffn_w_up": ffn_w_up, "ffn_w_down": ffn_w_down,
        "pool_w_in": pool_w_in, "pool_w_group": pool_w_group, "pool_scale": pool_scale,
        "pool_w_out": pool_w_out, "kv_norm_gain": kv_norm_gain, "w_k": w_k, "w_v": w_v,
        "attn_w_q": attn_w_q, "attn_w_o": attn_w_o,
    }

def second_block(x, positions, norm_gain, ffn_w_gate, ffn_w_up, ffn_w_down, pool_w_in, pool_w_group,
              pool_scale, pool_w_out, kv_norm_gain, w_k, w_v, attn_w_q, attn_w_o):
    cos, sin = rope_tables_2(positions)
    h = x
    k_sh = None
    v_sh = None
    for layer in range(DEPTH):
        g = norm_gain[layer]
        f = swiglu(rms_norm_2(h, g[0]), ffn_w_gate[layer, 0], ffn_w_up[layer, 0], ffn_w_down[layer, 0])
        h = h + 0.5 * rms_norm_2(f, g[1])
        hm = rms_norm_2(h, g[2])
        if layer < N_A_LAYERS:
            mix = pool_mixer(hm, pool_w_in[layer], pool_w_group[layer], pool_scale[layer], pool_w_out[layer])
        else:
            b = layer - N_A_LAYERS
            mix = dilated_mixer(hm, cos, sin, attn_w_q[b], k_sh, v_sh, attn_w_o[b])
        h = h + rms_norm_2(mix, g[3])
        f = swiglu(rms_norm_2(h, g[4]), ffn_w_gate[layer, 1], ffn_w_up[layer, 1], ffn_w_down[layer, 1])
        h = h + 0.5 * rms_norm_2(f, g[5])
        if layer == N_A_LAYERS - 1:
            k_sh, v_sh = shared_kv(h, kv_norm_gain, w_k, w_v, cos, sin)
    return h


def setup_inputs(seed=0):
    out = dict(first_inputs(seed))
    for name, value in second_inputs(seed + 1).items():
        if name != "x":
            out[name + "_2"] = value
    return out


def reference(
    x, w_in, attn_sinks, c_q_norm_g, c_kv_norm_g, w_uq, w_ukv, w_out, ln1_g, ln1_b, w_router,
    router_bias, w_gate, w_up, w_down, ln2_g, ln2_b, positions_2, norm_gain_2, ffn_w_gate_2,
    ffn_w_up_2, ffn_w_down_2, pool_w_in_2, pool_w_group_2, pool_scale_2, pool_w_out_2,
    kv_norm_gain_2, w_k_2, w_v_2, attn_w_q_2, attn_w_o_2,
):
    x = first_block(
        x, w_in, attn_sinks, c_q_norm_g, c_kv_norm_g, w_uq, w_ukv, w_out, ln1_g, ln1_b,
        w_router, router_bias, w_gate, w_up, w_down, ln2_g, ln2_b,
    )
    return second_block(
        x, positions_2, norm_gain_2, ffn_w_gate_2, ffn_w_up_2, ffn_w_down_2, pool_w_in_2,
        pool_w_group_2, pool_scale_2, pool_w_out_2, kv_norm_gain_2, w_k_2, w_v_2, attn_w_q_2,
        attn_w_o_2,
    )


_drawn_inputs = setup_inputs


def setup_inputs(seed=0):
    import zlib

    import numpy as np

    out = dict(_drawn_inputs(seed))
    spreads = {}
    factors = {'attn_sinks': 6.903, 'c_q_norm_g': 8.0, 'c_kv_norm_g': 8.0}
    for name, (base, spread) in spreads.items():
        noise = np.random.default_rng([zlib.crc32(name.encode()), seed]).standard_normal(out[name].shape)
        drawn = base * np.exp(spread * noise) if base else spread * noise
        out[name] = __import__('jax').numpy.asarray(drawn.astype(out[name].dtype))
    for name, factor in factors.items():
        out[name] = (out[name] * factor).astype(out[name].dtype)
    return out
```

```python
from contextlib import ExitStack

import numpy as np

import concourse.bass as bass
from concourse import mybir

F32, F32R, I32 = mybir.dt.float32, mybir.dt.float32r, mybir.dt.int32
ALU = mybir.AluOpType
ACT = mybir.ActivationFunctionType
AX = mybir.AxisListType

P, T, D, L = 128, 512, 1024, 2
KD = D // P
NT = T // P
HD = 64
ALPHA = float((2 * L) ** 0.25)
LN_EPS, RMS_EPS = 1e-5, 1e-6
TOPK = 128
E, TOKG = 16, 4
RING = 2
SLOT = 12 * P + 32
GK = 11
MASKED = -1.0e30
CAUSAL = -1.0e38
TAKEN = -3.0e38

J_ROPE, N_ROPE, J_UP, J_OUT, N_JOBS = 6, 11, 17, 18, 18 + 8 + 96
A_ROPE, A_UP, A_OUT, A_ROUTER, A_MOE, N_ACC = 6, 17, 25, 33, 34, 130
J_MOE = J_OUT + 8
UNITS = 64
UNITS_D = 64 * 1

W_FULL, W_KR, W_VA, W_VB, W_UP, W_DOWN = KD * P, KD * 64, KD * P, KD * 68, 12 * P, GK * P


TWO_PI = (6.28125, 0.0019350051879882812, 3.019916050561733e-07)
PI_BELOW = 3.1415925


def build_program(nc, a, out):
    gates_dram = nc.dram_tensor("gates_scratch", (E, T), F32, kind="Internal").ap()
    hk_dram = nc.dram_tensor("hk_scratch", (P, KD * T), F32, kind="Internal").ap()

    with ExitStack() as ctx:
        cursor = [(nc.sbuf_base + 63) // 64 * 64]

        def sb(name, shape, dt=F32):
            size = int(np.prod(shape[1:])) * 4
            t = nc.alloc_sbuf_tensor_at(name, shape, dt, offset=cursor[0])
            cursor[0] += (size + 31) // 32 * 32
            assert cursor[0] <= nc.sbuf_usable_end, name
            return t

        def flat(t):
            return t[:, :, :].rearrange("p k t -> p (k t)")

        def one(ap, i):
            return ap[bass.ds(i, 1)].rearrange("a p n -> (a p) n")

        x = sb("x", [P, KD, T])
        xs_hi, xs_lo = sb("xs_hi", [P, KD, T], F32R), sb("xs_lo", [P, KD, T], F32R)
        stage = sb("w_stage", [P, RING, SLOT])
        w_hi, w_lo = sb("w_hi", [P, RING, SLOT], F32R), sb("w_lo", [P, RING, SLOT], F32R)
        sum1, sum2, sq = sb("sum1", [P, T]), sb("sum2", [P, T]), sb("sq", [P, T])
        tmp, rot = sb("tmp", [P, 2, T]), sb("rotated", [P, 2, T])
        ident, ones = sb("ident", [P, P]), sb("ones", [P, 1])
        small = sb("small", [P, 64])
        ngain = sb("ngain", [P, 13, KD])
        col = sb("attn_cols", [P, 2, 8])
        region0 = cursor[0]
        tabs, tabc = sb("rope_tab", [P, 2, T]), sb("rope_tab_c", [P, T])
        mask_a, mask_c = sb("mask_a", [P, 2 * P]), sb("mask_c", [P, T])
        tri = sb("ties", [P, 16])
        wr = sb("w_router", [P, KD * E])
        wr_hi, wr_lo = sb("w_router_hi", [P, KD * E], F32R), sb("w_router_lo", [P, KD * E], F32R)
        rbias = sb("router_bias", [P, E])
        nsink, cg, lng = sb("neg_sinks", [P, 8]), sb("c_gain", [P, 3]), sb("ln_gain", [P, 4, KD])
        region1 = cursor[0]
        heads = sb("heads", [P, N_ROPE, T])
        cfeat = sb("c_feat", [P, 3, T])
        cs_hi, cs_lo = sb("c_hi", [P, 3, T], F32R), sb("c_lo", [P, 3, T], F32R)
        qc, kc, krope = sb("q_c", [P, 4, T]), sb("k_c", [P, 4, T]), sb("k_rope", [P, T])
        va, vb, vc = sb("v_a", [P, NT, P]), sb("v_b", [P, NT, 68]), sb("v_c", [P, NT, 256])
        maskb = sb("mask_b", [P, NT, T])
        rl = sb("index_relu", [P, 2, T])
        prob, probt = sb("prob", [P, 2, T]), sb("prob_t", [P, 2, T])
        max8 = sb("max8", [P, 8])
        cursor[0] = region1
        y = sb("y", [P, KD, T])
        gb, sg, hh = sb("gate_bcast", [P, T]), sb("silu", [P, T]), sb("hidden", [P, T])
        gates_t = sb("gates_t", [E, T])
        rt, pairs = sb("router_work", [P, 8, 64]), sb("router_pairs", [P, 2, 256])
        region2 = cursor[0]
        hs_hi, hs_lo = sb("h_hi", [P, GK, T], F32R), sb("h_lo", [P, GK, T], F32R)
        cursor[0] = region2
        u0, uw = sb("pool_u", [P, 16 + T]), sb("pool_sum", [P, 2, 16 + T])
        cnt, pgain = sb("pool_count", [P, 4, 16]), sb("pool_gain", [P, KD])
        po_hi, po_lo = sb("pooled_hi", [P, KD, T], F32R), sb("pooled_lo", [P, KD, T], F32R)
        cursor[0] = region0
        dq, dv = sb("d_heads", [P, 6, T]), sb("d_v", [P, NT, 384])
        dtab = sb("d_tab", [P, 2, T])
        dcol = sb("d_cols", [P, 2])
        mask_d = sb("mask_d", [P, NT, T + 2 * P])
        dprob, dprobt = sb("d_prob", [P, 2, 768]), sb("d_prob_t", [P, 768])
        dm_hi, dm_lo = sb("d_mix_hi", [P, 4, T], F32R), sb("d_mix_lo", [P, 4, T], F32R)
        region3 = cursor[0]
        ks_hi, ks_lo = sb("k_in_hi", [P, KD, T], F32R), sb("k_in_lo", [P, KD, T], F32R)
        cursor[0] = region3
        yd = sb("y_dilated", [P, KD, T])
        cursor[0] = region0
        hk_in = sb("hk_landing", [P, KD, T])

        ps = ctx.enter_context(nc.psum_tensor("ps", [P, 8, T], F32))
        STAT, RB, MB = 2, 3, 4

        sem = lambda name: ctx.enter_context(nc.semaphore(name))
        const_landed, layer_landed, late_landed = sem("const_landed"), sem("layer_landed"), sem("late_landed")
        w_landed = [sem(f"w_landed{s}") for s in range(RING)]
        w_hi_done = sem("w_hi_done")
        w_split = sem("w_split")
        acc_full = sem("acc_full")
        acc_free = [sem(f"acc_free{b}") for b in range(RING)]
        consts_made = sem("consts_made")
        tile_ready, xs_hi_done, xs_ready = sem("tile_ready"), sem("xs_hi_done"), sem("xs_ready")
        stat_in, stat_full, rstd_ready, rb_full = sem("stat_in"), sem("stat_full"), sem("rstd_ready"), sem("rb_full")
        rot_ready = sem("rot_ready")
        act_copied, heads_ready, qc_ready = sem("act_copied"), sem("heads_ready"), sem("qc_ready")
        kr_ready, kr_copied = sem("kr_ready"), sem("kr_copied")
        c_tile, c_hi_done, c_ready = sem("c_tile"), sem("c_hi_done"), sem("c_ready")
        ix_full, ix_relu, ix_used = sem("ix_full"), sem("ix_relu"), sem("ix_used")
        s_full, masked, p_exp, p_norm = sem("s_full"), sem("masked"), sem("p_exp"), sem("p_norm")
        pt_full, pt_copied = sem("pt_full"), sem("pt_copied")
        o_full, o_hi_done, o_split = sem("o_full"), sem("o_hi_done"), sem("o_split")
        h_ready, c_copied, wr_hi_done = sem("h_ready"), sem("c_copied"), sem("w_router_hi")
        wr_ready, r_tanh, gates_ready = sem("w_router_ready"), sem("router_tanh"), sem("gates_ready")
        gt_full, gt_copied, gates_stored = sem("gates_t_full"), sem("gates_t_copied"), sem("gates_stored")
        gb_landed, gb_used = sem("gate_landed"), sem("gate_used")
        sg_ready, sg_used = sem("silu_ready"), sem("silu_used")
        place_free = sem("place_free")
        hk_ready, hk_stored = sem("hk_ready"), sem("hk_stored")
        k_hi_done, k_ready = sem("k_hi_done"), sem("k_ready")
        tab_in, tab_done = sem("tab_in"), sem("tab_done")
        y_final, out_stored = sem("y_final"), sem("out_stored")

        JL, AL = N_JOBS // 2, N_ACC // 2
        SECOND = ["ffn0", "pool", "ffn1", "ffn2", "dilated", "ffn3"]
        PAIRS = {"f": 30, "p": 12, "d": 24}
        JS = {n: L * JL + sum(PAIRS[m[0]] for m in SECOND[:i]) for i, n in enumerate(SECOND)}
        AS = {n: L * AL + JS[n] - L * JL for n in SECOND}
        FILL = {"ffn0": 4, "pool": 5, "pool_out": 6, "ffn1": 7, "ffn2": 8, "dilated": 9, "ffn3": 10}
        NORM = {n: 6 + i for i, n in enumerate(
            ["ffn0", "ffn0_out", "pool", "pool_out", "ffn1", "ffn1_out", "keys", "ffn2", "ffn2_out",
             "dilated", "dilated_out", "ffn3", "ffn3_out"])}
        GAIN = {"ffn0": 0, "ffn0_out": 1, "pool": 2, "pool_out": 3, "ffn1": 4, "ffn1_out": 5, "ffn2": 6,
                "ffn2_out": 7, "dilated": 8, "dilated_out": 9, "ffn3": 10, "ffn3_out": 11, "keys": 12}
        COPIES = 12

        def units():
            for t in range(4):
                for h in range(2):
                    for qt in range(NT):
                        r, k0 = slice(64 * h, 64 * h + 64), max(qt - 1, 0)
                        yield dict(q=heads[r, t, qt * P:qt * P + P], keys=[(heads[r, 4, k0 * P:qt * P + P], 0)],
                                   W=(qt - k0 + 1) * P, mask=mask_a[:, (0 if qt else P):2 * P], scale=0.125,
                                   sink=4 * h + t, v=[va[:, b, 64 * h:64 * h + 64] for b in range(k0, qt + 1)],
                                   row=64 * h, tile=t, at=qt * P)
            for h in range(4):
                for qt in range(NT):
                    yield dict(q=qc[0:96, h, qt * P:qt * P + P], keys=[(kc[0:96, h, 0:qt * P + P], 0)],
                               W=(qt + 1) * P, mask=mask_c[:, (3 - qt) * P:T], scale=96 ** -0.5, sink=None,
                               v=[vc[:, b, 64 * h:64 * h + 64] for b in range(qt + 1)],
                               row=64 * (h % 2), tile=6 + h // 2, at=qt * P)
            for h in range(4):
                for qt in range(NT):
                    r = slice(64 * (h % 2), 64 * (h % 2) + 64)
                    yield dict(q=heads[r, 5 + h // 2, qt * P:qt * P + P], keys=[(heads[r, 7, 0:qt * P + P], 0)],
                               W=(qt + 1) * P, mask=maskb[:, qt, 0:(qt + 1) * P], scale=0.125, sink=None,
                               v=[vb[:, b, 0:64] for b in range(qt + 1)],
                               row=64 * (h % 2), tile=4 + h // 2, at=qt * P)

        def units_d():
            for h in range(2):
                r = slice(64 * h, 64 * h + 64)
                for c in range(4):
                    cols = slice(c * P, c * P + P)
                    yield dict(q=[dq[r, g, cols] for g in range(3)],
                               keys=[(dq[r, 3, :], 0), (dq[r, 4, cols], T), (dq[r, 5, cols], T + P)],
                               W=T + 2 * P, mask=c, scale=0.125, sink=None,
                               v=[dv[:, b, 64 * h:64 * h + 64] for b in range(4)]
                                 + [dv[:, c, g * P + 64 * h:g * P + 64 * h + 64] for g in (1, 2)],
                               row=64 * h, at=c * P)

        UN, UD = list(units()), list(units_d())
        IX = [(qt, h) for qt in range(1, NT) for h in range(4)]

        waited = sem("waited")

        def hold(eng, sem_, value):
            eng.wait_ge(sem_, value)
            eng.sem_inc(waited, 1)

        block = ctx.enter_context(nc.Block())

        @block.sync
        def _(sp):
            def load(jp, s, n, src):
                sp.wait_ge(w_split, 2 * jp + s + 1)
                sp.dma_start(stage[:, s, 0:n], src).then_inc(w_landed[s], 16)

            for dst, src in ((flat(x), a["xT"]), (flat(tabs), a["tab"]), (tabc[:, :], a["tabc"]),
                             (mask_a[:, :], a["mask_a"]), (mask_c[:, :], a["mask_c"]), (tri[:, :], a["tri"]),
                             (ident[:, :], a["ident"]), (wr[:, :], a["w_router"]),
                             (rbias[:, :].rearrange("p (a n) -> p a n", a=1), a["rbias"].partition_broadcast(P)), (flat(ngain), a["ngain"])):
                sp.dma_start(dst, src).then_inc(const_landed, 16)
            with sp.Fori(0, L) as l:
                j = l * JL
                for i in range(2):
                    load(j, i, W_FULL, one(a["w_in"], l * 15 + i))
                sp.wait_ge(place_free, l + 1)
                sp.dma_start(nsink[:, :].rearrange("p (a n) -> p a n", a=1), a["nsink"][bass.ds(l, 1), :].partition_broadcast(P)).then_inc(layer_landed, 16)
                sp.dma_start(cg[:, :], one(a["c_g"], l)).then_inc(layer_landed, 16)
                sp.dma_start(flat(lng), one(a["ln"], l)).then_inc(layer_landed, 16)
                load(j + 1, 0, W_FULL, one(a["w_in"], l * 15 + 2))
                load(j + 1, 1, W_KR, one(a["w_kr"], l))
                load(j + 2, 0, W_VA, one(a["w_in"], l * 15 + 3))
                load(j + 2, 1, W_VB, one(a["w_vb"], l))
                with sp.Fori(0, 5) as i:
                    for s in range(2):
                        load(j + 3 + i, s, W_FULL, one(a["w_in"], l * 15 + 4 + s + 2 * i))
                load(j + 8, 0, W_FULL, one(a["w_in"], l * 15 + 14))
                load(j + 8, 1, W_UP, one(a["w_up"], l))
                with sp.Fori(0, 4) as i:
                    for s in range(2):
                        load(j + 9 + i, s, W_FULL, one(a["w_out"], l * 8 + 2 * i + s))
                with sp.Fori(0, 4) as q:
                    with sp.Fori(0, 8) as i:
                        for s in range(2):
                            load(j + J_MOE // 2 + q * 12 + i, s, W_FULL, one(a["w_gu"], l * 64 + q * 16 + 2 * i + s))
                    with sp.Fori(0, 4) as i:
                        for s in range(2):
                            load(j + J_MOE // 2 + 8 + q * 12 + i, s, W_FULL, one(a["w_dn"], l * 32 + q * 8 + 2 * i + s))
            for name in SECOND:
                j = JS[name]
                if name[0] == "f":
                    n = int(name[3])
                    for g in range(2):
                        with sp.Fori(0, GK) as i:
                            for s in range(2):
                                load(j + 15 * g + i, s, W_FULL, one(a["f_gu"], n * 44 + g * 22 + s + 2 * i))
                        with sp.Fori(0, 4) as i:
                            for s in range(2):
                                load(j + 15 * g + 11 + i, s, W_DOWN, one(a["f_dn"], n * 16 + g * 8 + s + 2 * i))
                elif name == "pool":
                    for s in range(2):
                        load(j, s, W_FULL, a["p_in"][s])
                    sp.wait_ge(place_free, L + 2)
                    sp.dma_start(flat(cnt), a["p_cnt"]).then_inc(late_landed, 16)
                    sp.dma_start(pgain[:, :], a["p_scale"]).then_inc(late_landed, 16)
                    for w, n, o, i0 in (("p_in", W_FULL, 0, 1), ("p_grp", 2 * P, 4, 0), ("p_out", W_FULL, 8, 0)):
                        with sp.Fori(i0, 4) as i:
                            for s in range(2):
                                load(j + o + i, s, n, one(a[w], 2 * i + s))
                else:
                    for s in range(2):
                        load(j, s, W_FULL, a["d_qk"][s])
                    sp.wait_ge(place_free, L + 3)
                    sp.wait_ge(hk_stored, 16)
                    for dst, src in ((flat(hk_in), hk_dram), (flat(mask_d), a["mask_d"]),
                                     (tmp[:, 0:1, :].bitcast(I32), a["pos"].partition_broadcast(P)), (dcol[:, :], a["dcol"])):
                        sp.dma_start(dst, src).then_inc(late_landed, 16)

                    def pair(p):
                        with sp.Fori(1, 3) as i:
                            for s in range(2):
                                load(j + p * 5 + i, s, W_FULL, one(a["d_qk"], p * 6 + 2 * i + s))
                        with sp.Fori(0, 2) as i:
                            for s in range(2):
                                load(j + p * 5 + 3 + i, s, KD * 96, one(a["d_v"], p * 4 + 2 * i + s))

                    with sp.Fori(0, 3) as p:
                        pair(p)
                        for s in range(2):
                            load(j + p * 5 + 5, s, W_FULL, one(a["d_qk"], p * 6 + 6 + s))
                    pair(3)
                    with sp.Fori(0, 4) as i:
                        for s in range(2):
                            load(j + 20 + i, s, 4 * P, one(a["d_out"], 2 * i + s))
            sp.wait_ge(y_final, 1)
            sp.dma_start(out, flat(x)).then_inc(out_stored, 16)
            sp.wait_ge(out_stored, 16)

        @block.gpsimd
        def _(pool):
            nc.gpsimd.memset(ones[:, :], 1.0).then_inc(consts_made, 1)
            with pool.Fori(0, L) as l:
                hold(pool, kr_ready, l + 1)
                for h in range(4):
                    nc.gpsimd.tensor_copy(kc[64:96, h, :], krope[64:96, :]).then_inc(kr_copied, 1)
                hold(pool, gt_copied, l + 1)
                pool.dma_start(gates_dram, gates_t[:, :]).then_inc(gates_stored, 16)
                hold(pool, gates_stored, l * 16 + 16)
                with pool.Fori(0, E) as e:
                    hold(pool, gb_used, l * E + e + 1)
                    pool.dma_start(gb[:, :].rearrange("p (a t) -> p a t", a=1), gates_dram[bass.ds(e, 1), :].partition_broadcast(P)).then_inc(gb_landed, 16)
            pool.wait_ge(hk_ready, 8)
            pool.dma_start(hk_dram, flat(y)).then_inc(hk_stored, 16)

        @block.tensor
        def _(pe):
            def three(o, lh, ll, rh, rl_, start, stop):
                pe.matmul(o, lh, rh, start=start, stop=False)
                pe.matmul(o, lh, rl_, start=False, stop=False)
                return pe.matmul(o, ll, rh, start=False, stop=stop)

            def begin(jp, s, ap, b):
                pe.wait_ge(w_split, 2 * jp + s + 1 + RING)
                pe.wait_ge(acc_free[b], ap + 1)

            def job(jp, s, ap, b, hi, lo, K=KD, M=P, waits=None):
                begin(jp, s, ap, b)
                for k in range(K):
                    if waits is not None:
                        pe.wait_ge(waits[0], waits[1] + k + 1)
                    last = three(ps[0:M, b, :], w_hi[:, s, k * M:k * M + M], w_lo[:, s, k * M:k * M + M],
                                 hi[:, k, :], lo[:, k, :], k == 0, k == K - 1)
                last.then_inc(acc_full, 1)

            def job_v(jp, s, ap, b, hi, lo, N):
                begin(jp, s, ap, b)
                for t in range(NT):
                    for k in range(KD):
                        last = three(ps[:, b, t * N:t * N + N], hi[:, k, t * P:t * P + P], lo[:, k, t * P:t * P + P],
                                     w_hi[:, s, k * N:k * N + N], w_lo[:, s, k * N:k * N + N], k == 0, k == KD - 1)
                last.then_inc(acc_full, 1)

            def stats(n, tables):
                pe.wait_ge(stat_in, n + 1)
                for i, t in enumerate(tables):
                    for q in range(NT):
                        last = pe.matmul(ps[:, STAT, 4 * i + q:4 * i + q + 1], t[:, q * P:q * P + P], ones[:, 0:1],
                                         start=True, stop=True)
                last.then_inc(stat_full, 1)

            def spread(n, banks):
                pe.wait_ge(rstd_ready, n + 1)
                for i, b in enumerate(banks):
                    for q in range(NT):
                        last = pe.matmul(ps[:, b, q * P:q * P + P],
                                         small[:, 4 * i + q:4 * i + q + 1].to_broadcast([P, P]), ident[:, :],
                                         start=True, stop=True)
                last.then_inc(rb_full, 1)

            def scores(u, n, ring, dn=None):
                un = u[n]
                b = 2 + ring * (n % 2)
                q = un["q"] if isinstance(un["q"], list) else [un["q"]]
                for i, (k, at) in enumerate(un["keys"]):
                    w = k.shape[-1]
                    last = pe.matmul(ps[:, b + at // T, at % T:at % T + w], q[i], k, start=True, stop=True)
                last.then_inc(s_full, 1)

            def transposes(un, n, c0, probs, bank):
                pe.wait_ge(p_norm, c0 + n + 1)
                for i in range(un["W"] // P):
                    last = pe.transpose(ps[:, bank + i // 4, (i % 4) * P:(i % 4) * P + P], probs[:, n % 2, i * P:i * P + P],
                                        ident[:, :])
                last.then_inc(pt_full, 1)

            def mix(un, n, c0, probs_t, o):
                pe.wait_ge(pt_copied, c0 + n + 1)
                if n >= 2:
                    pe.wait_ge(o_split, c0 + n - 1)
                nb = un["W"] // P
                for i in range(nb):
                    last = pe.matmul(o, un["v"][i], probs_t[:, i * P:i * P + P], start=(i == 0), stop=(i == nb - 1))
                last.then_inc(o_full, 1)

            pe.wait_ge(consts_made, 1)
            pe.wait_ge(const_landed, 160)
            with pe.Fori(0, L) as l:
                j, c = l * JL, l * AL
                for i in range(4):
                    job(j + i // 2, i % 2, c + i // 2, i % 2, xs_hi, xs_lo, M=64 if i == 3 else P,
                        waits=(xs_ready, l * 16) if i == 0 else None)
                job_v(j + 2, 0, c + 2, 0, xs_hi, xs_lo, P)
                job_v(j + 2, 1, c + 2, 1, xs_hi, xs_lo, 68)
                stats(3 * l, [sum2, sum1])
                with pe.Fori(0, 5) as i:
                    for s in range(2):
                        job(j + 3 + i, s, c + 3 + i, s, xs_hi, xs_lo)
                spread(3 * l, [RB, MB])
                job(j + 8, 0, c + 8, 0, xs_hi, xs_lo)
                pe.wait_ge(w_split, 2 * (j + 8) + 2 + RING)
                for i in range(4):
                    pe.wait_ge(acc_free[(i + 1) % 2], c + 8 + (i + 1) // 2 + 1)
                    for k in range(2):
                        if i == 0:
                            pe.wait_ge(c_ready, l * 3 + k + 1)
                        m = i * 2 * P + k * P
                        last = three(ps[:, (i + 1) % 2, :], w_hi[:, 1, m:m + P], w_lo[:, 1, m:m + P],
                                     cs_hi[:, k, :], cs_lo[:, k, :], k == 0, k == 1)
                    last.then_inc(acc_full, 1)
                pe.wait_ge(c_ready, l * 3 + 3)
                for i in range(2):
                    pe.wait_ge(acc_free[(i + 1) % 2], c + 10 + (i + 1) // 2 + 1)
                    m = 8 * P + i * P
                    three(ps[:, (i + 1) % 2, :], w_hi[:, 1, m:m + P], w_lo[:, 1, m:m + P],
                          cs_hi[:, 2, :], cs_lo[:, 2, :], True, True).then_inc(acc_full, 1)
                for i in range(2):
                    pe.wait_ge(acc_free[(i + 1) % 2], c + 11 + (i + 1) // 2 + 1)
                    for t in (2 * i, 2 * i + 1):
                        last = three(ps[:, (i + 1) % 2, 256 * (t % 2):256 * (t % 2) + 256],
                                     cs_hi[:, 2, t * P:t * P + P], cs_lo[:, 2, t * P:t * P + P],
                                     w_hi[:, 1, 10 * P:12 * P], w_lo[:, 1, 10 * P:12 * P], True, True)
                    last.then_inc(acc_full, 1)
                pe.wait_ge(heads_ready, l * N_ROPE + N_ROPE)
                for n, (qt, h) in enumerate(IX):
                    if n >= 2:
                        pe.wait_ge(ix_relu, l * len(IX) + n - 1)
                    r = slice(64 * (h % 2), 64 * (h % 2) + 64)
                    pe.matmul(ps[:, 2 + n % 2, 0:(qt + 1) * P], heads[r, 8 + h // 2, qt * P:qt * P + P],
                              heads[r, 10, 0:(qt + 1) * P], start=True, stop=True).then_inc(ix_full, 1)
                pe.wait_ge(ix_relu, l * len(IX) + len(IX))
                pe.wait_ge(act_copied, l * COPIES + COPIES)
                pe.wait_ge(qc_ready, l * 4 + 4)
                pe.wait_ge(kr_copied, l * 4 + 4)
                u0_ = l * UNITS
                scores(UN, 0, 1)
                scores(UN, 1, 1)
                for n, un in enumerate(UN):
                    transposes(un, n, u0_, prob, 4 + n % 2)
                    if n + 2 < UNITS:
                        scores(UN, n + 2, 1)
                    mix(un, n, u0_, probt[:, n % 2, :], ps[un["row"]:un["row"] + 64, 6 + n % 2, 0:P])
                hold(pe, o_split, u0_ + UNITS)
                with pe.Fori(0, 4) as i:
                    job(j + 9 + i, 0, c + 12 + i, 1, xs_hi, xs_lo)
                    job(j + 9 + i, 1, c + 13 + i, 0, xs_hi, xs_lo)
                stats(3 * l + 1, [sum2, sum1])
                spread(3 * l + 1, [RB, MB])
                pe.wait_ge(wr_ready, 1)
                pe.wait_ge(acc_free[1], c + 17)
                for k in range(KD):
                    pe.wait_ge(xs_ready, l * 16 + 8 + k + 1)
                for t in range(NT):
                    for k in range(KD):
                        last = three(ps[:, 1, t * E:t * E + E], xs_hi[:, k, t * P:t * P + P], xs_lo[:, k, t * P:t * P + P],
                                     wr_hi[:, k * E:k * E + E], wr_lo[:, k * E:k * E + E], k == 0, k == KD - 1)
                last.then_inc(acc_full, 1)
                pe.wait_ge(gates_ready, l + 1)
                for t in range(NT):
                    last = pe.transpose(ps[0:E, STAT, t * P:t * P + P], rt[:, 0, t * E:t * E + E], ident[:, :])
                last.then_inc(gt_full, 1)
                with pe.Fori(0, 4) as q:
                    jq, cq = j + J_MOE // 2 + q * 12, c + A_MOE // 2 + q * 12
                    with pe.Fori(0, 8) as i:
                        for s in range(2):
                            job(jq + i, s, cq + i, s, xs_hi, xs_lo)
                    with pe.Fori(0, 4) as i:
                        for s in range(2):
                            pe.wait_ge(h_ready, l * 32 + q * 8 + 8)
                            job(jq + 8 + i, s, cq + 8 + i, s, hs_hi, hs_lo)
                stats(3 * l + 2, [sum2, sum1])
                spread(3 * l + 2, [RB, MB])

            def dense(name):
                j, c, n = JS[name], AS[name], int(name[3])
                stats(NORM[name], [sum2])
                spread(NORM[name], [RB])
                for g in range(2):
                    if g == 0:
                        pe.wait_ge(xs_ready, FILL[name] * 8 + 8)
                    with pe.Fori(0, GK) as i:
                        for s in range(2):
                            job(j + 15 * g + i, s, c + 15 * g + i, s, xs_hi, xs_lo)
                    pe.wait_ge(h_ready, 64 + n * 22 + g * GK + GK)
                    with pe.Fori(0, 4) as i:
                        for s in range(2):
                            job(j + 15 * g + 11 + i, s, c + 15 * g + 11 + i, s, hs_hi, hs_lo, K=GK)
                stats(NORM[name + "_out"], [sum2])
                spread(NORM[name + "_out"], [RB])

            def pooling():
                j, c = JS["pool"], AS["pool"]
                stats(NORM["pool"], [sum2])
                spread(NORM["pool"], [RB])
                pe.wait_ge(xs_ready, FILL["pool"] * 8 + 8)
                with pe.Fori(0, 4) as i:
                    for s in range(2):
                        job(j + i, s, c + i, s, xs_hi, xs_lo)
                for g in range(4):
                    pe.wait_ge(k_ready, 2 * g + 2)
                    for s in range(2):
                        job(j + 4 + g, s, c + 4 + g, s, po_hi[:, 2 * g:2 * g + 2, :], po_lo[:, 2 * g:2 * g + 2, :], K=2)
                pe.wait_ge(xs_ready, FILL["pool_out"] * 8 + 8)
                with pe.Fori(0, 4) as i:
                    for s in range(2):
                        job(j + 8 + i, s, c + 8 + i, s, xs_hi, xs_lo)
                stats(NORM["pool_out"], [sum2])
                spread(NORM["pool_out"], [RB])

            def dilated():
                j, c = JS["dilated"], AS["dilated"]
                stats(NORM["dilated"], [sum2])
                spread(NORM["dilated"], [RB])
                pe.wait_ge(xs_ready, FILL["dilated"] * 8 + 8)
                pe.wait_ge(k_ready, 16)
                with pe.Fori(0, 4) as p:
                    jp, cp = j + p * 5, c + p * 5
                    for i in range(6):
                        hi, lo = (xs_hi, xs_lo) if i < 3 else (ks_hi, ks_lo)
                        job(jp + i // 2, i % 2, cp + i // 2, i % 2, hi, lo)
                    for i in range(4):
                        job_v(jp + 3 + i // 2, i % 2, cp + 3 + i // 2, i % 2, ks_hi, ks_lo, 96)
                    pe.wait_ge(heads_ready, L * N_ROPE + p * 6 + 6)
                    pe.wait_ge(act_copied, L * COPIES + p * 4 + 4)
                    c0 = L * UNITS + p * 8
                    scores(UD, 0, 2)
                    scores(UD, 1, 2)
                    for n, un in enumerate(UD):
                        if n >= 1:
                            pe.wait_ge(o_split, c0 + n)
                        transposes(un, n, c0, dprob, 6)
                        if n + 2 < 8:
                            scores(UD, n + 2, 2)
                        mix(un, n, c0, dprobt, ps[un["row"]:un["row"] + 64, 7, 2 * P:3 * P])
                pe.wait_ge(o_split, L * UNITS + 32)
                with pe.Fori(0, 4) as i:
                    for s in range(2):
                        job(j + 20 + i, s, c + 20 + i, s, dm_hi, dm_lo, K=4)
                stats(NORM["dilated_out"], [sum2])
                spread(NORM["dilated_out"], [RB])

            dense("ffn0")
            pooling()
            dense("ffn1")
            stats(NORM["keys"], [sum2])
            spread(NORM["keys"], [RB])
            dense("ffn2")
            dilated()
            dense("ffn3")

        @block.scalar
        def _(act):
            copy = lambda o, i: nc.scalar.activation(o, i, ACT.Copy)

            def split(jp, s, n, free_at=None):
                act.wait_ge(w_landed[s], 16 * jp + 16)
                if free_at is not None:
                    act.wait_ge(acc_full, free_at)
                copy(w_hi[:, s, 0:n], stage[:, s, 0:n]).then_inc(w_hi_done, 1)

            def fill(f, src=None, perm=False):
                for m in range(KD):
                    act.wait_ge(tile_ready, 8 * f + m + 1)
                    s_, d = (tmp[:, m % 2, :] if src is None else src(m)), xs_hi[:, m, :]
                    if perm:
                        s_, d = s_.rearrange("p (i c) -> p c i", c=4), d.rearrange("p (c i) -> p c i", c=4)
                    copy(d, s_).then_inc(xs_hi_done, 1)

            def rotate(c2, b, full):
                act.wait_ge(acc_full, c2 + 1)
                for h in range(4):
                    last = copy(rot[32 * h:32 * h + 32, b, :], ps[32 * (h ^ 1):32 * (h ^ 1) + 32, b, :])
                last.then_inc(rot_ready, 1)

            def exps(un, n, c0, probs):
                b = n % 2
                act.wait_ge(masked, c0 + n + 1)
                if un["sink"] is not None:
                    nc.scalar.activation(col[:, b, 2:3], nsink[:, un["sink"]:un["sink"] + 1], ACT.Exp,
                                         bias=col[:, b, 0:1], scale=-1.0)
                nc.scalar.activation(probs[:, b, 0:un["W"]], probs[:, b, 0:un["W"]], ACT.Exp, bias=col[:, b, 0:1],
                                     scale=-1.0, accum_out=col[:, b, 1:2]).then_inc(p_exp, 1)

            def attend(U, c0, probs, probs_t, t_bank, o_of, hi_of, one_t):
                N = len(U)
                exps(U[0], 0, c0, probs)
                for n in range(N + 1):
                    if n + 1 < N:
                        exps(U[n + 1], n + 1, c0, probs)
                    if n < N:
                        W = U[n]["W"]
                        act.wait_ge(pt_full, c0 + n + 1)
                        if n >= (1 if one_t else 2):
                            act.wait_ge(o_full, c0 + n - (0 if one_t else 1))
                        tb = t_bank(n)
                        src = ps[:, tb, 0:W] if W <= T else ps[:, tb:tb + 2, :].rearrange("p b t -> p (b t)")[:, 0:W]
                        copy(probs_t(n)[:, 0:W], src).then_inc(pt_copied, 1)
                    m = n if one_t else n - 1
                    if 0 <= m < N:
                        act.wait_ge(o_full, c0 + m + 1)
                        copy(hi_of(U[m]), o_of(U[m], m)).then_inc(o_hi_done, 1)

            def silu_pair(jp, ap, n, s0, s1):
                split(jp + 1, 0, s0, 2 * ap + 1)
                act.wait_ge(sg_used, n + 1)
                nc.scalar.activation(sg[:, :], ps[:, 0, :], ACT.Silu).then_inc(sg_ready, 1)
                act.drain().then_inc(acc_free[0], 1)
                split(jp + 1, 1, s1, 2 * ap + 2)

            split(0, 0, W_FULL)
            split(0, 1, W_FULL)
            act.wait_ge(const_landed, 160)
            copy(wr_hi[:, :], wr[:, :]).then_inc(wr_hi_done, 1)
            with act.Fori(0, L) as l:
                j, c = l * JL, l * AL
                act.preload_act_table(ACT.Exp)
                fill(2 * l, lambda m: x[:, m, :])
                for i in range(3):
                    split(j + 1 + i // 2, i % 2, (W_FULL, W_KR, W_VA)[i], 2 * c + i + 1)
                    act.wait_ge(acc_full, 2 * c + i + 1)
                    copy(cfeat[:, i, :], ps[:, i % 2, :]).then_inc(c_copied, 1)
                    act.drain().then_inc(acc_free[i % 2], 1)
                act.wait_ge(acc_full, 2 * c + 4)
                split(j + 2, 1, W_VB, 2 * c + 4)
                split(j + 3, 0, W_FULL, 2 * c + 5)
                copy(flat(va), ps[:, 0, :]).then_inc(act_copied, 1)
                act.drain().then_inc(acc_free[0], 1)
                split(j + 3, 1, W_FULL, 2 * c + 6)
                copy(flat(vb), ps[:, 1, 0:4 * 68]).then_inc(act_copied, 1)
                act.drain().then_inc(acc_free[1], 1)
                with act.Fori(0, 4) as i:
                    for s in range(2):
                        split(j + 4 + i, s, W_FULL, 2 * (c + 3 + i) + s + 1)
                        rotate(2 * (c + 3 + i) + s, s, True)
                for s in range(2):
                    split(j + 8, s, (W_FULL, W_UP)[s], 2 * (c + 7) + s + 1)
                    rotate(2 * (c + 7) + s, s, True)
                for i in range(3):
                    act.wait_ge(c_tile, 3 * l + i + 1)
                    copy(cs_hi[:, i, :], cfeat[:, i, :]).then_inc(c_hi_done, 1)
                split(j + 9, 0, W_FULL, 2 * c + 17)
                rotate(2 * c + 16, 0, True)
                for i in range(4):
                    act.wait_ge(acc_full, 2 * c + 18 + i)
                    copy(qc[0:64, i, :], ps[0:64, (i + 1) % 2, :]).then_inc(act_copied, 1)
                for i in range(2):
                    act.wait_ge(acc_full, 2 * c + 22 + i)
                    copy(kc[0:64, 2 * i, :], ps[0:64, (i + 1) % 2, :]).then_inc(act_copied, 1)
                    copy(kc[0:64, 2 * i + 1, :], ps[64:128, (i + 1) % 2, :]).then_inc(act_copied, 1)
                    act.drain().then_inc(acc_free[(i + 1) % 2], 1)
                for i in range(2):
                    act.wait_ge(acc_full, 2 * c + 24 + i)
                    copy(vc[:, 2 * i:2 * i + 2, :].rearrange("p a b -> p (a b)"), ps[:, (i + 1) % 2, :]).then_inc(act_copied, 1)
                    act.drain().then_inc(acc_free[(i + 1) % 2], 1)
                split(j + 9, 1, W_FULL, 2 * c + 25)
                for n, (qt, h) in enumerate(IX):
                    act.wait_ge(ix_full, l * len(IX) + n + 1)
                    if n >= 2:
                        act.wait_ge(ix_used, l * len(IX) + n - 1)
                    nc.scalar.activation(rl[:, n % 2, 0:(qt + 1) * P], ps[:, 2 + n % 2, 0:(qt + 1) * P], ACT.Relu,
                                         scale=1.0 / 16).then_inc(ix_relu, 1)
                attend(UN, l * UNITS, prob, lambda n: probt[:, n % 2, :], lambda n: 4 + n % 2,
                       lambda un, n: ps[un["row"]:un["row"] + 64, 6 + n % 2, 0:P],
                       lambda un: xs_hi[un["row"]:un["row"] + 64, un["tile"], un["at"]:un["at"] + P], False)
                with act.Fori(0, 4) as i:
                    for s in range(2):
                        split(j + 10 + i, s, W_FULL, 2 * (c + 12 + i) + s + 2)
                fill(2 * l + 1, lambda m: x[:, m, :])
                act.wait_ge(acc_full, 2 * c + 34)
                nc.scalar.activation(rt[:, 1, :], ps[:, 1, 0:NT * E], ACT.Tanh, scale=0.5).then_inc(r_tanh, 1)
                act.wait_ge(gt_full, l + 1)
                copy(gates_t[:, :], ps[0:E, STAT, :]).then_inc(gt_copied, 1)
                act.preload_act_table(ACT.Silu)
                with act.Fori(0, 4) as q:
                    jq, cq = j + J_MOE // 2 + q * 12, c + A_MOE // 2 + q * 12
                    with act.Fori(0, 8) as i:
                        silu_pair(jq + i, cq + i, l * 32 + q * 8 + i, W_FULL, W_FULL)
                    with act.Fori(0, 4) as i:
                        for s in range(2):
                            split(jq + 9 + i, s, W_FULL, 2 * (cq + 8 + i) + s + 1)

            def dense(name, last=False):
                j, c, n = JS[name], AS[name], int(name[3])
                fill(FILL[name])
                act.preload_act_table(ACT.Silu)
                for g in range(2):
                    jg, c_g, n_g = j + 15 * g, c + 15 * g, 64 + 22 * n + GK * g
                    with act.Fori(0, GK - 1) as i:
                        silu_pair(jg + i, c_g + i, n_g + i, W_FULL, W_FULL)
                    silu_pair(jg + 10, c_g + 10, n_g + 10, W_DOWN, W_DOWN)
                    with act.Fori(0, 3) as i:
                        for s in range(2):
                            split(jg + 12 + i, s, W_DOWN, 2 * (c_g + 11 + i) + s + 1)
                    if not (last and g == 1):
                        for s in range(2):
                            split(jg + 15, s, W_FULL, 2 * (c_g + 14) + s + 1)

            dense("ffn0")
            j, c = JS["pool"], AS["pool"]
            fill(FILL["pool"])
            for m in range(8):
                n_w = W_FULL if m < 6 else 2 * P
                split(j + 1 + m // 2, m % 2, n_w, 2 * c + m + 1)
                act.wait_ge(c_tile, 3 * L + m + 1)
                copy(po_hi[:, m, :], tmp[:, m % 2, :]).then_inc(k_hi_done, 1)
            for m in range(8):
                n_w = 2 * P if m < 6 else W_FULL
                split(j + 5 + m // 2, m % 2, n_w, 2 * c + 8 + m + 1)
                act.wait_ge(tile_ready, 8 * FILL["pool_out"] + m + 1)
                copy(xs_hi[:, m, :], tmp[:, m % 2, :]).then_inc(xs_hi_done, 1)
            with act.Fori(0, 4) as i:
                for s in range(2):
                    split(j + 9 + i, s, W_FULL, 2 * (c + 8 + i) + s + 1)
            dense("ffn1")
            dense("ffn2")
            j, c = JS["dilated"], AS["dilated"]
            for i in range(2):
                act.wait_ge(tab_in, i + 1)
                nc.scalar.activation(dtab[:, i, :], tmp[:, i, :], ACT.Sin).then_inc(tab_done, 1)
            act.wait_ge(late_landed, 16 * 6)
            for m in range(KD):
                copy(ks_hi[:, m, :].rearrange("p (c i) -> p c i", c=4),
                     hk_in[:, m, :].rearrange("p (i c) -> p c i", c=4)).then_inc(k_hi_done, 1)
            fill(FILL["dilated"], perm=True)
            act.preload_act_table(ACT.Exp)
            with act.Fori(0, 4) as p:
                jp, cp = j + p * 5, c + p * 5
                for i in range(6):
                    split(jp + 1 + i // 2, i % 2, W_FULL if i < 4 else KD * 96, 2 * cp + i + 1)
                    rotate(2 * cp + i, i % 2, True)
                for i in range(2):
                    split(jp + 4, i, KD * 96, 2 * cp + 7 + i)
                    copy(dv[:, :, 96 * i:96 * i + 96], ps[:, i, 0:384].rearrange("p (t n) -> p t n", t=4)).then_inc(act_copied, 1)
                    act.drain().then_inc(acc_free[i], 1)
                for i in range(2):
                    split(jp + 5, i, W_FULL, 2 * cp + 9 + i)
                    copy(dv[:, :, 96 * (i + 2):96 * (i + 2) + 96],
                         ps[:, i, 0:384].rearrange("p (t n) -> p t n", t=4)).then_inc(act_copied, 1)
                    act.drain().then_inc(acc_free[i], 1)
                attend(UD, L * UNITS + p * 8, dprob, lambda n: dprobt[:, :], lambda n: 6,
                       lambda un, n: ps[un["row"]:un["row"] + 64, 7, 2 * P:3 * P],
                       lambda un: dm_hi[un["row"]:un["row"] + 64, bass.ds(p, 1), un["at"]:un["at"] + P], True)
            with act.Fori(0, 3) as i:
                for s in range(2):
                    split(j + 21 + i, s, 4 * P, 2 * (c + 20 + i) + s + 1)
            for s in range(2):
                split(j + 24, s, W_FULL, 2 * (c + 23) + s + 1)
            dense("ffn3", last=True)
        @block.vector
        def _(v):
            V = nc.vector
            tt, ts, stt = V.tensor_tensor, V.tensor_scalar, V.scalar_tensor_tensor

            def split(jp, s, n):
                v.wait_ge(w_hi_done, 2 * jp + s + 1)
                tt(w_lo[:, s, 0:n], stage[:, s, 0:n], w_hi[:, s, 0:n].bitcast(F32), ALU.subtract).then_inc(w_split, 1)

            def fill(f, make, src=None, perm=False):
                for m in range(KD + 1):
                    if m < KD:
                        make(m)
                    if m >= 1:
                        v.wait_ge(xs_hi_done, 8 * f + m)
                        s_, hi, lo = (tmp[:, (m - 1) % 2, :] if src is None else src(m - 1)), xs_hi[:, m - 1, :], xs_lo[:, m - 1, :]
                        if perm:
                            s_, hi, lo = (s_.rearrange("p (i c) -> p c i", c=4), hi.rearrange("p (c i) -> p c i", c=4),
                                          lo.rearrange("p (c i) -> p c i", c=4))
                        tt(lo, s_, hi.bitcast(F32), ALU.subtract).then_inc(xs_ready, 1)

            def clear_sums():
                V.memset(sum1[:, :], 0.0)
                V.memset(sum2[:, :], 0.0)
                v.drain()

            def add_up(t, first=False, mean=False):
                v.drain()
                tt(sq3, t, t, ALU.mult)
                if mean:
                    tt(sum1_3, sum1_3, t, ALU.add)
                v.drain()
                tt(sum2_3, sum2_3, sq3, ALU.add)
                v.drain()

            sq3, sum1_3, sum2_3 = (t[:, :].rearrange("p (a t) -> p a t", a=1) for t in (sq, sum1, sum2))

            def norm_columns(n, kind, half=False):
                v.drain().then_inc(stat_in, 1)
                v.wait_ge(stat_full, n + 1)
                r, mean, var, t = small[:, 0:8], small[:, 4:8], small[:, 16:24], small[:, 24:32]
                w = 8 if kind == "c" else 4
                if kind == "ln":
                    ts(mean, ps[:, STAT, 4:8], 1.0 / D, None, ALU.mult)
                    v.drain()
                    tt(t[:, 0:4], mean, mean, ALU.mult)
                    v.drain()
                    stt(var[:, 0:4], ps[:, STAT, 0:4], 1.0 / D, t[:, 0:4], ALU.mult, ALU.subtract)
                    v.drain()
                    ts(var[:, 0:4], var[:, 0:4], LN_EPS, None, ALU.add)
                elif kind == "rms":
                    ts(var[:, 0:4], ps[:, STAT, 0:4], 1.0 / D, RMS_EPS, ALU.mult, ALU.add)
                else:
                    ts(var[:, 0:4], ps[:, STAT, 0:4], 1.0 / 256, RMS_EPS, ALU.mult, ALU.add)
                    ts(var[:, 4:8], ps[:, STAT, 4:8], 1.0 / 128, RMS_EPS, ALU.mult, ALU.add)
                v.drain()
                r, var, t = r[:, 0:w], var[:, 0:w], t[:, 0:w]
                ts(t.bitcast(I32), var.bitcast(I32), 1, None, ALU.logical_shift_right)
                v.drain()
                ts(r.bitcast(I32), t.bitcast(I32), -1.0, float(0x5F3759DF), ALU.mult, ALU.add)
                v.drain()
                for _ in range(4):
                    tt(t, r, r, ALU.mult)
                    v.drain()
                    tt(t, t, var, ALU.mult)
                    v.drain()
                    ts(t, t, -0.5, 1.5, ALU.mult, ALU.add)
                    v.drain()
                    tt(r, r, t, ALU.mult)
                    v.drain()
                if half:
                    ts(r, r, 0.5, None, ALU.mult)
                v.drain().then_inc(rstd_ready, 1)

            def norm(n, kind, half=False):
                norm_columns(n, kind, half)
                hold(v, rb_full, n + 1)

            def rope(a2, r, b, dst, cos, sin):
                v.wait_ge(acc_full, a2 + 1)
                v.wait_ge(rot_ready, r + 1)
                tt(dst, ps[:, b:b + 1, :], cos, ALU.mult)
                tt(tmp[:, b:b + 1, :], rot[:, b:b + 1, :], sin, ALU.mult).then_inc(acc_free[b], 1)
                v.drain()
                tt(dst, dst, tmp[:, b:b + 1, :], ALU.add).then_inc(heads_ready, 1)

            def mask_scores(un, n, c0, ring, probs):
                b, W, bank = n % 2, un["W"], 2 + ring * (n % 2)
                if n >= 2:
                    v.wait_ge(pt_full, c0 + n - 1)
                hold(v, s_full, c0 + n + 1)
                src = ps[:, bank, 0:W] if ring == 1 else ps[:, bank:bank + 2, :].rearrange("p b t -> p (b t)")[:, 0:W]
                m = un["mask"] if ring == 1 else mask_d[:, un["mask"], :]
                init = 3.0e38 if un["sink"] is None else nsink[:, un["sink"]:un["sink"] + 1]
                V.tensor_tensor_reduce(probs[:, b, 0:W], src, m, -un["scale"], init, ALU.add, ALU.min,
                                       col[:, b, 0:1]).then_inc(masked, 1)

            def normalise(un, n, c0, probs):
                b = n % 2
                v.wait_ge(p_exp, c0 + n + 1)
                if un["sink"] is not None:
                    tt(col[:, b, 1:2], col[:, b, 1:2], col[:, b, 2:3], ALU.add)
                    v.drain()
                V.reciprocal(col[:, b, 3:4], col[:, b, 1:2])
                v.drain()
                ts(probs[:, b, 0:un["W"]], probs[:, b, 0:un["W"]], col[:, b, 3:4], None, ALU.mult).then_inc(p_norm, 1)

            def attend(U, c0, ring, probs, o_of, hi_of, lo_of, lag, between=None):
                N = len(U)
                mask_scores(U[0], 0, c0, ring, probs)
                for n in range(N + lag):
                    if n + 1 < N:
                        mask_scores(U[n + 1], n + 1, c0, ring, probs)
                    if n < N:
                        normalise(U[n], n, c0, probs)
                    m = n - lag
                    if m >= 0:
                        v.wait_ge(o_hi_done, c0 + m + 1)
                        tt(lo_of(U[m]), o_of(U[m], m), hi_of(U[m]).bitcast(F32), ALU.subtract).then_inc(o_split, 1)
                    if between is not None:
                        between(n)

            def topk_round(qt):
                work = maskb[:, qt, 0:(qt + 1) * P]
                v.drain()
                V.max(max8[:, :], work)
                v.drain()
                V.match_replace(work, max8[:, :], work, TAKEN)

            def router():
                v4 = lambda i: rt[:, i, :].rearrange("p (g e) -> p g e", e=TOKG)
                scores, biased, rank, sel = rt[:, 2, :], rt[:, 3, :], rt[:, 4, :], rt[:, 5, :]
                ts(scores, rt[:, 1, :], 0.5, 0.5, ALU.mult, ALU.add)
                v.drain()
                tt(biased.rearrange("p (t e) -> p t e", e=E), scores.rearrange("p (t e) -> p t e", e=E),
                   rbias[:, :].unsqueeze(1).to_broadcast([P, NT, E]), ALU.add)
                v.drain()

                def ranks(o, vals, g):
                    other = vals.unsqueeze(2).to_broadcast([P, g, 4, 4])
                    own = vals.unsqueeze(3).to_broadcast([P, g, 4, 4])
                    gt, eq = (pairs[:, i, 0:16 * g].rearrange("p (g j i) -> p g j i", j=4, i=4) for i in range(2))
                    tt(gt, other, own, ALU.is_gt)
                    tt(eq, other, own, ALU.is_equal)
                    v.drain()
                    tt(eq, eq, tri[:, :].rearrange("p (j i) -> p j i", j=4).unsqueeze(1).to_broadcast([P, g, 4, 4]), ALU.mult)
                    v.drain()
                    tt(gt, gt, eq, ALU.add)
                    v.drain()
                    V.tensor_reduce(o, gt, AX.X, ALU.add)
                    v.drain()

                ranks(v4(4), v4(3), 16)
                ts(sel, rank, 1.5, None, ALU.is_lt)
                v.drain()
                tt(rt[:, 6, :], biased, sel, ALU.mult)
                v.drain()
                gsum, grank = rt[:, 7, 0:16], rt[:, 7, 16:32]
                V.tensor_reduce(gsum, v4(6), AX.X, ALU.add)
                v.drain()
                ranks(grank.rearrange("p (t g) -> p t g", g=4), gsum.rearrange("p (t g) -> p t g", g=4), 4)
                ts(grank, grank, 0.5, None, ALU.is_lt)
                v.drain()
                tt(v4(5), v4(5), grank.unsqueeze(2).to_broadcast([P, 16, 4]), ALU.mult)
                v.drain()
                tt(rt[:, 6, :], scores, sel, ALU.mult)
                v.drain()
                total, inv = rt[:, 7, 32:36], rt[:, 7, 36:40]
                V.tensor_reduce(total, rt[:, 6, :].rearrange("p (t e) -> p t e", e=E), AX.X, ALU.add)
                v.drain()
                V.reciprocal(inv, total)
                v.drain()
                tt(rt[:, 0, :].rearrange("p (t e) -> p t e", e=E), rt[:, 6, :].rearrange("p (t e) -> p t e", e=E),
                   inv.unsqueeze(2).to_broadcast([P, NT, E]), ALU.mult).then_inc(gates_ready, 1)

            def hidden(ap, n, k, gate=None, last_of_gate=False):
                v.drain()
                v.wait_ge(sg_ready, n + 1)
                v.wait_ge(acc_full, 2 * ap + 2)
                tt(hh[:, :], sg[:, :], ps[:, 1, :], ALU.mult).then_inc(acc_free[1], 1)
                v.drain().then_inc(sg_used, 1)
                if gate is not None:
                    v.wait_ge(gb_landed, gate)
                    tt(hh[:, :], hh[:, :], gb[:, :], ALU.mult)
                    v.drain()
                    if last_of_gate:
                        v.drain().then_inc(gb_used, 1)
                h3 = hh[:, :].rearrange("p (a t) -> p a t", a=1)
                ts(hs_hi[:, bass.ds(k, 1), :], h3, 1.0, None, ALU.mult)
                v.drain()
                tt(hs_lo[:, bass.ds(k, 1), :], h3, hs_hi[:, bass.ds(k, 1), :].bitcast(F32), ALU.subtract).then_inc(h_ready, 1)

            v.sem_inc(w_split, RING)
            for b in range(RING):
                v.sem_inc(acc_free[b], 1)
            for s_ in (gb_used, sg_used, place_free):
                v.sem_inc(s_, 1)
            v.wait_ge(const_landed, 160)
            split(0, 0, W_FULL)
            split(0, 1, W_FULL)
            v.wait_ge(wr_hi_done, 1)
            tt(wr_lo[:, :], wr[:, :], wr_hi[:, :].bitcast(F32), ALU.subtract).then_inc(wr_ready, 1)
            with v.Fori(0, L) as l:
                j, c = l * JL, l * AL
                v.sem_inc(tile_ready, KD)
                fill(2 * l, lambda m: None, lambda m: x[:, m, :])
                v.wait_ge(layer_landed, l * 48 + 48)
                ts(nsink[:, :], nsink[:, :], -1.0, None, ALU.mult)
                for i in range(3):
                    split(j + 1 + i // 2, i % 2, (W_FULL, W_KR, W_VA)[i])
                    v.wait_ge(c_copied, 3 * l + i + 1)
                    tt((sum2, sq, sum1)[i][:, :], cfeat[:, i, :], cfeat[:, i, :], ALU.mult)
                    if i == 1:
                        v.drain()
                        tt(sum2[:, :], sum2[:, :], sq[:, :], ALU.add)
                split(j + 2, 1, W_VB)
                v.wait_ge(acc_full, 2 * c + 4)
                tt(krope[64:96, :], ps[0:32, 1, :], tabc[0:32, :], ALU.mult)
                tt(tmp[64:96, 1, :], ps[32:64, 1, :], tabc[32:64, :], ALU.mult).then_inc(acc_free[1], 1)
                v.drain()
                tt(krope[64:96, :], krope[64:96, :], tmp[64:96, 1, :], ALU.add).then_inc(kr_ready, 1)
                split(j + 3, 0, W_FULL)
                split(j + 3, 1, W_FULL)
                norm_columns(3 * l, "c")
                cos, sin = tabs[:, 0:1, :], tabs[:, 1:2, :]
                with v.Fori(0, 4) as i:
                    for s in range(2):
                        split(j + 4 + i, s, W_FULL)
                        rope(2 * (c + 3 + i) + s, l * N_ROPE + 2 * i + s, s, heads[:, bass.ds(2 * i + s, 1), :], cos, sin)
                for s in range(2):
                    split(j + 8, s, (W_FULL, W_UP)[s])
                    rope(2 * (c + 7) + s, l * N_ROPE + 8 + s, s, heads[:, 8 + s:9 + s, :], cos, sin)
                v.wait_ge(rb_full, 3 * l + 1)
                for i in range(3):
                    stt(cfeat[:, i, :], cfeat[:, i, :], cg[:, i:i + 1], ps[:, (RB, RB, MB)[i], :], ALU.mult, ALU.mult)\
                        .then_inc(c_tile, 1)
                for i in range(3):
                    v.wait_ge(c_hi_done, 3 * l + i + 1)
                    tt(cs_lo[:, i, :], cfeat[:, i, :], cs_hi[:, i, :].bitcast(F32), ALU.subtract).then_inc(c_ready, 1)
                split(j + 9, 0, W_FULL)
                rope(2 * c + 16, l * N_ROPE + 10, 0, heads[:, 10:11, :], cos, sin)
                for i in range(4):
                    b = (i + 1) % 2
                    v.wait_ge(acc_full, 2 * c + 18 + i)
                    v.wait_ge(act_copied, l * COPIES + 3 + i)
                    tt(qc[64:96, i, :], ps[64:96, b, :], tabc[64:96, :], ALU.mult)
                    tt(tmp[64:96, b, :], ps[96:128, b, :], tabc[96:128, :], ALU.mult).then_inc(acc_free[b], 1)
                    v.drain()
                    tt(qc[64:96, i, :], qc[64:96, i, :], tmp[64:96, b, :], ALU.add).then_inc(qc_ready, 1)
                split(j + 9, 1, W_FULL)
                for n, (qt, h) in enumerate(IX):
                    work, src, wcol = maskb[:, qt, 0:(qt + 1) * P], rl[:, n % 2, 0:(qt + 1) * P], vb[:, qt, 64 + h:65 + h]
                    v.drain()
                    v.wait_ge(ix_relu, l * len(IX) + n + 1)
                    if h == 0:
                        ts(work, src, wcol, None, ALU.mult).then_inc(ix_used, 1)
                    else:
                        stt(work, src, wcol, work, ALU.mult, ALU.add).then_inc(ix_used, 1)
                v.drain()
                for qt in range(1, NT):
                    work = maskb[:, qt, 0:(qt + 1) * P]
                    stt(work, mask_c[:, (3 - qt) * P:T], CAUSAL / MASKED, work, ALU.mult, ALU.add)
                V.tensor_copy(maskb[:, 0, 0:P], mask_c[:, 3 * P:T])
                rounds = [(qt, i) for qt in range(1, NT) for i in range(TOPK // 8)]

                def between(n):
                    for qt, i in rounds[n * 24 // 23:(n + 1) * 24 // 23]:
                        topk_round(qt)
                    if n == 45:
                        v.drain()
                        for qt in range(1, NT):
                            work = maskb[:, qt, 0:(qt + 1) * P]
                            ts(work, work, TAKEN * 0.99, MASKED, ALU.is_gt, ALU.mult)
                        v.drain()

                attend(UN, l * UNITS, 1, prob, lambda un, n: ps[un["row"]:un["row"] + 64, 6 + n % 2, 0:P],
                       lambda un: xs_hi[un["row"]:un["row"] + 64, un["tile"], un["at"]:un["at"] + P],
                       lambda un: xs_lo[un["row"]:un["row"] + 64, un["tile"], un["at"]:un["at"] + P], 2, between)
                clear_sums()
                with v.Fori(0, 4) as i:
                    for s in range(2):
                        split(j + 10 + i, s, W_FULL)
                        v.wait_ge(acc_full, 2 * (c + 12 + i) + s + 2)
                        xm = x[:, bass.ds(2 * i + s, 1), :]
                        stt(xm, xm, ALPHA, ps[:, 1 - s:2 - s, :], ALU.mult, ALU.add).then_inc(acc_free[1 - s], 1)
                        add_up(xm, mean=True)
                norm(3 * l + 1, "ln")

                def layer_norm(src, g, inc):
                    def make(m):
                        v.drain()
                        tt(tmp[:, m % 2, :], src[:, m, :], ps[:, MB, :], ALU.subtract)
                        v.drain()
                        stt(tmp[:, m % 2, :], tmp[:, m % 2, :], lng[:, g, m:m + 1], ps[:, RB, :], ALU.mult, ALU.mult)
                        v.drain()
                        last = ts(x[:, m, :], tmp[:, m % 2, :], lng[:, g + 1, m:m + 1], None, ALU.add)
                        if inc:
                            last.then_inc(tile_ready, 1)
                    return make

                fill(2 * l + 1, layer_norm(x, 0, True), lambda m: x[:, m, :])
                v.wait_ge(r_tanh, l + 1)
                v.sem_inc(acc_free[1], 1)
                router()
                ts(flat(y), flat(x), ALPHA, None, ALU.mult)
                v.drain()
                with v.Fori(0, 4) as q:
                    jq, cq = j + J_MOE // 2 + q * 12, c + A_MOE // 2 + q * 12
                    with v.Fori(0, 4) as e:
                        for f in range(2):
                            for s in range(2):
                                split(jq + 1 + 2 * e + f, s, W_FULL)
                            hidden(cq + 2 * e + f, l * 32 + q * 8 + 2 * e + f, 2 * e + f,
                                   gate=(l * 16 + q * 4 + e) * 16 + 16, last_of_gate=(f == 1))
                    with v.Fori(0, 4) as i:
                        for s in range(2):
                            split(jq + 9 + i, s, W_FULL)
                            v.wait_ge(acc_full, 2 * (cq + 8 + i) + s + 1)
                            ym = y[:, bass.ds(2 * i + s, 1), :]
                            tt(ym, ym, ps[:, s:s + 1, :], ALU.add).then_inc(acc_free[s], 1)
                v.drain()
                clear_sums()
                with v.Fori(0, KD) as m:
                    add_up(y[:, bass.ds(m, 1), :], mean=True)
                norm(3 * l + 2, "ln")
                for m in range(KD):
                    layer_norm(y, 2, False)(m)
                v.drain().then_inc(place_free, 1)

            def rms_fill(name, perm=False):
                def make(m):
                    v.drain()
                    stt(tmp[:, m % 2, :], x[:, m, :], ngain[:, GAIN[name], m:m + 1], ps[:, RB, :], ALU.mult, ALU.mult)\
                        .then_inc(tile_ready, 1)
                norm(NORM[name], "rms")
                fill(FILL[name], make, perm=perm)

            def residual(name, t, half, sums=True):
                norm(NORM[name], "rms", half)
                V.memset(sum2[:, :], 0.0)
                for m in range(KD):
                    v.drain()
                    stt(tmp[:, 0, :], t[:, m, :], ngain[:, GAIN[name], m:m + 1], ps[:, RB, :], ALU.mult, ALU.mult)
                    v.drain()
                    tt(x[:, m, :], x[:, m, :], tmp[:, 0, :], ALU.add)
                    if sums:
                        add_up(x[:, m:m + 1, :])

            def dense(name, last=False):
                j, c, n = JS[name], AS[name], int(name[3])
                rms_fill(name)
                V.memset(flat(y), 0.0)
                clear_sums()
                for g in range(2):
                    jg, c_g = j + 15 * g, c + 15 * g
                    with v.Fori(0, GK - 1) as i:
                        for s in range(2):
                            split(jg + 1 + i, s, W_FULL)
                        hidden(c_g + i, 64 + 22 * n + GK * g + i, i)
                    for s in range(2):
                        split(jg + GK, s, W_DOWN)
                    hidden(c_g + GK - 1, 64 + 22 * n + GK * g + GK - 1, GK - 1)

                    def add_tile(i, s):
                        v.wait_ge(acc_full, 2 * (c_g + GK + i) + s + 1)
                        ym = y[:, bass.ds(2 * i + s, 1), :]
                        tt(ym, ym, ps[:, s:s + 1, :], ALU.add).then_inc(acc_free[s], 1)
                        if g == 1:
                            add_up(ym)

                    with v.Fori(0, 3) as i:
                        for s in range(2):
                            split(jg + 12 + i, s, W_DOWN)
                            add_tile(i, s)
                    for s in range(2):
                        if not (last and g == 1):
                            split(jg + 15, s, W_FULL)
                        add_tile(3, s)
                    v.drain()
                if name == "ffn0":
                    v.drain().then_inc(place_free, 1)
                residual(name + "_out", y, True, sums=not last)

            v.drain()
            clear_sums()
            with v.Fori(0, KD) as m:
                add_up(x[:, bass.ds(m, 1), :])
            dense("ffn0")

            j, c = JS["pool"], AS["pool"]
            rms_fill("pool")
            V.memset(u0[:, 0:16], 0.0)
            V.memset(uw[:, 0, 0:16], 0.0)
            V.memset(uw[:, 1, 0:16], 0.0)
            v.wait_ge(late_landed, 32)
            for m in range(KD):
                g = m // 2
                split(j + 1 + m // 2, m % 2, W_FULL if m < 6 else 2 * P)
                v.wait_ge(acc_full, 2 * c + m + 1)
                v.drain()
                V.tensor_copy(u0[:, 16:16 + T], ps[:, m % 2, :]).then_inc(acc_free[m % 2], 1)
                if m >= 2:
                    v.wait_ge(k_hi_done, m - 1)
                src = u0
                for i in range(g + 1):
                    dst = uw[:, i % 2, :]
                    v.drain()
                    tt(dst[:, 16:16 + T], src[:, 16:16 + T], src[:, 16 - (1 << i):16 + T - (1 << i)], ALU.add)
                    src = dst
                v.drain()
                t = tmp[:, m % 2, :]
                stt(t, src[:, 16:16 + T], 1.0 / (2 << g), u0[:, 16:16 + T], ALU.mult, ALU.subtract)
                v.drain()
                tt(t[:, 0:16], src[:, 16:32], cnt[:, g, :], ALU.mult)
                v.drain()
                tt(t[:, 0:16], t[:, 0:16], u0[:, 16:32], ALU.subtract).then_inc(c_tile, 1)
                v.wait_ge(k_hi_done, m + 1)
                v.drain()
                tt(po_lo[:, m, :], t, po_hi[:, m, :].bitcast(F32), ALU.subtract).then_inc(k_ready, 1)
            for m in range(KD):
                split(j + 5 + m // 2, m % 2, 2 * P if m < 6 else W_FULL)
                v.wait_ge(acc_full, 2 * c + 8 + m + 1)
                v.drain()
                ts(tmp[:, m % 2, :], ps[:, m % 2, :], pgain[:, m:m + 1], None, ALU.mult).then_inc(tile_ready, 1)
                v.wait_ge(xs_hi_done, 8 * FILL["pool_out"] + m + 1)
                v.sem_inc(acc_free[m % 2], 1)
                tt(xs_lo[:, m, :], tmp[:, m % 2, :], xs_hi[:, m, :].bitcast(F32), ALU.subtract).then_inc(xs_ready, 1)
            clear_sums()
            with v.Fori(0, 4) as i:
                for s in range(2):
                    split(j + 9 + i, s, W_FULL)
                    v.wait_ge(acc_full, 2 * (c + 8 + i) + s + 1)
                    ym = y[:, bass.ds(2 * i + s, 1), :]
                    ts(ym, ps[:, s:s + 1, :], 1.0, None, ALU.mult).then_inc(acc_free[s], 1)
                    add_up(ym)
            residual("pool_out", y, False)
            dense("ffn1")

            norm(NORM["keys"], "rms")
            for m in range(KD):
                stt(y[:, m, :], x[:, m, :], ngain[:, GAIN["keys"], m:m + 1], ps[:, RB, :], ALU.mult, ALU.mult).then_inc(hk_ready, 1)
            v.wait_ge(hk_stored, 16)
            dense("ffn2")

            j, c = JS["dilated"], AS["dilated"]
            v.drain().then_inc(place_free, 1)
            v.wait_ge(late_landed, 16 * 6)
            pos, ang, turns = tmp[:, 0, :], rot[:, 0, :], rot[:, 1, :]
            V.tensor_copy(sq[:, :], pos.bitcast(I32))
            v.drain()
            ts(ang, sq[:, :], dcol[:, 0:1], None, ALU.mult)
            v.drain()
            for i, shift in ((0, 0.25), (1, 0.0)):
                ts(turns, ang, 1.0 / (2 * np.pi), shift, ALU.mult, ALU.add)
                v.drain()
                ts(turns, turns, 12582912.0, None, ALU.add)
                v.drain()
                ts(turns, turns, 12582912.0, None, ALU.subtract)
                v.drain()
                o = tmp[:, i, :]
                stt(o, turns, -TWO_PI[0], ang, ALU.mult, ALU.add)
                v.drain()
                stt(o, turns, -TWO_PI[1], o, ALU.mult, ALU.add)
                v.drain()
                stt(o, turns, -TWO_PI[2], o, ALU.mult, ALU.add)
                v.drain()
                if i == 0:
                    ts(o, o, float(np.pi / 2), None, ALU.add)
                    v.drain()
                ts(o, o, PI_BELOW, -PI_BELOW, ALU.min, ALU.max).then_inc(tab_in, 1)
            v.wait_ge(tab_done, 2)
            v.drain()
            ts(dtab[:, 1, :], dtab[:, 1, :], dcol[:, 1:2], None, ALU.mult)
            for m in range(KD):
                v.wait_ge(k_hi_done, 8 + m + 1)
                tt(ks_lo[:, m, :].rearrange("p (c i) -> p c i", c=4), hk_in[:, m, :].rearrange("p (i c) -> p c i", c=4),
                   ks_hi[:, m, :].rearrange("p (c i) -> p c i", c=4).bitcast(F32), ALU.subtract).then_inc(k_ready, 1)
            rms_fill("dilated", perm=True)
            cos, sin = dtab[:, 0:1, :], dtab[:, 1:2, :]
            with v.Fori(0, 4) as p:
                jp, cp = j + p * 5, c + p * 5
                for i in range(6):
                    split(jp + 1 + i // 2, i % 2, W_FULL if i < 4 else KD * 96)
                    rope(2 * cp + i, L * N_ROPE + p * 6 + i, i % 2, dq[:, i:i + 1, :], cos, sin)
                for i in range(2):
                    split(jp + 4, i, KD * 96)
                for i in range(2):
                    split(jp + 5, i, W_FULL)
                attend(UD, L * UNITS + p * 8, 2, dprob, lambda un, n: ps[un["row"]:un["row"] + 64, 7, 2 * P:3 * P],
                       lambda un: dm_hi[un["row"]:un["row"] + 64, bass.ds(p, 1), un["at"]:un["at"] + P],
                       lambda un: dm_lo[un["row"]:un["row"] + 64, bass.ds(p, 1), un["at"]:un["at"] + P], 0)
            clear_sums()

            def back_in_order(i, s):
                v.wait_ge(acc_full, 2 * (c + 20 + i) + s + 1)
                ym = yd[:, bass.ds(2 * i + s, 1), :]
                ts(ym.rearrange("p a (i c) -> p a c i", c=4), ps[:, s:s + 1, :].rearrange("p a (c i) -> p a c i", c=4),
                   1.0, None, ALU.mult).then_inc(acc_free[s], 1)
                add_up(ym)

            with v.Fori(0, 3) as i:
                for s in range(2):
                    split(j + 21 + i, s, 4 * P)
                    back_in_order(i, s)
            for s in range(2):
                split(j + 24, s, W_FULL)
                back_in_order(3, s)
            residual("dilated_out", yd, False)
            dense("ffn3", last=True)
            v.drain().then_inc(y_final, 1)



def tiles(w):
    k = w.shape[0] // P
    return w.reshape(k, P, -1).transpose(1, 0, 2).reshape(P, -1)


def columns(w):
    return np.stack([tiles(w[:, i:i + P]) for i in range(0, w.shape[1], P)])


def rope_rows(rows, dim, positions):
    inv = (1.0 / (np.float32(10000.0) ** (np.arange(0, dim, 2, dtype=np.float32) / dim))).astype(np.float32)
    return positions.astype(np.float32)[None, :] * inv[rows][:, None]


def first_constants():
    pos = np.arange(T)
    row = np.arange(P)
    ang = rope_rows(row % 32, HD, pos)
    sign = np.where(row % 64 < 32, -1.0, 1.0).astype(np.float32)[:, None]
    tab = np.stack([np.cos(ang), np.sin(ang) * sign], axis=1)
    angc = rope_rows(row % 16, 32, pos)
    signc = np.where(row % 32 < 16, -1.0, 1.0).astype(np.float32)[:, None]
    tabc = np.where((row % 64 < 32)[:, None], np.cos(angc), np.sin(angc) * signc)
    q, k = np.arange(P)[:, None], np.arange(2 * P)[None, :]
    diff = q + P - k
    mask_a = np.where((diff >= 0) & (diff < P), 0.0, MASKED)
    mask_c = np.zeros((P, T))
    mask_c[:, 3 * P:] = np.where(np.arange(P)[None, :] <= q, 0.0, MASKED)
    j, i = np.arange(4)[:, None], np.arange(4)[None, :]
    tri = np.broadcast_to((i < j).reshape(1, 16), (P, 16))
    t_all = (4 * np.arange(P)[None, :] + np.arange(4)[:, None]).reshape(-1)
    mask_d = np.full((P, 4, T + 2 * P), MASKED)
    for c in range(4):
        d = (4 * np.arange(P) + c)[:, None] - t_all[None, :]
        mask_d[:, c, :T] = np.where((d >= 0) & (d <= P), 0.0, MASKED)
        d = np.arange(P)[:, None] - np.arange(P)[None, :]
        mask_d[:, c, T:T + P] = np.where(d >= 0, 0.0, MASKED)
        mask_d[:, c, T + P:] = np.where((d >= 0) & (d % 4 == 0), 0.0, MASKED)
    inv = (np.float32(10000.0) ** (-np.arange(0, HD, 2, dtype=np.float32) / HD)).astype(np.float32)
    dcol = np.stack([inv[row % 32], sign[:, 0]], axis=1)
    w = np.array([2, 4, 8, 16])[:, None]
    cnt = np.broadcast_to((1.0 / np.minimum(np.arange(16)[None, :] + 1, w)).reshape(1, 64), (P, 64))
    f = lambda v: np.ascontiguousarray(v, dtype=np.float32)
    return dict(tab=f(tab).reshape(P, -1), tabc=f(tabc), mask_a=f(mask_a), mask_c=f(mask_c), tri=f(tri),
                ident=np.eye(P, dtype=np.float32), mask_d=f(mask_d).reshape(P, -1), dcol=f(dcol), p_cnt=f(cnt))


def lay_out(i):
    cat = np.concatenate
    out = first_constants()
    out["xT"] = tiles(i["x"][0].T)
    w_in, w_kr, w_vb, w_up, w_out = [], [], [], [], []
    for l in range(L):
        o = np.cumsum([0, 512, 128, 128, 256, 64, 64, 256, 64, 4, 256, 128, 32])
        aq, ak, av, bq, bk, bv, iq, ik, iw, cq, ckv, ckr = (i["w_in"][l][:, o[n]:o[n + 1]] for n in range(12))
        pair = [aq[:, 64 * h:64 * h + 64] for t in range(4) for h in (t, 4 + t)]
        w_in.append(columns(cat([cq, ckv, av] + pair + [ak, bq, bk, bk, iq, ik, ik], axis=1)))
        w_kr.append(tiles(cat([ckr, ckr[:, 16:], ckr[:, :16]], axis=1)))
        w_vb.append(tiles(cat([bv, iw], axis=1)))
        uq, ukv = i["w_uq"][l], i["w_ukv"][l]
        q = [tiles(cat([uq[:, 96 * h:96 * h + 96], uq[:, 96 * h + 80:96 * h + 96], uq[:, 96 * h + 64:96 * h + 80]], axis=1))
             for h in range(4)]
        k = [ukv[:, P * h:P * h + 64] for h in range(4)]
        v = [ukv[:, P * h + 64:P * h + P] for h in range(4)]
        w_up.append(cat(q + k + v, axis=1))
        wo = i["w_out"][l]
        rows = [wo[64 * h:64 * h + 64] for t in range(4) for h in (t, 4 + t)]
        w_out.append(columns(cat(rows + [wo[512:]], axis=0)))
    stack = lambda v: np.ascontiguousarray(np.stack(v))
    out["w_in"], out["w_out"] = np.concatenate(w_in), np.concatenate(w_out)
    out["w_kr"], out["w_vb"], out["w_up"] = stack(w_kr), stack(w_vb), stack(w_up)
    out["w_router"] = tiles(i["w_router"])
    out["rbias"] = i["router_bias"].reshape(1, E)
    out["nsink"] = i["attn_sinks"]
    cols = lambda v: v.reshape(-1, P).T
    out["c_g"] = stack([cat([cols(i["c_q_norm_g"][l]), cols(i["c_kv_norm_g"][l])], axis=1) for l in range(L)])
    out["ln"] = stack([cat([cols(i[n][l]) for n in ("ln1_g", "ln1_b", "ln2_g", "ln2_b")], axis=1) for l in range(L)])
    gu = stack([i["w_gate"], i["w_up"]]).reshape(2, L, E, KD, P, 2, P)
    out["w_gu"] = gu.transpose(1, 2, 5, 0, 4, 3, 6).reshape(-1, P, D)
    dn = i["w_down"].reshape(L, 4, 8, P, KD, P)
    out["w_dn"] = dn.transpose(0, 1, 4, 3, 2, 5).reshape(-1, P, 8 * P)
    out["ngain"] = cat([cols(g) for g in i["norm_gain_2"].reshape(12, D)] + [cols(i["kv_norm_gain_2"])], axis=1)
    F = i["ffn_w_gate_2"].shape[-1]
    gu = stack([i["ffn_w_gate_2"], i["ffn_w_up_2"]]).reshape(2, 4, KD, P, F // P, P)
    out["f_gu"] = gu.transpose(1, 4, 0, 3, 2, 5).reshape(-1, P, D)
    dn = i["ffn_w_down_2"].reshape(4, 2, GK, P, KD, P)
    out["f_dn"] = dn.transpose(0, 1, 4, 3, 2, 5).reshape(-1, P, GK * P)
    out["p_in"], out["p_out"] = columns(i["pool_w_in_2"][0]), columns(i["pool_w_out_2"][0])
    out["p_grp"] = np.concatenate([columns(g) for g in i["pool_w_group_2"][0]])
    out["p_scale"] = cols(i["pool_scale_2"][0])
    pairs = lambda w: [w[:, 512 * g + P * p:512 * g + P * p + P] for p in range(4) for g in range(3)]
    q, k, v = pairs(i["attn_w_q_2"][0]), pairs(i["w_k_2"]), pairs(i["w_v_2"])
    out["d_qk"] = stack([tiles(w) for p in range(4) for w in q[3 * p:3 * p + 3] + k[3 * p:3 * p + 3]])
    out["d_v"] = stack([tiles(cat(v[3 * p:3 * p + 3], axis=1)[:, 96 * n:96 * n + 96]) for p in range(4) for n in range(4)])
    out["d_out"] = columns(i["attn_w_o_2"][0])
    out["pos"] = i["positions_2"].reshape(P, 4).T.reshape(1, T).astype(np.int32)
    return {n: np.ascontiguousarray(v) for n, v in out.items()}


def kernel(**inputs):
    import concourse.bacc as bacc
    from concourse.bass_utils import run_bass_kernel_spmd

    nc = bacc.Bacc("TRN2", target_bir_lowering=False, num_devices=1)
    arrays = lay_out({n: np.asarray(v) for n, v in inputs.items()})
    args = {n: nc.dram_tensor(f"in_{n}", v.shape, mybir.dt.from_np(v.dtype), kind="ExternalInput").ap()
            for n, v in arrays.items()}
    out = nc.dram_tensor("out_hT", (P, KD * T), F32, kind="ExternalOutput").ap()
    build_program(nc, args, out)
    r = run_bass_kernel_spmd(nc, [{f"in_{n}": v for n, v in arrays.items()}], core_ids=[0])
    got = np.asarray(r.results[0]["out_hT"])
    return got.reshape(P, KD, T).transpose(2, 1, 0).reshape(1, T, D)
```

```python
from contextlib import ExitStack

import numpy as np

import concourse.bass as bass
from concourse import mybir

F32, F32R, I32 = mybir.dt.float32, mybir.dt.float32r, mybir.dt.int32
ALU = mybir.AluOpType
ACT = mybir.ActivationFunctionType
AX = mybir.AxisListType

P, T, D, L = 128, 512, 1024, 2
KD = D // P
NT = T // P
HD = 64
ALPHA = float((2 * L) ** 0.25)
LN_EPS, RMS_EPS = 1e-5, 1e-6
TOPK = 128
E, TOKG = 16, 4
RING = 2
SLOT = 12 * P + 32
GK = 11
MASKED = -1.0e30
CAUSAL = -1.0e38
TAKEN = -3.0e38

J_ROPE, N_ROPE, J_UP, J_OUT, N_JOBS = 6, 11, 17, 18, 18 + 8 + 96
A_ROPE, A_UP, A_OUT, A_ROUTER, A_MOE, N_ACC = 6, 17, 25, 33, 34, 130
J_MOE = J_OUT + 8
UNITS = 64
UNITS_D = 64 * 1

W_FULL, W_KR, W_VA, W_VB, W_UP, W_DOWN = KD * P, KD * 64, KD * P, KD * 68, 12 * P, GK * P


TWO_PI = (6.28125, 0.0019350051879882812, 3.019916050561733e-07)
PI_BELOW = 3.1415925


def build_program(nc, a, out):
    gates_dram = nc.dram_tensor("gates_scratch", (E, T), F32, kind="Internal").ap()
    keys_dram = [nc.dram_tensor(f"keys_scratch_{n}", (P, KD * T), F32R, kind="Internal").ap() for n in ("hi", "lo")]

    with ExitStack() as ctx:
        cursor = [(nc.sbuf_base + 63) // 64 * 64]

        def sb(name, shape, dt=F32):
            size = int(np.prod(shape[1:])) * 4
            t = nc.alloc_sbuf_tensor_at(name, shape, dt, offset=cursor[0])
            cursor[0] += (size + 31) // 32 * 32
            assert cursor[0] <= nc.sbuf_usable_end, name
            return t

        def flat(t):
            return t[:, :, :].rearrange("p k t -> p (k t)")

        def one(ap, i):
            return ap[bass.ds(i, 1)].rearrange("a p n -> (a p) n")

        x = sb("x", [P, KD, T])
        xs_hi, xs_lo = sb("xs_hi", [P, KD, T], F32R), sb("xs_lo", [P, KD, T], F32R)
        stage = sb("w_stage", [P, RING, SLOT])
        w_hi, w_lo = sb("w_hi", [P, RING, SLOT], F32R), sb("w_lo", [P, RING, SLOT], F32R)
        sum1, sum2, sq = sb("sum1", [P, T]), sb("sum2", [P, T]), sb("squares", [P, 2, T])
        tmp, rot = sb("tmp", [P, 2, T]), sb("rotated", [P, 2, T])
        ident, ones = sb("ident", [P, P]), sb("ones", [P, 1])
        pick = sb("pick", [P, 64])
        small = sb("small", [P, 64])
        ngain = sb("ngain", [P, 13, KD])
        col = sb("attn_cols", [P, 2, 8])
        region0 = cursor[0]
        tabs, tabc = sb("rope_tab", [P, 2, T]), sb("rope_tab_c", [P, T])
        mask_a, mask_c = sb("mask_a", [P, 2 * P]), sb("mask_c", [P, T])
        tri = sb("ties", [P, 16])
        wr = sb("w_router", [P, KD * E])
        wr_hi, wr_lo = sb("w_router_hi", [P, KD * E], F32R), sb("w_router_lo", [P, KD * E], F32R)
        rbias = sb("router_bias", [P, E])
        nsink, cg, lng = sb("neg_sinks", [P, 8]), sb("c_gain", [P, 3]), sb("ln_gain", [P, 4, KD])
        region1 = cursor[0]
        heads = sb("heads", [P, N_ROPE, T])
        cfeat = sb("c_feat", [P, 3, T])
        cs_hi, cs_lo = sb("c_hi", [P, 3, T], F32R), sb("c_lo", [P, 3, T], F32R)
        qc, kc, krope = sb("q_c", [P, 4, T]), sb("k_c", [P, 4, T]), sb("k_rope", [P, T])
        va, vb, vc = sb("v_a", [P, NT, P]), sb("v_b", [P, NT, 68]), sb("v_c", [P, NT, 256])
        maskb = sb("mask_b", [P, NT, T])
        rl = sb("index_relu", [P, 2, T])
        prob, probt = sb("prob", [P, 2, T]), sb("prob_t", [P, 2, T])
        max8 = sb("max8", [P, 8])
        cursor[0] = region1
        y = sb("y", [P, KD, T])
        gb, sg, hh = sb("gate_bcast", [P, T]), sb("silu", [P, T]), sb("hidden", [P, T])
        gates_t = sb("gates_t", [E, T])
        rt, pairs = sb("router_work", [P, 8, 64]), sb("router_pairs", [P, 2, 256])
        region2 = cursor[0]
        hs_hi, hs_lo = sb("h_hi", [P, GK, T], F32R), sb("h_lo", [P, GK, T], F32R)
        cursor[0] = region2
        u0, uw = sb("pool_u", [P, 16 + T]), sb("pool_sum", [P, 2, 16 + T])
        cnt, pgain = sb("pool_count", [P, 4, 16]), sb("pool_gain", [P, KD])
        po_hi, po_lo = sb("pooled_hi", [P, KD, T], F32R), sb("pooled_lo", [P, KD, T], F32R)
        cursor[0] = region0
        dtab = sb("d_tab", [P, 2, T])
        dcol = sb("d_cols", [P, 2])
        dq, dv = sb("d_heads", [P, 6, T]), sb("d_v", [P, NT, 384])
        mask_d = sb("mask_d", [P, NT, T + 2 * P])
        dprob, dprobt = sb("d_prob", [P, 2, 768]), sb("d_prob_t", [P, 768])
        dm_hi, dm_lo = sb("d_mix_hi", [P, 4, T], F32R), sb("d_mix_lo", [P, 4, T], F32R)
        region3 = cursor[0]
        ks_hi, ks_lo = sb("k_in_hi", [P, KD, T], F32R), sb("k_in_lo", [P, KD, T], F32R)
        cursor[0] = region3
        yd = sb("y_dilated", [P, KD, T])

        ps = ctx.enter_context(nc.psum_tensor("ps", [P, 8, T], F32))
        STAT, RB, MB = 2, 3, 4

        sem = lambda name: ctx.enter_context(nc.semaphore(name))
        const_landed, layer_landed, late_landed = sem("const_landed"), sem("layer_landed"), sem("late_landed")
        mask_landed = sem("mask_landed")
        w_landed = [sem(f"w_landed{s}") for s in range(RING)]
        w_hi_done = sem("w_hi_done")
        w_split = sem("w_split")
        acc_full = sem("acc_full")
        acc_free = [sem(f"acc_free{b}") for b in range(RING)]
        consts_made = sem("consts_made")
        tile_ready, xs_hi_done, xs_ready = sem("tile_ready"), sem("xs_hi_done"), sem("xs_ready")
        sq_ready, sq_used = sem("squares_ready"), sem("squares_used")
        x_new, x_landed = sem("x_new"), sem("x_landed")
        stat_in, stat_full, rstd_ready, rb_full = sem("stat_in"), sem("stat_full"), sem("rstd_ready"), sem("rb_full")
        rot_ready = sem("rot_ready")
        act_copied, heads_ready, qc_ready = sem("act_copied"), sem("heads_ready"), sem("qc_ready")
        kr_ready, kr_copied = sem("kr_ready"), sem("kr_copied")
        c_tile, c_hi_done, c_ready = sem("c_tile"), sem("c_hi_done"), sem("c_ready")
        v_evacuated, v_turned = sem("v_evacuated"), sem("v_turned")
        logits_copied, logits_full = sem("logits_copied"), sem("logits_full")
        ix_full, ix_relu, ix_used = sem("ix_full"), sem("ix_relu"), sem("ix_used")
        s_full, masked, p_exp, p_norm = sem("s_full"), sem("masked"), sem("p_exp"), sem("p_norm")
        pt_full, pt_copied = sem("pt_full"), sem("pt_copied")
        o_full, o_hi_done, o_split = sem("o_full"), sem("o_hi_done"), sem("o_split")
        h_ready, c_copied, wr_hi_done = sem("h_ready"), sem("c_copied"), sem("w_router_hi")
        wr_ready, r_tanh, gates_ready = sem("w_router_ready"), sem("router_tanh"), sem("gates_ready")
        gt_full, gt_copied, gates_stored = sem("gates_t_full"), sem("gates_t_copied"), sem("gates_stored")
        gb_landed, gb_used = sem("gate_landed"), sem("gate_used")
        sg_ready, sg_used = sem("silu_ready"), sem("silu_used")
        place_free = sem("place_free")
        hk_ready, hk_hi_done, hk_split = sem("hk_ready"), sem("hk_hi_done"), sem("hk_split")
        hk_stored, hk_landed, pos_landed = sem("hk_stored"), sem("hk_landed"), sem("pos_landed")
        k_hi_done, k_ready = sem("k_hi_done"), sem("k_ready")
        tab_in, tab_done = sem("tab_in"), sem("tab_done")
        y_final, out_stored = sem("y_final"), sem("out_stored")

        JL, AL = N_JOBS // 2, N_ACC // 2
        SECOND = ["ffn0", "pool", "ffn1", "ffn2", "dilated", "ffn3"]
        PAIRS = {"f": 30, "p": 12, "d": 24}
        JS = {n: L * JL + sum(PAIRS[m[0]] for m in SECOND[:i]) for i, n in enumerate(SECOND)}
        AS = {n: L * AL + JS[n] - L * JL for n in SECOND}
        FILL = {"ffn0": 5, "pool": 6, "pool_out": 7, "ffn1": 8, "ffn2": 9, "dilated": 10, "ffn3": 11}
        NORM = {n: 6 + i for i, n in enumerate(
            ["ffn0", "ffn0_out", "pool", "pool_out", "ffn1", "ffn1_out", "ffn2", "ffn2_out",
             "dilated", "dilated_out", "ffn3", "ffn3_out"])}
        SQ = {n: 8 * (i - 6) + 32 for n, i in NORM.items()}
        X_NEW = {"ffn0": None, "pool": 0, "ffn1": 8, "ffn2": 16, "dilated": 24, "ffn3": 32}
        GAIN = {"ffn0": 0, "ffn0_out": 1, "pool": 2, "pool_out": 3, "ffn1": 4, "ffn1_out": 5, "ffn2": 6,
                "ffn2_out": 7, "dilated": 8, "dilated_out": 9, "ffn3": 10, "ffn3_out": 11, "keys": 12}
        COPIES = 12

        def units():
            for t in range(4):
                for h in range(2):
                    for qt in range(NT):
                        r, k0 = slice(64 * h, 64 * h + 64), max(qt - 1, 0)
                        yield dict(q=heads[r, t, qt * P:qt * P + P], keys=[(heads[r, 4, k0 * P:qt * P + P], 0)],
                                   W=(qt - k0 + 1) * P, mask=mask_a[:, (0 if qt else P):2 * P], scale=0.125,
                                   sink=4 * h + t, v=[va[:, b, 64 * h:64 * h + 64] for b in range(k0, qt + 1)],
                                   row=64 * h, tile=t, at=qt * P)
            for h in range(4):
                for qt in range(NT):
                    yield dict(q=qc[0:96, h, qt * P:qt * P + P], keys=[(kc[0:96, h, 0:qt * P + P], 0)],
                               W=(qt + 1) * P, mask=mask_c[:, (3 - qt) * P:T], scale=96 ** -0.5, sink=None,
                               v=[vc[:, b, 64 * h:64 * h + 64] for b in range(qt + 1)],
                               row=64 * (h % 2), tile=6 + h // 2, at=qt * P)
            for h in range(4):
                for qt in range(NT):
                    r = slice(64 * (h % 2), 64 * (h % 2) + 64)
                    yield dict(q=heads[r, 5 + h // 2, qt * P:qt * P + P], keys=[(heads[r, 7, 0:qt * P + P], 0)],
                               W=(qt + 1) * P, mask=maskb[:, qt, 0:(qt + 1) * P], scale=0.125, sink=None,
                               v=[vb[:, b, 0:64] for b in range(qt + 1)],
                               row=64 * (h % 2), tile=4 + h // 2, at=qt * P)

        def units_d():
            for h in range(2):
                r = slice(64 * h, 64 * h + 64)
                for c in range(4):
                    cols = slice(c * P, c * P + P)
                    yield dict(q=[dq[r, g, cols] for g in range(3)],
                               keys=[(dq[r, 3, :], 0), (dq[r, 4, cols], T), (dq[r, 5, cols], T + P)],
                               W=T + 2 * P, mask=c, scale=0.125, sink=None,
                               v=[dv[:, b, 64 * h:64 * h + 64] for b in range(4)]
                                 + [dv[:, c, g * P + 64 * h:g * P + 64 * h + 64] for g in (1, 2)],
                               row=64 * h, at=c * P)

        def by_class(t, ordered=False):
            return t.rearrange("p (c i) -> p c i", c=4) if ordered else t.rearrange("p (i c) -> p c i", c=4)

        def norm_tile(m):
            return (tmp, rot)[m // 2 % 2][:, m % 2, :]

        UN, UD = list(units()), list(units_d())
        IX = [(qt, h) for qt in range(1, NT) for h in range(4)]

        waited = sem("waited")

        def hold(eng, sem_, value):
            eng.wait_ge(sem_, value)
            eng.sem_inc(waited, 1)

        block = ctx.enter_context(nc.Block())

        @block.sync
        def _(sp):
            def load(jp, s, n, src):
                sp.wait_ge(w_split, 2 * jp + s + 1)
                sp.dma_start(stage[:, s, 0:n], src).then_inc(w_landed[s], 16)

            sp.dma_start(flat(x), a["xT"]).then_inc(x_landed, 16)
            load(0, 0, W_FULL, a["w_in"][0])
            load(0, 1, W_FULL, a["w_in"][1])
            for dst, src in ((flat(tabs), a["tab"]), (tabc[:, :], a["tabc"]),
                             (mask_a[:, :], a["mask_a"]), (mask_c[:, :], a["mask_c"]), (tri[:, :], a["tri"]),
                             (ident[:, :], a["ident"]), (wr[:, :], a["w_router"]),
                             (rbias[:, :].rearrange("p (a n) -> p a n", a=1), a["rbias"].partition_broadcast(P)), (flat(ngain), a["ngain"])):
                sp.dma_start(dst, src).then_inc(const_landed, 16)
            with sp.Fori(0, L) as l:
                j = l * JL
                sp.wait_ge(place_free, l + 1)
                sp.dma_start(nsink[:, :].rearrange("p (a n) -> p a n", a=1), a["nsink"][bass.ds(l, 1), :].partition_broadcast(P)).then_inc(layer_landed, 16)
                sp.dma_start(cg[:, :], one(a["c_g"], l)).then_inc(layer_landed, 16)
                sp.dma_start(flat(lng), one(a["ln"], l)).then_inc(layer_landed, 16)
                load(j + 1, 0, W_FULL, one(a["w_in"], l * 15 + 2))
                load(j + 1, 1, W_KR, one(a["w_kr"], l))
                load(j + 2, 0, W_VA, one(a["w_in"], l * 15 + 3))
                load(j + 2, 1, W_VB, one(a["w_vb"], l))
                with sp.Fori(0, 5) as i:
                    for s in range(2):
                        load(j + 3 + i, s, W_FULL, one(a["w_in"], l * 15 + 4 + s + 2 * i))
                load(j + 8, 0, W_FULL, one(a["w_in"], l * 15 + 14))
                load(j + 8, 1, W_UP, one(a["w_up"], l))
                with sp.Fori(0, 4) as i:
                    for s in range(2):
                        load(j + 9 + i, s, W_FULL, one(a["w_out"], l * 8 + 2 * i + s))
                with sp.Fori(0, 4) as q:
                    with sp.Fori(0, 8) as i:
                        for s in range(2):
                            load(j + J_MOE // 2 + q * 12 + i, s, W_FULL, one(a["w_gu"], l * 64 + q * 16 + 2 * i + s))
                    with sp.Fori(0, 4) as i:
                        for s in range(2):
                            load(j + J_MOE // 2 + 8 + q * 12 + i, s, W_FULL, one(a["w_dn"], l * 32 + q * 8 + 2 * i + s))
                for s in range(2):
                    load(j + JL, s, W_FULL, one(a["next_in"], 2 * l + s))
            for name in SECOND:
                j = JS[name]
                if name[0] == "f":
                    n = int(name[3])
                    for g in range(2):
                        first = 1 if n + g == 0 else 0
                        with sp.Fori(first, GK) as i:
                            for s in range(2):
                                load(j + 15 * g + i, s, W_FULL, one(a["f_gu"], n * 44 + g * 22 + s + 2 * i))
                        with sp.Fori(0, 4) as i:
                            for s in range(2):
                                load(j + 15 * g + 11 + i, s, W_DOWN, one(a["f_dn"], n * 16 + g * 8 + s + 2 * i))
                elif name == "pool":
                    for s in range(2):
                        load(j, s, W_FULL, a["p_in"][s])
                    sp.wait_ge(place_free, L + 2)
                    sp.dma_start(flat(cnt), a["p_cnt"]).then_inc(late_landed, 16)
                    sp.dma_start(pgain[:, :], a["p_scale"]).then_inc(late_landed, 16)
                    for w, n, o, i0 in (("p_in", W_FULL, 0, 1), ("p_grp", 2 * P, 4, 0), ("p_out", W_FULL, 8, 0)):
                        with sp.Fori(i0, 4) as i:
                            for s in range(2):
                                load(j + o + i, s, n, one(a[w], 2 * i + s))
                else:
                    for s in range(2):
                        load(j, s, W_FULL, a["d_qk"][s])
                    def pair(p):
                        with sp.Fori(1, 3) as i:
                            for s in range(2):
                                load(j + p * 5 + i, s, W_FULL, one(a["d_qk"], p * 6 + 2 * i + s))
                        with sp.Fori(0, 2) as i:
                            for s in range(2):
                                load(j + p * 5 + 3 + i, s, KD * 96, one(a["d_v"], p * 4 + 2 * i + s))

                    with sp.Fori(0, 3) as p:
                        pair(p)
                        for s in range(2):
                            load(j + p * 5 + 5, s, W_FULL, one(a["d_qk"], p * 6 + 6 + s))
                    pair(3)
                    with sp.Fori(0, 4) as i:
                        for s in range(2):
                            load(j + 20 + i, s, 4 * P, one(a["d_out"], 2 * i + s))
            for m in range(0, KD, 2):
                sp.wait_ge(y_final, m + 2)
                sp.dma_start(out[:, m * T:(m + 2) * T], x[:, m:m + 2, :].rearrange("p k t -> p (k t)")).then_inc(out_stored, 16)
            sp.wait_ge(out_stored, 64)

        @block.gpsimd
        def _(pool):
            nc.gpsimd.memset(ones[:, :], 1.0).then_inc(consts_made, 1)
            nc.gpsimd.memset(pick[:, :], 0.0)
            pool.drain()
            for i in range(8):
                nc.gpsimd.memset(pick[:, 9 * i:9 * i + 1], 1.0).then_inc(consts_made, 1)
            with pool.Fori(0, L) as l:
                hold(pool, kr_ready, l + 1)
                for h in range(4):
                    nc.gpsimd.tensor_copy(kc[64:96, h, :], krope[64:96, :]).then_inc(kr_copied, 1)
                hold(pool, gt_copied, l + 1)
                pool.dma_start(gates_dram, gates_t[:, :]).then_inc(gates_stored, 16)
                hold(pool, gates_stored, l * 16 + 16)
                with pool.Fori(0, E) as e:
                    hold(pool, gb_used, l * E + e + 1)
                    pool.dma_start(gb[:, :].rearrange("p (a t) -> p a t", a=1), gates_dram[bass.ds(e, 1), :].partition_broadcast(P)).then_inc(gb_landed, 16)
            hold(pool, place_free, L + 1)
            pool.dma_start(dcol[:, :], a["dcol"]).then_inc(pos_landed, 16)
            pool.dma_start(sum1[:, :].bitcast(I32).rearrange("p (a t) -> p a t", a=1), a["pos"].partition_broadcast(P)).then_inc(pos_landed, 16)
            hold(pool, hk_split, KD)
            for t, d in ((hs_hi, keys_dram[0]), (hs_lo, keys_dram[1])):
                pool.dma_start(d, t[:, GK - KD:GK, :].rearrange("p k t -> p (k t)")).then_inc(hk_stored, 16)
            hold(pool, hk_stored, 32)
            hold(pool, acc_full, 2 * (AS["ffn2"] + 30))
            for t, d in ((ks_hi, keys_dram[0]), (ks_lo, keys_dram[1])):
                pool.dma_start(flat(t), d).then_inc(hk_landed, 16)
            hold(pool, place_free, L + 3)
            pool.dma_start(flat(mask_d), a["mask_d"]).then_inc(mask_landed, 16)

        @block.tensor
        def _(pe):
            def three(o, lh, ll, rh, rl_, start, stop):
                pe.matmul(o, lh, rh, start=start, stop=False)
                pe.matmul(o, lh, rl_, start=False, stop=False)
                return pe.matmul(o, ll, rh, start=False, stop=stop)

            def begin(jp, s, ap, b):
                pe.wait_ge(w_split, 2 * jp + s + 1 + RING)
                pe.wait_ge(acc_free[b], ap + 1)

            def job(jp, s, ap, b, hi, lo, K=KD, M=P, waits=None):
                begin(jp, s, ap, b)
                for k in range(K):
                    if waits is not None:
                        pe.wait_ge(waits[0], waits[1] + k + 1)
                    last = three(ps[0:M, b, :], w_hi[:, s, k * M:k * M + M], w_lo[:, s, k * M:k * M + M],
                                 hi[:, k, :], lo[:, k, :], k == 0, k == K - 1)
                last.then_inc(acc_full, 1)

            def turn(n, b, N, bank):
                pe.wait_ge(v_evacuated, n + 1)
                for t in range(NT):
                    last = pe.transpose(ps[:, bank, t * N:t * N + N], rot[0:N, b, t * P:t * P + P], ident[0:N, 0:N])
                last.then_inc(v_turned, 1)

            def stats(n, tables):
                pe.wait_ge(stat_in, n + 1)
                for i, t in enumerate(tables):
                    for q in range(NT):
                        last = pe.matmul(ps[:, STAT, 4 * i + q:4 * i + q + 1], t[:, q * P:q * P + P], ones[:, 0:1],
                                         start=True, stop=True)
                last.then_inc(stat_full, 1)

            def add_stats(n0, m, values=None):
                pe.wait_ge(sq_ready, n0 + m + 1)
                for q in range(NT):
                    at = slice(q * P, q * P + P)
                    if values is not None:
                        pe.matmul(ps[:, STAT, 0:8], values[:, m, at], pick[:, 8 * q + 32:8 * q + 40],
                                  start=m == 0 and q == 0, stop=False)
                    last = pe.matmul(ps[:, STAT, 0:8], sq[:, m % 2, at], pick[:, 8 * q:8 * q + 8],
                                     start=m == 0 and q == 0 and values is None, stop=m == KD - 1 and q == NT - 1)
                last.then_inc(sq_used, 1)

            def all_stats(n0):
                for m in range(KD):
                    add_stats(n0, m)

            def with_stats(n0, tile_job, values=None):
                for m in range(KD + 2):
                    if m < KD:
                        tile_job(m)
                    if m >= 2:
                        add_stats(n0, m - 2, values)

            def spread(n, banks):
                pe.wait_ge(rstd_ready, n + 1)
                for i, b in enumerate(banks):
                    for q in range(NT):
                        last = pe.matmul(ps[:, b, q * P:q * P + P],
                                         small[:, 4 * i + q:4 * i + q + 1].to_broadcast([P, P]), ident[:, :],
                                         start=True, stop=True)
                last.then_inc(rb_full, 1)

            def scores(u, n, ring, dn=None):
                un = u[n]
                b = 2 + ring * (n % 2)
                q = un["q"] if isinstance(un["q"], list) else [un["q"]]
                for i, (k, at) in enumerate(un["keys"]):
                    w = k.shape[-1]
                    last = pe.matmul(ps[:, b + at // T, at % T:at % T + w], q[i], k, start=True, stop=True)
                last.then_inc(s_full, 1)

            def transposes(un, n, c0, probs, bank):
                pe.wait_ge(p_norm, c0 + n + 1)
                for i in range(un["W"] // P):
                    last = pe.transpose(ps[:, bank + i // 4, (i % 4) * P:(i % 4) * P + P], probs[:, n % 2, i * P:i * P + P],
                                        ident[:, :])
                last.then_inc(pt_full, 1)

            def mix(un, n, c0, probs_t, o):
                pe.wait_ge(pt_copied, c0 + n + 1)
                if n >= 2:
                    pe.wait_ge(o_split, c0 + n - 1)
                nb = un["W"] // P
                for i in range(nb):
                    last = pe.matmul(o, un["v"][i], probs_t[:, i * P:i * P + P], start=(i == 0), stop=(i == nb - 1))
                last.then_inc(o_full, 1)

            pe.wait_ge(consts_made, 9)
            pe.wait_ge(const_landed, 144)
            with pe.Fori(0, L) as l:
                j, c = l * JL, l * AL
                for i in range(4):
                    job(j + i // 2, i % 2, c + i // 2, i % 2, xs_hi, xs_lo, M=64 if i == 3 else P,
                        waits=(xs_ready, l * 16) if i == 0 else None)
                job(j + 2, 0, c + 2, 0, xs_hi, xs_lo)
                job(j + 2, 1, c + 2, 1, xs_hi, xs_lo, M=68)
                turn(2 * l, 0, P, 5)
                turn(2 * l + 1, 1, 68, 6)
                stats(l, [sum2, sum1])
                with pe.Fori(0, 5) as i:
                    for s in range(2):
                        job(j + 3 + i, s, c + 3 + i, s, xs_hi, xs_lo)
                spread(3 * l, [RB, MB])
                job(j + 8, 0, c + 8, 0, xs_hi, xs_lo)
                pe.wait_ge(w_split, 2 * (j + 8) + 2 + RING)
                for i in range(4):
                    pe.wait_ge(acc_free[(i + 1) % 2], c + 8 + (i + 1) // 2 + 1)
                    for k in range(2):
                        if i == 0:
                            pe.wait_ge(c_ready, l * 3 + k + 1)
                        m = i * 2 * P + k * P
                        last = three(ps[:, (i + 1) % 2, :], w_hi[:, 1, m:m + P], w_lo[:, 1, m:m + P],
                                     cs_hi[:, k, :], cs_lo[:, k, :], k == 0, k == 1)
                    last.then_inc(acc_full, 1)
                pe.wait_ge(c_ready, l * 3 + 3)
                for i in range(2):
                    pe.wait_ge(acc_free[(i + 1) % 2], c + 10 + (i + 1) // 2 + 1)
                    m = 8 * P + i * P
                    three(ps[:, (i + 1) % 2, :], w_hi[:, 1, m:m + P], w_lo[:, 1, m:m + P],
                          cs_hi[:, 2, :], cs_lo[:, 2, :], True, True).then_inc(acc_full, 1)
                for i in range(2):
                    pe.wait_ge(acc_free[(i + 1) % 2], c + 11 + (i + 1) // 2 + 1)
                    for t in (2 * i, 2 * i + 1):
                        last = three(ps[:, (i + 1) % 2, 256 * (t % 2):256 * (t % 2) + 256],
                                     cs_hi[:, 2, t * P:t * P + P], cs_lo[:, 2, t * P:t * P + P],
                                     w_hi[:, 1, 10 * P:12 * P], w_lo[:, 1, 10 * P:12 * P], True, True)
                    last.then_inc(acc_full, 1)
                pe.wait_ge(heads_ready, l * N_ROPE + N_ROPE)
                for n, (qt, h) in enumerate(IX):
                    if n >= 2:
                        pe.wait_ge(ix_relu, l * len(IX) + n - 1)
                    r = slice(64 * (h % 2), 64 * (h % 2) + 64)
                    pe.matmul(ps[:, 2 + n % 2, 0:(qt + 1) * P], heads[r, 8 + h // 2, qt * P:qt * P + P],
                              heads[r, 10, 0:(qt + 1) * P], start=True, stop=True).then_inc(ix_full, 1)
                pe.wait_ge(ix_relu, l * len(IX) + len(IX))
                pe.wait_ge(act_copied, l * COPIES + COPIES)
                pe.wait_ge(qc_ready, l * 4 + 4)
                pe.wait_ge(kr_copied, l * 4 + 4)
                u0_ = l * UNITS
                scores(UN, 0, 1)
                scores(UN, 1, 1)
                for n, un in enumerate(UN):
                    transposes(un, n, u0_, prob, 4 + n % 2)
                    if n + 2 < UNITS:
                        scores(UN, n + 2, 1)
                    mix(un, n, u0_, probt[:, n % 2, :], ps[un["row"]:un["row"] + 64, 6 + n % 2, 0:P])
                hold(pe, o_split, u0_ + UNITS)
                with_stats(l * 16, lambda m: job(j + 9 + m // 2, m % 2, c + 12 + (m + 1) // 2, 1 - m % 2, xs_hi, xs_lo), x)
                spread(3 * l + 1, [RB, MB])
                pe.wait_ge(wr_ready, 1)
                pe.wait_ge(acc_free[1], c + 17)
                for k in range(KD):
                    pe.wait_ge(xs_ready, l * 16 + 8 + k + 1)
                    last = three(ps[0:E, 1, :], wr_hi[:, k * E:k * E + E], wr_lo[:, k * E:k * E + E],
                                 xs_hi[:, k, :], xs_lo[:, k, :], k == 0, k == KD - 1)
                last.then_inc(acc_full, 1)
                hold(pe, logits_copied, l + 1)
                for t in range(NT):
                    last = pe.transpose(ps[:, STAT, t * E:t * E + E], gates_t[:, t * P:t * P + P], ident[0:E, 0:E])
                last.then_inc(logits_full, 1)
                jm, cm = j + J_MOE // 2, c + A_MOE // 2

                def gate_up(q, i):
                    for s in range(2):
                        job(jm + q * 12 + i, s, cm + q * 12 + i, s, xs_hi, xs_lo)

                gate_up(0, 0)
                pe.wait_ge(gates_ready, l + 1)
                for t in range(NT):
                    last = pe.transpose(ps[0:E, STAT, t * P:t * P + P], rt[:, 0, t * E:t * E + E], ident[:, :])
                last.then_inc(gt_full, 1)
                with pe.Fori(0, 3) as q:
                    with pe.Fori(1, 8) as i:
                        gate_up(q, i)
                    with pe.Fori(0, 4) as i:
                        for s in range(2):
                            job(jm + q * 12 + 8 + i, s, cm + q * 12 + 8 + i, s, hs_hi, hs_lo,
                                waits=(h_ready, l * 32 + q * 8) if s == 0 else None)
                    gate_up(q + 1, 0)
                with pe.Fori(1, 8) as i:
                    gate_up(3, i)
                with_stats(l * 16 + 8, lambda m: job(jm + 44 + m // 2, m % 2, cm + 44 + m // 2, m % 2, hs_hi, hs_lo,
                                                     waits=(h_ready, l * 32 + 24) if m == 0 else None), y)
                spread(3 * l + 2, [RB, MB])

            def start(name):
                all_stats(SQ[name])
                spread(NORM[name], [RB])

            def dense(name):
                j, c, n = JS[name], AS[name], int(name[3])
                start(name)
                ready = (xs_ready, FILL[name] * 8)
                for g in range(2):
                    with pe.Fori(0, GK) as i:
                        for s in range(2):
                            job(j + 15 * g + i, s, c + 15 * g + i, s, xs_hi, xs_lo, waits=ready if g + s == 0 else None)
                    h_tiles = (h_ready, 64 + n * 22 + g * GK)
                    if g == 0:
                        with pe.Fori(0, 4) as i:
                            for s in range(2):
                                job(j + 11 + i, s, c + 11 + i, s, hs_hi, hs_lo, K=GK, waits=h_tiles if s == 0 else None)
                with_stats(SQ[name + "_out"],
                           lambda m: job(j + 26 + m // 2, m % 2, c + 26 + m // 2, m % 2, hs_hi, hs_lo, K=GK,
                                         waits=h_tiles if m == 0 else None))
                spread(NORM[name + "_out"], [RB])

            def pooling():
                j, c = JS["pool"], AS["pool"]
                start("pool")
                with pe.Fori(0, 4) as i:
                    for s in range(2):
                        job(j + i, s, c + i, s, xs_hi, xs_lo, waits=(xs_ready, FILL["pool"] * 8) if s == 0 else None)
                for g in range(4):
                    pe.wait_ge(k_ready, 2 * g + 2)
                    for s in range(2):
                        job(j + 4 + g, s, c + 4 + g, s, po_hi[:, 2 * g:2 * g + 2, :], po_lo[:, 2 * g:2 * g + 2, :], K=2)
                with_stats(SQ["pool_out"], lambda m: job(j + 8 + m // 2, m % 2, c + 8 + m // 2, m % 2, xs_hi, xs_lo,
                                                         waits=(xs_ready, FILL["pool_out"] * 8) if m == 0 else None))
                spread(NORM["pool_out"], [RB])

            def dilated():
                j, c = JS["dilated"], AS["dilated"]
                start("dilated")
                with pe.Fori(0, 4) as p:
                    jp, cp = j + p * 5, c + p * 5
                    pe.wait_ge(o_split, L * UNITS + p * 8)
                    for i in range(6):
                        hi, lo = (xs_hi, xs_lo) if i < 3 else (ks_hi, ks_lo)
                        if i == 3:
                            pe.wait_ge(hk_landed, 32)
                        job(jp + i // 2, i % 2, cp + i // 2, i % 2, hi, lo,
                            waits=(xs_ready, FILL["dilated"] * 8) if i == 0 else None)
                    for i in range(4):
                        job(jp + 3 + i // 2, i % 2, cp + 3 + i // 2, i % 2, ks_hi, ks_lo, M=96)
                        if i >= 1:
                            if i == 3:
                                pe.wait_ge(act_copied, L * COPIES + p * 4 + 1)
                            turn(2 * L + p * 4 + i - 1, (i - 1) % 2, 96, 6 + (i - 1) % 2)
                    pe.wait_ge(act_copied, L * COPIES + p * 4 + 2)
                    turn(2 * L + p * 4 + 3, 1, 96, 7)
                    pe.wait_ge(heads_ready, L * N_ROPE + p * 6 + 6)
                    pe.wait_ge(act_copied, L * COPIES + p * 4 + 4)
                    c0 = L * UNITS + p * 8
                    scores(UD, 0, 2)
                    scores(UD, 1, 2)
                    for n, un in enumerate(UD):
                        transposes(un, n, c0, dprob, 6)
                        if n + 2 < 8:
                            scores(UD, n + 2, 2)
                        mix(un, n, c0, dprobt, ps[un["row"]:un["row"] + 64, n % 2, 0:P])
                pe.wait_ge(o_split, L * UNITS + 32)
                with_stats(SQ["dilated_out"],
                           lambda m: job(j + 20 + m // 2, m % 2, c + 20 + m // 2, m % 2, dm_hi, dm_lo, K=4))
                spread(NORM["dilated_out"], [RB])

            dense("ffn0")
            pooling()
            dense("ffn1")
            dense("ffn2")
            dilated()
            dense("ffn3")

        @block.scalar
        def _(act):
            copy = lambda o, i: nc.scalar.activation(o, i, ACT.Copy)

            def split(jp, s, n, free_at=None):
                act.wait_ge(w_landed[s], 16 * jp + 16)
                if free_at is not None:
                    act.wait_ge(acc_full, free_at)
                copy(w_hi[:, s, 0:n], stage[:, s, 0:n]).then_inc(w_hi_done, 1)

            def fill(f, src=None, perm=False):
                for m in range(KD):
                    act.wait_ge(tile_ready, 8 * f + m + 1)
                    s_, d = (tmp[:, m % 2, :] if src is None else src(m)), xs_hi[:, m, :]
                    if perm:
                        s_, d = by_class(s_), by_class(d, True)
                    copy(d, s_).then_inc(xs_hi_done, 1)

            def square(n, s, t):
                act.wait_ge(sq_used, n + 1)
                nc.scalar.activation(sq[:, s:s + 1, :], t, ACT.Square).then_inc(sq_ready, 1)

            def squares_of_x(name):
                for m in range(KD):
                    if X_NEW[name] is not None:
                        act.wait_ge(x_new, X_NEW[name] + m + 1)
                    square(SQ[name] + m, m % 2, x[:, m:m + 1, :])

            def layer_norm(f, g):
                for m in range(KD):
                    act.wait_ge(tile_ready, 8 * f + m + 1)
                    for o in (x[:, m, :], xs_hi[:, m, :]):
                        last = nc.scalar.activation(o, norm_tile(m), ACT.Identity, bias=lng[:, g + 1, m:m + 1],
                                                    scale=lng[:, g, m:m + 1])
                    last.then_inc(xs_hi_done, 1)

            def rotate(c2, b, full):
                act.wait_ge(acc_full, c2 + 1)
                for h in range(4):
                    last = copy(rot[32 * h:32 * h + 32, b, :], ps[32 * (h ^ 1):32 * (h ^ 1) + 32, b, :])
                last.then_inc(rot_ready, 1)

            def exps(un, n, c0, probs):
                b = n % 2
                act.wait_ge(masked, c0 + n + 1)
                if un["sink"] is not None:
                    nc.scalar.activation(col[:, b, 2:3], nsink[:, un["sink"]:un["sink"] + 1], ACT.Exp,
                                         bias=col[:, b, 0:1], scale=-1.0)
                nc.scalar.activation(probs[:, b, 0:un["W"]], probs[:, b, 0:un["W"]], ACT.Exp, bias=col[:, b, 0:1],
                                     scale=-1.0, accum_out=col[:, b, 1:2]).then_inc(p_exp, 1)

            def attend(U, c0, probs, probs_t, t_bank, o_of, hi_of, one_t):
                N = len(U)
                exps(U[0], 0, c0, probs)
                for n in range(N + 1):
                    if n + 1 < N:
                        exps(U[n + 1], n + 1, c0, probs)
                    if n < N:
                        W = U[n]["W"]
                        act.wait_ge(pt_full, c0 + n + 1)
                        if n >= (1 if one_t else 2):
                            act.wait_ge(o_full, c0 + n - (0 if one_t else 1))
                        tb = t_bank(n)
                        src = ps[:, tb, 0:W] if W <= T else ps[:, tb:tb + 2, :].rearrange("p b t -> p (b t)")[:, 0:W]
                        copy(probs_t(n)[:, 0:W], src).then_inc(pt_copied, 1)
                    m = n - 1
                    if m >= 0:
                        act.wait_ge(o_full, c0 + m + 1)
                        copy(hi_of(U[m]), o_of(U[m], m)).then_inc(o_hi_done, 1)

            def silu_pair(jp, ap, n, s0, s1):
                split(jp + 1, 0, s0, 2 * ap + 1)
                act.wait_ge(sg_used, n + 1)
                nc.scalar.activation(sg[:, :], ps[:, 0, :], ACT.Silu).then_inc(sg_ready, 1)
                act.drain().then_inc(acc_free[0], 1)
                split(jp + 1, 1, s1, 2 * ap + 2)

            def down_squares(n0, j1, c1, n_w, n_next, Y=y):
                with act.Fori(0, 3) as i:
                    for s in range(2):
                        split(j1 + i, s, n_w, 2 * (c1 + i) + s + 1)
                        act.wait_ge(acc_free[s], c1 + 2 + i)
                        square(n0 + 2 * i + s, s, Y[:, bass.ds(2 * i + s, 1), :])
                if n_next is not None:
                    split(j1 + 3, 0, n_next, 2 * (c1 + 3) + 1)
                for s in range(2):
                    act.wait_ge(acc_free[s], c1 + 5)
                    square(n0 + 6 + s, s, Y[:, 6 + s:7 + s, :])
                if n_next is not None:
                    split(j1 + 3, 1, n_next, 2 * (c1 + 3) + 2)

            act.wait_ge(x_landed, 16)
            for m in range(KD):
                copy(xs_hi[:, m, :], x[:, m, :]).then_inc(xs_hi_done, 1)
            split(0, 0, W_FULL)
            split(0, 1, W_FULL)
            act.wait_ge(const_landed, 144)
            copy(wr_hi[:, :], wr[:, :]).then_inc(wr_hi_done, 1)
            with act.Fori(0, L) as l:
                j, c = l * JL, l * AL
                act.preload_act_table(ACT.Exp)
                for i in range(3):
                    split(j + 1 + i // 2, i % 2, (W_FULL, W_KR, W_VA)[i], 2 * c + i + 1)
                    act.wait_ge(acc_full, 2 * c + i + 1)
                    copy(cfeat[:, i, :], ps[:, i % 2, :]).then_inc(c_copied, 1)
                    act.drain().then_inc(acc_free[i % 2], 1)
                act.wait_ge(acc_full, 2 * c + 4)
                split(j + 2, 1, W_VB, 2 * c + 4)
                for s, N in ((0, P), (1, 68)):
                    act.wait_ge(acc_full, 2 * c + 5 + s)
                    copy(rot[0:N, s, :], ps[0:N, s, :]).then_inc(v_evacuated, 1)
                    act.drain().then_inc(acc_free[s], 1)
                    split(j + 3, s, W_FULL, 2 * c + 5 + s)
                for s, N, o in ((0, P, va), (1, 68, vb)):
                    act.wait_ge(v_turned, 2 * l + s + 1)
                    copy(flat(o), ps[:, 5 + s, 0:NT * N]).then_inc(act_copied, 1)
                with act.Fori(0, 4) as i:
                    for s in range(2):
                        split(j + 4 + i, s, W_FULL, 2 * (c + 3 + i) + s + 1)
                        rotate(2 * (c + 3 + i) + s, s, True)
                for s in range(2):
                    split(j + 8, s, (W_FULL, W_UP)[s], 2 * (c + 7) + s + 1)
                    rotate(2 * (c + 7) + s, s, True)
                for i in range(3):
                    act.wait_ge(c_tile, 3 * l + i + 1)
                    copy(cs_hi[:, i, :], cfeat[:, i, :]).then_inc(c_hi_done, 1)
                split(j + 9, 0, W_FULL, 2 * c + 17)
                rotate(2 * c + 16, 0, True)
                for i in range(4):
                    act.wait_ge(acc_full, 2 * c + 18 + i)
                    copy(qc[0:64, i, :], ps[0:64, (i + 1) % 2, :]).then_inc(act_copied, 1)
                for i in range(2):
                    act.wait_ge(acc_full, 2 * c + 22 + i)
                    copy(kc[0:64, 2 * i, :], ps[0:64, (i + 1) % 2, :]).then_inc(act_copied, 1)
                    copy(kc[0:64, 2 * i + 1, :], ps[64:128, (i + 1) % 2, :]).then_inc(act_copied, 1)
                    act.drain().then_inc(acc_free[(i + 1) % 2], 1)
                for i in range(2):
                    act.wait_ge(acc_full, 2 * c + 24 + i)
                    copy(vc[:, 2 * i:2 * i + 2, :].rearrange("p a b -> p (a b)"), ps[:, (i + 1) % 2, :]).then_inc(act_copied, 1)
                    act.drain().then_inc(acc_free[(i + 1) % 2], 1)
                split(j + 9, 1, W_FULL, 2 * c + 25)
                for n, (qt, h) in enumerate(IX):
                    act.wait_ge(ix_full, l * len(IX) + n + 1)
                    if n >= 2:
                        act.wait_ge(ix_used, l * len(IX) + n - 1)
                    nc.scalar.activation(rl[:, n % 2, 0:(qt + 1) * P], ps[:, 2 + n % 2, 0:(qt + 1) * P], ACT.Relu,
                                         scale=1.0 / 16).then_inc(ix_relu, 1)
                attend(UN, l * UNITS, prob, lambda n: probt[:, n % 2, :], lambda n: 4 + n % 2,
                       lambda un, n: ps[un["row"]:un["row"] + 64, 6 + n % 2, 0:P],
                       lambda un: xs_hi[un["row"]:un["row"] + 64, un["tile"], un["at"]:un["at"] + P], False)
                for m in range(KD):
                    split(j + 10 + m // 2, m % 2, W_FULL, 2 * (c + 12) + m + 2)
                    act.wait_ge(acc_free[1 - m % 2], c + 14 + (m + 1) // 2)
                    square(l * 16 + m, m % 2, x[:, m:m + 1, :])
                layer_norm(2 * l + 1, 0)
                act.wait_ge(acc_full, 2 * c + 34)
                copy(gates_t[:, :], ps[0:E, 1, :]).then_inc(logits_copied, 1)
                act.drain().then_inc(acc_free[1], 1)
                act.wait_ge(logits_full, l + 1)
                nc.scalar.activation(rt[:, 1, :], ps[:, STAT, 0:NT * E], ACT.Tanh, scale=0.5).then_inc(r_tanh, 1)
                act.wait_ge(gt_full, l + 1)
                copy(gates_t[:, :], ps[0:E, STAT, :]).then_inc(gt_copied, 1)
                act.preload_act_table(ACT.Silu)
                jm, cm = j + J_MOE // 2, c + A_MOE // 2

                def gate_up(q):
                    with act.Fori(0, 8) as i:
                        silu_pair(jm + q * 12 + i, cm + q * 12 + i, l * 32 + q * 8 + i, W_FULL, W_FULL)

                with act.Fori(0, 3) as q:
                    gate_up(q)
                    with act.Fori(0, 4) as i:
                        for s in range(2):
                            split(jm + q * 12 + 9 + i, s, W_FULL, 2 * (cm + q * 12 + 8 + i) + s + 1)
                gate_up(3)
                down_squares(l * 16 + 8, jm + 45, cm + 44, W_FULL, W_FULL)
                layer_norm(2 * l + 2, 2)

            def dense(name, last=False):
                j, c, n = JS[name], AS[name], int(name[3])
                squares_of_x(name)
                fill(FILL[name])
                if name == "ffn0":
                    for i in range(2):
                        act.wait_ge(tab_in, i + 1)
                        nc.scalar.activation(dtab[:, i, :], dtab[:, i, :], ACT.Sin).then_inc(tab_done, 1)
                if name == "ffn2":
                    for m in range(KD):
                        act.wait_ge(hk_ready, m + 1)
                        copy(by_class(hs_hi[:, GK - KD + m, :], True), by_class(y[:, m, :])).then_inc(hk_hi_done, 1)
                act.preload_act_table(ACT.Silu)
                for g in range(2):
                    jg, c_g, n_g = j + 15 * g, c + 15 * g, 64 + 22 * n + GK * g
                    with act.Fori(0, GK - 1) as i:
                        silu_pair(jg + i, c_g + i, n_g + i, W_FULL, W_FULL)
                    silu_pair(jg + 10, c_g + 10, n_g + 10, W_DOWN, W_DOWN)
                    if g == 0:
                        with act.Fori(0, 3) as i:
                            for s in range(2):
                                split(jg + 12 + i, s, W_DOWN, 2 * (c_g + 11 + i) + s + 1)
                        for s in range(2):
                            split(jg + 15, s, W_FULL, 2 * (c_g + 14) + s + 1)
                down_squares(SQ[name + "_out"], j + 27, c + 26, W_DOWN, None if last else W_FULL)

            dense("ffn0")
            j, c = JS["pool"], AS["pool"]
            squares_of_x("pool")
            fill(FILL["pool"])
            for m in range(8):
                n_w = W_FULL if m < 6 else 2 * P
                split(j + 1 + m // 2, m % 2, n_w, 2 * c + m + 1)
                act.wait_ge(c_tile, 3 * L + m + 1)
                copy(po_hi[:, m, :], tmp[:, m % 2, :]).then_inc(k_hi_done, 1)
            for m in range(8):
                n_w = 2 * P if m < 6 else W_FULL
                split(j + 5 + m // 2, m % 2, n_w, 2 * c + 8 + m + 1)
                act.wait_ge(tile_ready, 8 * FILL["pool_out"] + m + 1)
                copy(xs_hi[:, m, :], tmp[:, m % 2, :]).then_inc(xs_hi_done, 1)
            down_squares(SQ["pool_out"], j + 9, c + 8, W_FULL, W_FULL)
            dense("ffn1")
            dense("ffn2")
            j, c = JS["dilated"], AS["dilated"]
            squares_of_x("dilated")
            fill(FILL["dilated"], perm=True)
            act.preload_act_table(ACT.Exp)
            with act.Fori(0, 4) as p:
                jp, cp = j + p * 5, c + p * 5
                for i in range(6):
                    split(jp + 1 + i // 2, i % 2, W_FULL if i < 4 else KD * 96, 2 * cp + i + 1)
                    rotate(2 * cp + i, i % 2, True)
                for i in range(5):
                    if i < 4:
                        act.wait_ge(acc_full, 2 * cp + 7 + i)
                        copy(rot[0:96, i % 2, :], ps[0:96, i % 2, :]).then_inc(v_evacuated, 1)
                        act.drain().then_inc(acc_free[i % 2], 1)
                        split(jp + 4 + i // 2, i % 2, KD * 96 if i < 2 else W_FULL, 2 * cp + 7 + i)
                    if i >= 1:
                        act.wait_ge(v_turned, 2 * L + p * 4 + i)
                        copy(dv[:, :, 96 * (i - 1):96 * i],
                             ps[:, 6 + (i - 1) % 2, 0:384].rearrange("p (t n) -> p t n", t=4)).then_inc(act_copied, 1)
                attend(UD, L * UNITS + p * 8, dprob, lambda n: dprobt[:, :], lambda n: 6,
                       lambda un, n: ps[un["row"]:un["row"] + 64, n % 2, 0:P],
                       lambda un: dm_hi[un["row"]:un["row"] + 64, bass.ds(p, 1), un["at"]:un["at"] + P], True)
            down_squares(SQ["dilated_out"], j + 21, c + 20, 4 * P, W_FULL, yd)
            dense("ffn3", last=True)
        @block.vector
        def _(v):
            V = nc.vector
            tt, ts, stt = V.tensor_tensor, V.tensor_scalar, V.scalar_tensor_tensor

            def split(jp, s, n):
                v.wait_ge(w_hi_done, 2 * jp + s + 1)
                tt(w_lo[:, s, 0:n], stage[:, s, 0:n], w_hi[:, s, 0:n].bitcast(F32), ALU.subtract).then_inc(w_split, 1)

            def fill(f, make, src=None, perm=False):
                for m in range(KD + 1):
                    if m < KD:
                        make(m)
                    if m >= 1:
                        v.wait_ge(xs_hi_done, 8 * f + m)
                        s_, hi, lo = (tmp[:, (m - 1) % 2, :] if src is None else src(m - 1)), xs_hi[:, m - 1, :], xs_lo[:, m - 1, :]
                        if perm:
                            s_, hi, lo = (s_.rearrange("p (i c) -> p c i", c=4), hi.rearrange("p (c i) -> p c i", c=4),
                                          lo.rearrange("p (c i) -> p c i", c=4))
                        tt(lo, s_, hi.bitcast(F32), ALU.subtract).then_inc(xs_ready, 1)

            def norm_columns(n, kind, n0, half=False):
                if kind == "c":
                    v.drain().then_inc(stat_in, 1)
                    v.wait_ge(stat_full, n0 + 1)
                else:
                    v.wait_ge(sq_used, n0 + KD + 2)
                r, mean, var, t = small[:, 0:8], small[:, 8:12], small[:, 16:24], small[:, 24:32]
                w = 8 if kind == "c" else 4
                if kind == "ln":
                    ts(mean, ps[:, STAT, 4:8], 1.0 / D, None, ALU.mult)
                    v.drain()
                    tt(t[:, 0:4], mean, mean, ALU.mult)
                    v.drain()
                    stt(var[:, 0:4], ps[:, STAT, 0:4], 1.0 / D, t[:, 0:4], ALU.mult, ALU.subtract)
                    v.drain()
                    ts(var[:, 0:4], var[:, 0:4], LN_EPS, None, ALU.add)
                elif kind == "rms":
                    ts(var[:, 0:4], ps[:, STAT, 0:4], 1.0 / D, RMS_EPS, ALU.mult, ALU.add)
                else:
                    ts(var[:, 0:4], ps[:, STAT, 0:4], 1.0 / 256, RMS_EPS, ALU.mult, ALU.add)
                    ts(var[:, 4:8], ps[:, STAT, 4:8], 1.0 / 128, RMS_EPS, ALU.mult, ALU.add)
                v.drain()
                r, var, t = r[:, 0:w], var[:, 0:w], t[:, 0:w]
                ts(t.bitcast(I32), var.bitcast(I32), 1, None, ALU.logical_shift_right)
                v.drain()
                ts(r.bitcast(I32), t.bitcast(I32), -1.0, float(0x5F3759DF), ALU.mult, ALU.add)
                v.drain()
                for _ in range(3):
                    stt(t, r, -0.5, r, ALU.mult, ALU.mult)
                    v.drain()
                    tt(t, t, var, ALU.mult)
                    v.drain()
                    stt(r, t, 1.5, r, ALU.add, ALU.mult)
                    v.drain()
                if half:
                    ts(r, r, 0.5, None, ALU.mult)
                if kind == "ln":
                    stt(small[:, 4:8], mean, -1.0, r, ALU.mult, ALU.mult)
                v.drain().then_inc(rstd_ready, 1)

            def norm(n, kind, n0, half=False, meanwhile=None):
                norm_columns(n, kind, n0, half)
                if meanwhile is not None:
                    meanwhile()
                hold(v, rb_full, n + 1)

            def layer_norm(n, f, src, n0, meanwhile=None):
                norm(n, "ln", n0, meanwhile=meanwhile)
                for i in range(KD + 3):
                    if i < KD:
                        tt(norm_tile(i), src[:, i, :], ps[:, RB, :], ALU.mult)
                    if 1 <= i <= KD:
                        tt(norm_tile(i - 1), norm_tile(i - 1), ps[:, MB, :], ALU.add).then_inc(tile_ready, 1)
                    if i >= 3:
                        m = i - 3
                        v.wait_ge(xs_hi_done, 8 * f + m + 1)
                        tt(xs_lo[:, m, :], x[:, m, :], xs_hi[:, m, :].bitcast(F32), ALU.subtract).then_inc(xs_ready, 1)
                    v.drain()

            def rope(a2, r, b, dst, cos, sin):
                v.wait_ge(acc_full, a2 + 1)
                v.wait_ge(rot_ready, r + 1)
                tt(dst, ps[:, b:b + 1, :], cos, ALU.mult)
                tt(tmp[:, b:b + 1, :], rot[:, b:b + 1, :], sin, ALU.mult).then_inc(acc_free[b], 1)
                v.drain()
                tt(dst, dst, tmp[:, b:b + 1, :], ALU.add).then_inc(heads_ready, 1)

            def mask_scores(un, n, c0, ring, probs):
                b, W, bank = n % 2, un["W"], 2 + ring * (n % 2)
                if n >= 2:
                    v.wait_ge(pt_full, c0 + n - 1)
                hold(v, s_full, c0 + n + 1)
                src = ps[:, bank, 0:W] if ring == 1 else ps[:, bank:bank + 2, :].rearrange("p b t -> p (b t)")[:, 0:W]
                m = un["mask"] if ring == 1 else mask_d[:, un["mask"], :]
                init = 3.0e38 if un["sink"] is None else nsink[:, un["sink"]:un["sink"] + 1]
                V.tensor_tensor_reduce(probs[:, b, 0:W], src, m, -un["scale"], init, ALU.add, ALU.min,
                                       col[:, b, 0:1]).then_inc(masked, 1)

            def normalise(un, n, c0, probs):
                b = n % 2
                v.wait_ge(p_exp, c0 + n + 1)
                if un["sink"] is not None:
                    tt(col[:, b, 1:2], col[:, b, 1:2], col[:, b, 2:3], ALU.add)
                    v.drain()
                V.reciprocal(col[:, b, 3:4], col[:, b, 1:2])
                v.drain()
                ts(probs[:, b, 0:un["W"]], probs[:, b, 0:un["W"]], col[:, b, 3:4], None, ALU.mult).then_inc(p_norm, 1)

            def attend(U, c0, ring, probs, o_of, hi_of, lo_of, lag, between=None):
                N = len(U)
                mask_scores(U[0], 0, c0, ring, probs)
                for n in range(N + lag):
                    if n + 1 < N:
                        mask_scores(U[n + 1], n + 1, c0, ring, probs)
                    if n < N:
                        normalise(U[n], n, c0, probs)
                    m = n - lag
                    if m >= 0:
                        v.wait_ge(o_hi_done, c0 + m + 1)
                        tt(lo_of(U[m]), o_of(U[m], m), hi_of(U[m]).bitcast(F32), ALU.subtract).then_inc(o_split, 1)
                    if between is not None:
                        between(n)

            def out_tile(ap, s, m, Y, add):
                v.wait_ge(acc_full, 2 * ap + s + 1)
                ym = Y[:, bass.ds(m, 1), :]
                if add:
                    tt(ym, ym, ps[:, s:s + 1, :], ALU.add).then_inc(acc_free[s], 1)
                else:
                    ts(ym, ps[:, s:s + 1, :], 1.0, None, ALU.mult).then_inc(acc_free[s], 1)

            def out_tiles(j1, c1, n_w, more, Y, add, tile=None):
                tile = tile or out_tile
                with v.Fori(0, 3) as i:
                    for s in range(2):
                        split(j1 + i, s, n_w)
                        tile(c1 + i, s, 2 * i + s, Y, add)
                if more:
                    split(j1 + 3, 0, W_FULL)
                for s in range(2):
                    tile(c1 + 3, s, 6 + s, Y, add)

            def topk_round(qt):
                work = maskb[:, qt, 0:(qt + 1) * P]
                v.drain()
                V.max(max8[:, :], work)
                v.drain()
                V.match_replace(work, max8[:, :], work, TAKEN)

            def router():
                v4 = lambda i: rt[:, i, :].rearrange("p (g e) -> p g e", e=TOKG)
                scores, biased, rank, sel = rt[:, 2, :], rt[:, 3, :], rt[:, 4, :], rt[:, 5, :]
                ts(scores, rt[:, 1, :], 0.5, 0.5, ALU.mult, ALU.add)
                v.drain()
                tt(biased.rearrange("p (t e) -> p t e", e=E), scores.rearrange("p (t e) -> p t e", e=E),
                   rbias[:, :].unsqueeze(1).to_broadcast([P, NT, E]), ALU.add)
                v.drain()

                def ranks(o, vals, g):
                    other = vals.unsqueeze(2).to_broadcast([P, g, 4, 4])
                    own = vals.unsqueeze(3).to_broadcast([P, g, 4, 4])
                    gt, eq = (pairs[:, i, 0:16 * g].rearrange("p (g j i) -> p g j i", j=4, i=4) for i in range(2))
                    tt(gt, other, own, ALU.is_gt)
                    tt(eq, other, own, ALU.is_equal)
                    v.drain()
                    tt(eq, eq, tri[:, :].rearrange("p (j i) -> p j i", j=4).unsqueeze(1).to_broadcast([P, g, 4, 4]), ALU.mult)
                    v.drain()
                    tt(gt, gt, eq, ALU.add)
                    v.drain()
                    V.tensor_reduce(o, gt, AX.X, ALU.add)
                    v.drain()

                ranks(v4(4), v4(3), 16)
                ts(sel, rank, 1.5, None, ALU.is_lt)
                v.drain()
                tt(rt[:, 6, :], biased, sel, ALU.mult)
                v.drain()
                gsum, grank = rt[:, 7, 0:16], rt[:, 7, 16:32]
                V.tensor_reduce(gsum, v4(6), AX.X, ALU.add)
                v.drain()
                ranks(grank.rearrange("p (t g) -> p t g", g=4), gsum.rearrange("p (t g) -> p t g", g=4), 4)
                ts(grank, grank, 0.5, None, ALU.is_lt)
                v.drain()
                tt(v4(5), v4(5), grank.unsqueeze(2).to_broadcast([P, 16, 4]), ALU.mult)
                v.drain()
                tt(rt[:, 6, :], scores, sel, ALU.mult)
                v.drain()
                total, inv = rt[:, 7, 32:36], rt[:, 7, 36:40]
                V.tensor_reduce(total, rt[:, 6, :].rearrange("p (t e) -> p t e", e=E), AX.X, ALU.add)
                v.drain()
                V.reciprocal(inv, total)
                v.drain()
                tt(rt[:, 0, :].rearrange("p (t e) -> p t e", e=E), rt[:, 6, :].rearrange("p (t e) -> p t e", e=E),
                   inv.unsqueeze(2).to_broadcast([P, NT, E]), ALU.mult).then_inc(gates_ready, 1)

            def hidden(ap, n, k, gate=None, last_of_gate=False):
                v.drain()
                v.wait_ge(sg_ready, n + 1)
                v.wait_ge(acc_full, 2 * ap + 2)
                tt(hh[:, :], sg[:, :], ps[:, 1, :], ALU.mult).then_inc(acc_free[1], 1)
                v.drain().then_inc(sg_used, 1)
                if gate is not None:
                    v.wait_ge(gb_landed, gate)
                    tt(hh[:, :], hh[:, :], gb[:, :], ALU.mult)
                    v.drain()
                    if last_of_gate:
                        v.drain().then_inc(gb_used, 1)
                h3 = hh[:, :].rearrange("p (a t) -> p a t", a=1)
                ts(hs_hi[:, bass.ds(k, 1), :], h3, 1.0, None, ALU.mult)
                v.drain()
                tt(hs_lo[:, bass.ds(k, 1), :], h3, hs_hi[:, bass.ds(k, 1), :].bitcast(F32), ALU.subtract).then_inc(h_ready, 1)

            v.sem_inc(w_split, RING)
            for b in range(RING):
                v.sem_inc(acc_free[b], 1)
            for s_ in (gb_used, sg_used, place_free):
                v.sem_inc(s_, 1)
            v.sem_inc(sq_used, 2)
            v.sem_inc(tile_ready, KD)
            for m in range(KD):
                v.wait_ge(xs_hi_done, m + 1)
                tt(xs_lo[:, m, :], x[:, m, :], xs_hi[:, m, :].bitcast(F32), ALU.subtract).then_inc(xs_ready, 1)
            split(0, 0, W_FULL)
            split(0, 1, W_FULL)
            v.wait_ge(const_landed, 144)
            v.wait_ge(wr_hi_done, 1)
            tt(wr_lo[:, :], wr[:, :], wr_hi[:, :].bitcast(F32), ALU.subtract).then_inc(wr_ready, 1)
            with v.Fori(0, L) as l:
                j, c = l * JL, l * AL
                v.wait_ge(layer_landed, l * 48 + 48)
                ts(nsink[:, :], nsink[:, :], -1.0, None, ALU.mult)
                for i in range(3):
                    split(j + 1 + i // 2, i % 2, (W_FULL, W_KR, W_VA)[i])
                    v.wait_ge(c_copied, 3 * l + i + 1)
                    tt((sum2[:, :], sq[:, 0, :], sum1[:, :])[i], cfeat[:, i, :], cfeat[:, i, :], ALU.mult)
                    if i == 1:
                        v.drain()
                        tt(sum2[:, :], sum2[:, :], sq[:, 0, :], ALU.add)
                split(j + 2, 1, W_VB)
                v.wait_ge(acc_full, 2 * c + 4)
                tt(krope[64:96, :], ps[0:32, 1, :], tabc[0:32, :], ALU.mult)
                tt(tmp[64:96, 1, :], ps[32:64, 1, :], tabc[32:64, :], ALU.mult).then_inc(acc_free[1], 1)
                v.drain()
                tt(krope[64:96, :], krope[64:96, :], tmp[64:96, 1, :], ALU.add).then_inc(kr_ready, 1)
                split(j + 3, 0, W_FULL)
                split(j + 3, 1, W_FULL)
                norm_columns(3 * l, "c", l)
                cos, sin = tabs[:, 0:1, :], tabs[:, 1:2, :]
                with v.Fori(0, 4) as i:
                    for s in range(2):
                        split(j + 4 + i, s, W_FULL)
                        rope(2 * (c + 3 + i) + s, l * N_ROPE + 2 * i + s, s, heads[:, bass.ds(2 * i + s, 1), :], cos, sin)
                for s in range(2):
                    split(j + 8, s, (W_FULL, W_UP)[s])
                    rope(2 * (c + 7) + s, l * N_ROPE + 8 + s, s, heads[:, 8 + s:9 + s, :], cos, sin)
                v.wait_ge(rb_full, 3 * l + 1)
                for i in range(3):
                    stt(cfeat[:, i, :], cfeat[:, i, :], cg[:, i:i + 1], ps[:, (RB, RB, MB)[i], :], ALU.mult, ALU.mult)\
                        .then_inc(c_tile, 1)
                for i in range(3):
                    v.wait_ge(c_hi_done, 3 * l + i + 1)
                    tt(cs_lo[:, i, :], cfeat[:, i, :], cs_hi[:, i, :].bitcast(F32), ALU.subtract).then_inc(c_ready, 1)
                split(j + 9, 0, W_FULL)
                rope(2 * c + 16, l * N_ROPE + 10, 0, heads[:, 10:11, :], cos, sin)
                for i in range(4):
                    b = (i + 1) % 2
                    v.wait_ge(acc_full, 2 * c + 18 + i)
                    v.wait_ge(act_copied, l * COPIES + 3 + i)
                    tt(qc[64:96, i, :], ps[64:96, b, :], tabc[64:96, :], ALU.mult)
                    tt(tmp[64:96, b, :], ps[96:128, b, :], tabc[96:128, :], ALU.mult).then_inc(acc_free[b], 1)
                    v.drain()
                    tt(qc[64:96, i, :], qc[64:96, i, :], tmp[64:96, b, :], ALU.add).then_inc(qc_ready, 1)
                split(j + 9, 1, W_FULL)
                for n, (qt, h) in enumerate(IX):
                    work, src, wcol = maskb[:, qt, 0:(qt + 1) * P], rl[:, n % 2, 0:(qt + 1) * P], vb[:, qt, 64 + h:65 + h]
                    v.drain()
                    v.wait_ge(ix_relu, l * len(IX) + n + 1)
                    if h == 0:
                        ts(work, src, wcol, None, ALU.mult).then_inc(ix_used, 1)
                    else:
                        stt(work, src, wcol, work, ALU.mult, ALU.add).then_inc(ix_used, 1)
                v.drain()
                for qt in range(1, NT):
                    work = maskb[:, qt, 0:(qt + 1) * P]
                    stt(work, mask_c[:, (3 - qt) * P:T], CAUSAL / MASKED, work, ALU.mult, ALU.add)
                V.tensor_copy(maskb[:, 0, 0:P], mask_c[:, 3 * P:T])
                rounds = [(qt, i) for qt in range(1, NT) for i in range(TOPK // 8)]

                def between(n):
                    for qt, i in rounds[n * 24 // 23:(n + 1) * 24 // 23]:
                        topk_round(qt)
                    if n == 45:
                        v.drain()
                        for qt in range(1, NT):
                            work = maskb[:, qt, 0:(qt + 1) * P]
                            ts(work, work, TAKEN * 0.99, MASKED, ALU.is_gt, ALU.mult)
                        v.drain()

                attend(UN, l * UNITS, 1, prob, lambda un, n: ps[un["row"]:un["row"] + 64, 6 + n % 2, 0:P],
                       lambda un: xs_hi[un["row"]:un["row"] + 64, un["tile"], un["at"]:un["at"] + P],
                       lambda un: xs_lo[un["row"]:un["row"] + 64, un["tile"], un["at"]:un["at"] + P], 2, between)
                for m in range(KD):
                    split(j + 10 + m // 2, m % 2, W_FULL)
                    v.wait_ge(acc_full, 2 * (c + 12) + m + 2)
                    b = 1 - m % 2
                    stt(x[:, m, :], x[:, m, :], ALPHA, ps[:, b, :], ALU.mult, ALU.add).then_inc(acc_free[b], 1)
                layer_norm(3 * l + 1, 2 * l + 1, x, l * 16)
                v.wait_ge(r_tanh, l + 1)
                router()
                ts(flat(y), flat(x), ALPHA, None, ALU.mult)
                v.drain()
                jm, cm = j + J_MOE // 2, c + A_MOE // 2

                def experts(q):
                    with v.Fori(0, 4) as e:
                        for f in range(2):
                            for s in range(2):
                                split(jm + q * 12 + 1 + 2 * e + f, s, W_FULL)
                            hidden(cm + q * 12 + 2 * e + f, l * 32 + q * 8 + 2 * e + f, 2 * e + f,
                                   gate=(l * 16 + q * 4 + e) * 16 + 16, last_of_gate=(f == 1))

                with v.Fori(0, 3) as q:
                    experts(q)
                    with v.Fori(0, 4) as i:
                        for s in range(2):
                            split(jm + q * 12 + 9 + i, s, W_FULL)
                            out_tile(cm + q * 12 + 8 + i, s, 2 * i + s, y, True)
                experts(3)
                out_tiles(jm + 45, cm + 44, W_FULL, True, y, True)
                layer_norm(3 * l + 2, 2 * l + 2, y, l * 16 + 8, lambda: split(jm + 48, 1, W_FULL))
                v.drain().then_inc(place_free, 1)

            def rms_fill(name, perm=False):
                def make(m):
                    v.drain()
                    stt(tmp[:, m % 2, :], x[:, m, :], ngain[:, GAIN[name], m:m + 1], ps[:, RB, :], ALU.mult, ALU.mult)\
                        .then_inc(tile_ready, 1)
                norm(NORM[name], "rms", SQ[name])
                fill(FILL[name], make, perm=perm)

            def residual(name, t, half, meanwhile, done=x_new):
                norm(NORM[name], "rms", SQ[name], half, meanwhile)
                for m in range(KD + 1):
                    if m < KD:
                        stt(tmp[:, m % 2, :], t[:, m, :], ngain[:, GAIN[name], m:m + 1], ps[:, RB, :], ALU.mult, ALU.mult)
                    if m >= 1:
                        tt(x[:, m - 1, :], x[:, m - 1, :], tmp[:, (m - 1) % 2, :], ALU.add).then_inc(done, 1)
                    v.drain()

            def dense(name, last=False):
                j, c, n = JS[name], AS[name], int(name[3])
                rms_fill(name)
                for g in range(2):
                    jg, c_g = j + 15 * g, c + 15 * g
                    n_g = 64 + 22 * n + GK * g

                    def gate_up(i0, i1):
                        with v.Fori(i0, i1) as i:
                            for s in range(2):
                                split(jg + 1 + i, s, W_FULL)
                            hidden(c_g + i, n_g + i, i)

                    if name == "ffn0" and g == 0:
                        angles()
                    if name == "ffn2" and g == 0:
                        keys_input()
                        gate_up(0, GK - KD)
                        v.wait_ge(hk_stored, 32)
                        gate_up(GK - KD, GK - 1)
                    else:
                        gate_up(0, GK - 1)
                    for s in range(2):
                        split(jg + GK, s, W_DOWN)
                    hidden(c_g + GK - 1, n_g + GK - 1, GK - 1)
                    if name == "ffn0" and g == 0:
                        v.wait_ge(tab_done, 2)
                        ts(dtab[:, 1, :], dtab[:, 1, :], dcol[:, 1:2], None, ALU.mult)
                    out_tiles(jg + 12, c_g + GK, W_DOWN, not (last and g == 1), y, g == 1)
                    if g == 0:
                        split(jg + 15, 1, W_FULL)
                if name == "ffn0":
                    v.drain().then_inc(place_free, 1)
                residual(name + "_out", y, True, None if last else lambda: split(j + 30, 1, W_FULL),
                         y_final if last else x_new)

            def angles():
                v.wait_ge(pos_landed, 32)
                ang, turns = sum2[:, :], sq[:, 0, :]
                V.tensor_copy(turns, sum1[:, :].bitcast(I32))
                v.drain()
                ts(ang, turns, dcol[:, 0:1], None, ALU.mult)
                v.drain()
                for i, shift in ((0, 0.25), (1, 0.0)):
                    ts(turns, ang, 1.0 / (2 * np.pi), shift, ALU.mult, ALU.add)
                    v.drain()
                    ts(turns, turns, 12582912.0, None, ALU.add)
                    v.drain()
                    ts(turns, turns, 12582912.0, None, ALU.subtract)
                    v.drain()
                    o = dtab[:, i, :]
                    for part in TWO_PI:
                        stt(o, turns, -part, ang if part == TWO_PI[0] else o, ALU.mult, ALU.add)
                        v.drain()
                    if i == 0:
                        ts(o, o, float(np.pi / 2), None, ALU.add)
                        v.drain()
                    ts(o, o, PI_BELOW, -PI_BELOW, ALU.min, ALU.max).then_inc(tab_in, 1)

            def keys_input():
                for m in range(KD):
                    stt(y[:, m, :], x[:, m, :], ngain[:, GAIN["keys"], m:m + 1], ps[:, RB, :], ALU.mult, ALU.mult).then_inc(hk_ready, 1)
                for m in range(KD):
                    v.wait_ge(hk_hi_done, m + 1)
                    k = GK - KD + m
                    tt(by_class(hs_lo[:, k, :], True), by_class(y[:, m, :]), by_class(hs_hi[:, k, :], True).bitcast(F32),
                       ALU.subtract).then_inc(hk_split, 1)

            dense("ffn0")

            j, c = JS["pool"], AS["pool"]
            rms_fill("pool")
            V.memset(u0[:, 0:16], 0.0)
            V.memset(uw[:, 0, 0:16], 0.0)
            V.memset(uw[:, 1, 0:16], 0.0)
            v.wait_ge(late_landed, 32)
            for m in range(KD):
                g = m // 2
                split(j + 1 + m // 2, m % 2, W_FULL if m < 6 else 2 * P)
                v.wait_ge(acc_full, 2 * c + m + 1)
                v.drain()
                V.tensor_copy(u0[:, 16:16 + T], ps[:, m % 2, :]).then_inc(acc_free[m % 2], 1)
                if m >= 2:
                    v.wait_ge(k_hi_done, m - 1)
                src = u0
                for i in range(g + 1):
                    dst = uw[:, i % 2, :]
                    v.drain()
                    tt(dst[:, 16:16 + T], src[:, 16:16 + T], src[:, 16 - (1 << i):16 + T - (1 << i)], ALU.add)
                    src = dst
                v.drain()
                t = tmp[:, m % 2, :]
                stt(t, src[:, 16:16 + T], 1.0 / (2 << g), u0[:, 16:16 + T], ALU.mult, ALU.subtract)
                v.drain()
                tt(t[:, 0:16], src[:, 16:32], cnt[:, g, :], ALU.mult)
                v.drain()
                tt(t[:, 0:16], t[:, 0:16], u0[:, 16:32], ALU.subtract).then_inc(c_tile, 1)
                v.wait_ge(k_hi_done, m + 1)
                v.drain()
                tt(po_lo[:, m, :], t, po_hi[:, m, :].bitcast(F32), ALU.subtract).then_inc(k_ready, 1)
            for m in range(KD):
                split(j + 5 + m // 2, m % 2, 2 * P if m < 6 else W_FULL)
                v.wait_ge(acc_full, 2 * c + 8 + m + 1)
                v.drain()
                ts(tmp[:, m % 2, :], ps[:, m % 2, :], pgain[:, m:m + 1], None, ALU.mult).then_inc(tile_ready, 1)
                v.wait_ge(xs_hi_done, 8 * FILL["pool_out"] + m + 1)
                v.sem_inc(acc_free[m % 2], 1)
                tt(xs_lo[:, m, :], tmp[:, m % 2, :], xs_hi[:, m, :].bitcast(F32), ALU.subtract).then_inc(xs_ready, 1)
            out_tiles(j + 9, c + 8, W_FULL, True, y, False)
            residual("pool_out", y, False, lambda: split(j + 12, 1, W_FULL))
            dense("ffn1")
            dense("ffn2")

            j, c = JS["dilated"], AS["dilated"]
            v.drain().then_inc(place_free, 1)
            rms_fill("dilated", perm=True)
            cos, sin = dtab[:, 0:1, :], dtab[:, 1:2, :]
            v.wait_ge(mask_landed, 16)
            with v.Fori(0, 4) as p:
                jp, cp = j + p * 5, c + p * 5
                for i in range(6):
                    split(jp + 1 + i // 2, i % 2, W_FULL if i < 4 else KD * 96)
                    rope(2 * cp + i, L * N_ROPE + p * 6 + i, i % 2, dq[:, i:i + 1, :], cos, sin)
                for i in range(2):
                    split(jp + 4, i, KD * 96)
                for i in range(2):
                    split(jp + 5, i, W_FULL)
                attend(UD, L * UNITS + p * 8, 2, dprob, lambda un, n: ps[un["row"]:un["row"] + 64, n % 2, 0:P],
                       lambda un: dm_hi[un["row"]:un["row"] + 64, bass.ds(p, 1), un["at"]:un["at"] + P],
                       lambda un: dm_lo[un["row"]:un["row"] + 64, bass.ds(p, 1), un["at"]:un["at"] + P], 1)

            def back_in_order(ap, s, m, Y, add):
                v.wait_ge(acc_full, 2 * ap + s + 1)
                ts(Y[:, bass.ds(m, 1), :].rearrange("p a (i c) -> p a c i", c=4),
                   ps[:, s:s + 1, :].rearrange("p a (c i) -> p a c i", c=4), 1.0, None, ALU.mult).then_inc(acc_free[s], 1)

            out_tiles(j + 21, c + 20, 4 * P, True, yd, False, back_in_order)
            residual("dilated_out", yd, False, lambda: split(j + 24, 1, W_FULL))
            dense("ffn3", last=True)



def tiles(w):
    k = w.shape[0] // P
    return w.reshape(k, P, -1).transpose(1, 0, 2).reshape(P, -1)


def columns(w):
    return np.stack([tiles(w[:, i:i + P]) for i in range(0, w.shape[1], P)])


def rope_rows(rows, dim, positions):
    inv = (1.0 / (np.float32(10000.0) ** (np.arange(0, dim, 2, dtype=np.float32) / dim))).astype(np.float32)
    return positions.astype(np.float32)[None, :] * inv[rows][:, None]


def first_constants():
    pos = np.arange(T)
    row = np.arange(P)
    ang = rope_rows(row % 32, HD, pos)
    sign = np.where(row % 64 < 32, -1.0, 1.0).astype(np.float32)[:, None]
    tab = np.stack([np.cos(ang), np.sin(ang) * sign], axis=1)
    angc = rope_rows(row % 16, 32, pos)
    signc = np.where(row % 32 < 16, -1.0, 1.0).astype(np.float32)[:, None]
    tabc = np.where((row % 64 < 32)[:, None], np.cos(angc), np.sin(angc) * signc)
    q, k = np.arange(P)[:, None], np.arange(2 * P)[None, :]
    diff = q + P - k
    mask_a = np.where((diff >= 0) & (diff < P), 0.0, MASKED)
    mask_c = np.zeros((P, T))
    mask_c[:, 3 * P:] = np.where(np.arange(P)[None, :] <= q, 0.0, MASKED)
    j, i = np.arange(4)[:, None], np.arange(4)[None, :]
    tri = np.broadcast_to((i < j).reshape(1, 16), (P, 16))
    t_all = (4 * np.arange(P)[None, :] + np.arange(4)[:, None]).reshape(-1)
    mask_d = np.full((P, 4, T + 2 * P), MASKED)
    for c in range(4):
        d = (4 * np.arange(P) + c)[:, None] - t_all[None, :]
        mask_d[:, c, :T] = np.where((d >= 0) & (d <= P), 0.0, MASKED)
        d = np.arange(P)[:, None] - np.arange(P)[None, :]
        mask_d[:, c, T:T + P] = np.where(d >= 0, 0.0, MASKED)
        mask_d[:, c, T + P:] = np.where((d >= 0) & (d % 4 == 0), 0.0, MASKED)
    inv = (np.float32(10000.0) ** (-np.arange(0, HD, 2, dtype=np.float32) / HD)).astype(np.float32)
    dcol = np.stack([inv[row % 32], sign[:, 0]], axis=1)
    w = np.array([2, 4, 8, 16])[:, None]
    cnt = np.broadcast_to((1.0 / np.minimum(np.arange(16)[None, :] + 1, w)).reshape(1, 64), (P, 64))
    f = lambda v: np.ascontiguousarray(v, dtype=np.float32)
    return dict(tab=f(tab).reshape(P, -1), tabc=f(tabc), mask_a=f(mask_a), mask_c=f(mask_c), tri=f(tri),
                ident=np.eye(P, dtype=np.float32), mask_d=f(mask_d).reshape(P, -1), dcol=f(dcol), p_cnt=f(cnt))


def lay_out(i):
    cat = np.concatenate
    out = first_constants()
    out["xT"] = tiles(i["x"][0].T)
    w_in, w_kr, w_vb, w_up, w_out = [], [], [], [], []
    for l in range(L):
        o = np.cumsum([0, 512, 128, 128, 256, 64, 64, 256, 64, 4, 256, 128, 32])
        aq, ak, av, bq, bk, bv, iq, ik, iw, cq, ckv, ckr = (i["w_in"][l][:, o[n]:o[n + 1]] for n in range(12))
        pair = [aq[:, 64 * h:64 * h + 64] for t in range(4) for h in (t, 4 + t)]
        w_in.append(columns(cat([cq, ckv, av] + pair + [ak, bq, bk, bk, iq, ik, ik], axis=1)))
        w_kr.append(tiles(cat([ckr, ckr[:, 16:], ckr[:, :16]], axis=1)))
        w_vb.append(tiles(cat([bv, iw], axis=1)))
        uq, ukv = i["w_uq"][l], i["w_ukv"][l]
        q = [tiles(cat([uq[:, 96 * h:96 * h + 96], uq[:, 96 * h + 80:96 * h + 96], uq[:, 96 * h + 64:96 * h + 80]], axis=1))
             for h in range(4)]
        k = [ukv[:, P * h:P * h + 64] for h in range(4)]
        v = [ukv[:, P * h + 64:P * h + P] for h in range(4)]
        w_up.append(cat(q + k + v, axis=1))
        wo = i["w_out"][l]
        rows = [wo[64 * h:64 * h + 64] for t in range(4) for h in (t, 4 + t)]
        w_out.append(columns(cat(rows + [wo[512:]], axis=0)))
    stack = lambda v: np.ascontiguousarray(np.stack(v))
    out["w_in"], out["w_out"] = np.concatenate(w_in), np.concatenate(w_out)
    out["w_kr"], out["w_vb"], out["w_up"] = stack(w_kr), stack(w_vb), stack(w_up)
    out["w_router"] = tiles(i["w_router"])
    out["rbias"] = i["router_bias"].reshape(1, E)
    out["nsink"] = i["attn_sinks"]
    cols = lambda v: v.reshape(-1, P).T
    out["c_g"] = stack([cat([cols(i["c_q_norm_g"][l]), cols(i["c_kv_norm_g"][l])], axis=1) for l in range(L)])
    out["ln"] = stack([cat([cols(i[n][l]) for n in ("ln1_g", "ln1_b", "ln2_g", "ln2_b")], axis=1) for l in range(L)])
    gu = stack([i["w_gate"], i["w_up"]]).reshape(2, L, E, KD, P, 2, P)
    out["w_gu"] = gu.transpose(1, 2, 5, 0, 4, 3, 6).reshape(-1, P, D)
    dn = i["w_down"].reshape(L, 4, 8, P, KD, P)
    out["w_dn"] = dn.transpose(0, 1, 4, 3, 2, 5).reshape(-1, P, 8 * P)
    out["ngain"] = cat([cols(g) for g in i["norm_gain_2"].reshape(12, D)] + [cols(i["kv_norm_gain_2"])], axis=1)
    F = i["ffn_w_gate_2"].shape[-1]
    gu = stack([i["ffn_w_gate_2"], i["ffn_w_up_2"]]).reshape(2, 4, KD, P, F // P, P)
    out["f_gu"] = gu.transpose(1, 4, 0, 3, 2, 5).reshape(-1, P, D)
    dn = i["ffn_w_down_2"].reshape(4, 2, GK, P, KD, P)
    out["f_dn"] = dn.transpose(0, 1, 4, 3, 2, 5).reshape(-1, P, GK * P)
    out["next_in"] = cat([out["w_in"][15:17], out["f_gu"][0:2]])
    out["p_in"], out["p_out"] = columns(i["pool_w_in_2"][0]), columns(i["pool_w_out_2"][0])
    out["p_grp"] = np.concatenate([columns(g) for g in i["pool_w_group_2"][0]])
    out["p_scale"] = cols(i["pool_scale_2"][0])
    pairs = lambda w: [w[:, 512 * g + P * p:512 * g + P * p + P] for p in range(4) for g in range(3)]
    q, k, v = pairs(i["attn_w_q_2"][0]), pairs(i["w_k_2"]), pairs(i["w_v_2"])
    out["d_qk"] = stack([tiles(w) for p in range(4) for w in q[3 * p:3 * p + 3] + k[3 * p:3 * p + 3]])
    out["d_v"] = stack([tiles(cat(v[3 * p:3 * p + 3], axis=1)[:, 96 * n:96 * n + 96]) for p in range(4) for n in range(4)])
    out["d_out"] = columns(i["attn_w_o_2"][0])
    out["pos"] = i["positions_2"].reshape(P, 4).T.reshape(1, T).astype(np.int32)
    return {n: np.ascontiguousarray(v) for n, v in out.items()}


def kernel(**inputs):
    import concourse.bacc as bacc
    from concourse.bass_utils import run_bass_kernel_spmd

    nc = bacc.Bacc("TRN2", target_bir_lowering=False, num_devices=1)
    arrays = lay_out({n: np.asarray(v) for n, v in inputs.items()})
    args = {n: nc.dram_tensor(f"in_{n}", v.shape, mybir.dt.from_np(v.dtype), kind="ExternalInput").ap()
            for n, v in arrays.items()}
    out = nc.dram_tensor("out_hT", (P, KD * T), F32, kind="ExternalOutput").ap()
    build_program(nc, args, out)
    r = run_bass_kernel_spmd(nc, [{f"in_{n}": v for n, v in arrays.items()}], core_ids=[0])
    got = np.asarray(r.results[0]["out_hT"])
    return got.reshape(P, KD, T).transpose(2, 1, 0).reshape(1, T, D)
```

```python
from contextlib import ExitStack

import numpy as np

import concourse.bass as bass
from concourse import mybir

F32, F32R, I32 = mybir.dt.float32, mybir.dt.float32r, mybir.dt.int32
ALU = mybir.AluOpType
ACT = mybir.ActivationFunctionType
AX = mybir.AxisListType

P, T, D, L = 128, 512, 1024, 2
KD = D // P
NT = T // P
HD = 64
ALPHA = float((2 * L) ** 0.25)
LN_EPS, RMS_EPS = 1e-5, 1e-6
TOPK = 128
E, TOKG = 16, 4
RING = 2
SLOT = 12 * P + 32
GK = 11
MASKED = -1.0e30
CAUSAL = -1.0e38
TAKEN = -3.0e38

J_ROPE, N_ROPE, J_UP, J_OUT, N_JOBS = 6, 11, 17, 18, 18 + 8 + 96
A_ROPE, A_UP, A_OUT, A_ROUTER, A_MOE, N_ACC = 6, 17, 25, 33, 34, 130
J_MOE = J_OUT + 8
UNITS = 64
UNITS_D = 64 * 1

W_FULL, W_KR, W_VA, W_VB, W_UP, W_DOWN = KD * P, KD * 64, KD * P, KD * 68, 12 * P, GK * P


TWO_PI = (6.28125, 0.0019350051879882812, 3.019916050561733e-07)
PI_BELOW = 3.1415925


def build_program(nc, a, out):
    gates_dram = nc.dram_tensor("gates_scratch", (E, T), F32, kind="Internal").ap()
    keys_dram = [nc.dram_tensor(f"keys_scratch_{n}", (P, KD * T), F32R, kind="Internal").ap() for n in ("hi", "lo")]

    with ExitStack() as ctx:
        cursor = [(nc.sbuf_base + 63) // 64 * 64]

        def sb(name, shape, dt=F32):
            size = int(np.prod(shape[1:])) * 4
            t = nc.alloc_sbuf_tensor_at(name, shape, dt, offset=cursor[0])
            cursor[0] += (size + 31) // 32 * 32
            assert cursor[0] <= nc.sbuf_usable_end, name
            return t

        def flat(t):
            return t[:, :, :].rearrange("p k t -> p (k t)")

        def one(ap, i):
            return ap[bass.ds(i, 1)].rearrange("a p n -> (a p) n")

        x = sb("x", [P, KD, T])
        xs_hi, xs_lo = sb("xs_hi", [P, KD, T], F32R), sb("xs_lo", [P, KD, T], F32R)
        stage = sb("w_stage", [P, RING, SLOT])
        w_hi, w_lo = sb("w_hi", [P, RING, SLOT], F32R), sb("w_lo", [P, RING, SLOT], F32R)
        sum1, sum2, sq = sb("sum1", [P, T]), sb("sum2", [P, T]), sb("squares", [P, 2, T])
        rstd = sb("rstd", [P, T])
        tmp, rot = sb("tmp", [P, 2, T]), sb("rotated", [P, 2, T])
        ident, ones = sb("ident", [P, P]), sb("ones", [P, 1])
        pick = sb("pick", [P, 64])
        small = sb("small", [P, 64])
        ngain = sb("ngain", [P, 13, KD])
        col = sb("attn_cols", [P, 4, 8])
        region0 = cursor[0]
        tabs, tabc = sb("rope_tab", [P, 2, T]), sb("rope_tab_c", [P, T])
        mask_a, mask_c = sb("mask_a", [P, 2 * P]), sb("mask_c", [P, T])
        tri = sb("ties", [P, 16])
        wr = sb("w_router", [P, KD * E])
        wr_hi, wr_lo = sb("w_router_hi", [P, KD * E], F32R), sb("w_router_lo", [P, KD * E], F32R)
        rbias = sb("router_bias", [P, E])
        nsink, cg, lng = sb("neg_sinks", [P, 8]), sb("c_gain", [P, 3]), sb("ln_gain", [P, 4, KD])
        region1 = cursor[0]
        heads = sb("heads", [P, N_ROPE, T])
        cfeat = sb("c_feat", [P, 3, T])
        cs_hi, cs_lo = sb("c_hi", [P, 3, T], F32R), sb("c_lo", [P, 3, T], F32R)
        qc, kc, krope = sb("q_c", [P, 4, T]), sb("k_c", [P, 4, T]), sb("k_rope", [P, T])
        va, vb, vc = sb("v_a", [P, NT, P]), sb("v_b", [P, NT, 68]), sb("v_c", [P, NT, 256])
        maskb = sb("mask_b", [P, NT, T])
        rl = sb("index_relu", [P, 2, T])
        prob, probt = sb("prob", [P, 4, T]), sb("prob_t", [P, 2, T])
        max8 = sb("max8", [P, 8])
        cursor[0] = region1
        y = sb("y", [P, KD, T])
        gb, sg, hh = sb("gate_bcast", [P, T]), sb("silu", [P, T]), sb("hidden", [P, T])
        gates_t = sb("gates_t", [E, T])
        rt, pairs = sb("router_work", [P, 8, 64]), sb("router_pairs", [P, 2, 256])
        region2 = cursor[0]
        hs_hi, hs_lo = sb("h_hi", [P, GK, T], F32R), sb("h_lo", [P, GK, T], F32R)
        cursor[0] = region2
        u0, uw = sb("pool_u", [P, 16 + T]), sb("pool_sum", [P, 2, 16 + T])
        cnt, pgain = sb("pool_count", [P, 4, 16]), sb("pool_gain", [P, KD])
        po_hi, po_lo = sb("pooled_hi", [P, KD, T], F32R), sb("pooled_lo", [P, KD, T], F32R)
        cursor[0] = region0
        dtab = sb("d_tab", [P, 2, T])
        dcol = sb("d_cols", [P, 2])
        dq, dv = sb("d_heads", [P, 6, T]), sb("d_v", [P, NT, 768])
        mask_d = sb("mask_d", [P, NT, T + 2 * P])
        dprob, dprobt = sb("d_prob", [P, 3, 768]), sb("d_prob_t", [P, 768])
        dm_hi, dm_lo = sb("d_mix_hi", [P, 4, T], F32R), sb("d_mix_lo", [P, 4, T], F32R)
        region3 = cursor[0]
        ks_hi, ks_lo = sb("k_in_hi", [P, KD, T], F32R), sb("k_in_lo", [P, KD, T], F32R)
        cursor[0] = region3
        yd = sb("y_dilated", [P, KD, T])

        ps = ctx.enter_context(nc.psum_tensor("ps", [P, 8, T], F32))
        STAT, RB, MB = 2, 3, 4

        sem = lambda name: ctx.enter_context(nc.semaphore(name))
        const_landed, layer_landed, late_landed = sem("const_landed"), sem("layer_landed"), sem("late_landed")
        mask_landed = sem("mask_landed")
        w_landed = [sem(f"w_landed{s}") for s in range(RING)]
        w_hi_done = sem("w_hi_done")
        w_split = sem("w_split")
        acc_full = sem("acc_full")
        acc_free = [sem(f"acc_free{b}") for b in range(RING)]
        consts_made = sem("consts_made")
        tile_ready, xs_hi_done, xs_ready = sem("tile_ready"), sem("xs_hi_done"), sem("xs_ready")
        sq_ready, sq_used = sem("squares_ready"), sem("squares_used")
        x_new, x_landed = sem("x_new"), [sem(f"x_landed{s}") for s in range(2)]
        stat_in, stat_full, rstd_ready, rb_full = sem("stat_in"), sem("stat_full"), sem("rstd_ready"), sem("rb_full")
        rot_ready = sem("rot_ready")
        act_copied, heads_ready, qc_ready = sem("act_copied"), sem("heads_ready"), sem("qc_ready")
        kr_ready, kr_copied = sem("kr_ready"), sem("kr_copied")
        c_tile, c_hi_done, c_ready = sem("c_tile"), sem("c_hi_done"), sem("c_ready")
        v_evacuated, v_turned = sem("v_evacuated"), sem("v_turned")
        logits_copied, logits_full = sem("logits_copied"), sem("logits_full")
        ix_full, ix_relu, ix_used = sem("ix_full"), sem("ix_relu"), sem("ix_used")
        s_full, masked, p_exp, p_norm = sem("s_full"), sem("masked"), sem("p_exp"), sem("p_norm")
        pt_full, pt_copied = sem("pt_full"), sem("pt_copied")
        o_full, o_hi_done, o_split = sem("o_full"), sem("o_hi_done"), sem("o_split")
        h_ready, c_copied, wr_hi_done = sem("h_ready"), sem("c_copied"), sem("w_router_hi")
        wr_ready, r_tanh, gates_ready = sem("w_router_ready"), sem("router_tanh"), sem("gates_ready")
        gt_full, gt_copied, gates_stored = sem("gates_t_full"), sem("gates_t_copied"), sem("gates_stored")
        gb_landed, gb_used = sem("gate_landed"), sem("gate_used")
        gate_scaled = sem("gate_scaled")
        sg_ready, sg_used = sem("silu_ready"), sem("silu_used")
        place_free = sem("place_free")
        hk_ready, hk_hi_done, hk_split = sem("hk_ready"), sem("hk_hi_done"), sem("hk_split")
        hk_stored, hk_landed, pos_landed = [sem(f"hk_stored{i}") for i in range(3)], sem("hk_landed"), sem("pos_landed")
        k_hi_done, k_ready = sem("k_hi_done"), sem("k_ready")
        tab_in, tab_done = sem("tab_in"), sem("tab_done")
        y_final, out_stored = sem("y_final"), sem("out_stored")

        JL, AL = N_JOBS // 2, N_ACC // 2
        SECOND = ["ffn0", "pool", "ffn1", "ffn2", "dilated", "ffn3"]
        PAIRS = {"f": 30, "p": 12, "d": 22}
        JS = {n: L * JL + sum(PAIRS[m[0]] for m in SECOND[:i]) for i, n in enumerate(SECOND)}
        AS = {n: L * AL + JS[n] - L * JL for n in SECOND}
        FILL = {"ffn0": 5, "pool": 6, "pool_out": 7, "ffn1": 8, "ffn2": 9, "dilated": 10, "ffn3": 11}
        NORM = {n: 6 + i for i, n in enumerate(
            ["ffn0", "ffn0_out", "pool", "pool_out", "ffn1", "ffn1_out", "ffn2", "ffn2_out",
             "dilated", "dilated_out", "ffn3", "ffn3_out"])}
        SQ = {n: 8 * (i - 6) + 32 for n, i in NORM.items()}
        X_NEW = {"ffn0": None, "pool": 0, "ffn1": 8, "ffn2": 16, "dilated": 24, "ffn3": 32}
        GAIN = {"ffn0": 0, "ffn0_out": 1, "pool": 2, "pool_out": 3, "ffn1": 4, "ffn1_out": 5, "ffn2": 6,
                "ffn2_out": 7, "dilated": 8, "dilated_out": 9, "ffn3": 10, "ffn3_out": 11, "keys": 12}
        COPIES = 12

        def units():
            for t in range(4):
                for h in range(2):
                    for qt in range(NT):
                        r, k0 = slice(64 * h, 64 * h + 64), max(qt - 1, 0)
                        yield dict(q=heads[r, t, qt * P:qt * P + P], keys=[(heads[r, 4, k0 * P:qt * P + P], 0)],
                                   W=(qt - k0 + 1) * P, mask=mask_a[:, (0 if qt else P):2 * P], scale=0.125,
                                   sink=4 * h + t, v=[va[:, b, 64 * h:64 * h + 64] for b in range(k0, qt + 1)],
                                   row=64 * h, tile=t, at=qt * P)
            for h in range(4):
                for qt in range(NT):
                    yield dict(q=qc[0:96, h, qt * P:qt * P + P], keys=[(kc[0:96, h, 0:qt * P + P], 0)],
                               W=(qt + 1) * P, mask=mask_c[:, (3 - qt) * P:T], scale=96 ** -0.5, sink=None,
                               v=[vc[:, b, 64 * h:64 * h + 64] for b in range(qt + 1)],
                               row=64 * (h % 2), tile=6 + h // 2, at=qt * P)
            for h in range(4):
                for qt in range(NT):
                    r = slice(64 * (h % 2), 64 * (h % 2) + 64)
                    yield dict(q=heads[r, 5 + h // 2, qt * P:qt * P + P], keys=[(heads[r, 7, 0:qt * P + P], 0)],
                               W=(qt + 1) * P, mask=maskb[:, qt, 0:(qt + 1) * P], scale=0.125, sink=None,
                               v=[vb[:, b, 0:64] for b in range(qt + 1)],
                               row=64 * (h % 2), tile=4 + h // 2, at=qt * P)

        def units_d(e):
            for h in range(2):
                r = slice(64 * h, 64 * h + 64)
                for c in range(4):
                    cols = slice(c * P, c * P + P)
                    yield dict(q=[dq[r, g, cols] for g in range(3)],
                               keys=[(dq[r, 3, :], 0), (dq[r, 4, cols], T), (dq[r, 5, cols], T + P)],
                               W=T + 2 * P, mask=c, scale=0.125, sink=None,
                               v=[dv[:, b, 3 * P * e + g * P + 64 * h:3 * P * e + g * P + 64 * h + 64]
                                  for b, g in ((0, 0), (1, 0), (2, 0), (3, 0), (c, 1), (c, 2))],
                               row=64 * h, at=c * P)

        def by_class(t, ordered=False):
            return t.rearrange("p (c i) -> p c i", c=4) if ordered else t.rearrange("p (i c) -> p c i", c=4)

        def norm_tile(m):
            return (tmp, rot)[m // 2 % 2][:, m % 2, :]

        UN, UD = list(units()), [list(units_d(e)) for e in range(2)]
        IX = [(qt, h) for qt in range(1, NT) for h in range(4)]

        DEEP = dict(ring=4, scores=3, exps=2, mix=1, o_hi=2, o_lo=3, banks=(2, 3, 0, 1))
        WIDE = dict(ring=3, scores=2, exps=1, mix=0, o_hi=1, o_lo=1, banks=(2, 4))

        KEY_TILES = [(0, 1, 2), (3, 4, 5), (6, 7)]

        waited = sem("waited")

        def hold(eng, sem_, value):
            eng.wait_ge(sem_, value)
            eng.sem_inc(waited, 1)

        block = ctx.enter_context(nc.Block())

        @block.sync
        def _(sp):
            def load(jp, s, n, src):
                sp.wait_ge(w_split, 2 * jp + s + 1)
                sp.dma_start(stage[:, s, 0:n], src).then_inc(w_landed[s], 16)

            for s in range(2):
                half = slice(s * KD // 2, (s + 1) * KD // 2)
                sp.dma_start(x[:, half, :].rearrange("p k t -> p (k t)"),
                             a["xT"][:, half.start * T:half.stop * T]).then_inc(x_landed[s], 16)
                load(0, s, W_FULL, a["w_in"][s])
            for dst, src in ((flat(tabs), a["tab"]), (tabc[:, :], a["tabc"]),
                             (mask_a[:, :], a["mask_a"]), (mask_c[:, :], a["mask_c"]), (tri[:, :], a["tri"]),
                             (ident[:, :], a["ident"]), (wr[:, :], a["w_router"]),
                             (rbias[:, :].rearrange("p (a n) -> p a n", a=1), a["rbias"].partition_broadcast(P)), (flat(ngain), a["ngain"])):
                sp.dma_start(dst, src).then_inc(const_landed, 16)
            with sp.Fori(0, L) as l:
                j = l * JL
                sp.wait_ge(place_free, l + 1)
                sp.dma_start(nsink[:, :].rearrange("p (a n) -> p a n", a=1), a["nsink"][bass.ds(l, 1), :].partition_broadcast(P)).then_inc(layer_landed, 16)
                sp.dma_start(cg[:, :], one(a["c_g"], l)).then_inc(layer_landed, 16)
                sp.dma_start(flat(lng), one(a["ln"], l)).then_inc(layer_landed, 16)
                load(j + 1, 0, W_FULL, one(a["w_in"], l * 15 + 2))
                load(j + 1, 1, W_KR, one(a["w_kr"], l))
                load(j + 2, 0, W_VA, one(a["w_in"], l * 15 + 3))
                load(j + 2, 1, W_VB, one(a["w_vb"], l))
                with sp.Fori(0, 5) as i:
                    for s in range(2):
                        load(j + 3 + i, s, W_FULL, one(a["w_in"], l * 15 + 4 + s + 2 * i))
                load(j + 8, 0, W_FULL, one(a["w_in"], l * 15 + 14))
                load(j + 8, 1, W_UP, one(a["w_up"], l))
                with sp.Fori(0, 4) as i:
                    for s in range(2):
                        load(j + 9 + i, s, W_FULL, one(a["w_out"], l * 8 + 2 * i + s))
                with sp.Fori(0, 4) as q:
                    with sp.Fori(0, 8) as i:
                        for s in range(2):
                            load(j + J_MOE // 2 + q * 12 + i, s, W_FULL, one(a["w_gu"], l * 64 + q * 16 + 2 * i + s))
                    with sp.Fori(0, 4) as i:
                        for s in range(2):
                            load(j + J_MOE // 2 + 8 + q * 12 + i, s, W_FULL, one(a["w_dn"], l * 32 + q * 8 + 2 * i + s))
                for s in range(2):
                    load(j + JL, s, W_FULL, one(a["next_in"], 2 * l + s))
            for name in SECOND:
                j = JS[name]
                if name[0] == "f":
                    n = int(name[3])
                    for g in range(2):
                        first = 1 if n + g == 0 else 0
                        with sp.Fori(first, GK) as i:
                            for s in range(2):
                                load(j + 15 * g + i, s, W_FULL, one(a["f_gu"], n * 44 + g * 22 + s + 2 * i))
                        with sp.Fori(0, 4) as i:
                            for s in range(2):
                                load(j + 15 * g + 11 + i, s, W_DOWN, one(a["f_dn"], n * 16 + g * 8 + s + 2 * i))
                elif name == "pool":
                    for s in range(2):
                        load(j, s, W_FULL, a["p_in"][s])
                    sp.wait_ge(place_free, L + 2)
                    sp.dma_start(flat(cnt), a["p_cnt"]).then_inc(late_landed, 16)
                    sp.dma_start(pgain[:, :], a["p_scale"]).then_inc(late_landed, 16)
                    for w, n, o, i0 in (("p_in", W_FULL, 0, 1), ("p_grp", 2 * P, 4, 0), ("p_out", W_FULL, 8, 0)):
                        with sp.Fori(i0, 4) as i:
                            for s in range(2):
                                load(j + o + i, s, n, one(a[w], 2 * i + s))
                else:
                    def qk(p2, e):
                        with sp.Fori(0, 3) as i:
                            for s in range(2):
                                load(j + p2 * 9 + 6 * e + i, s, W_FULL, one(a["d_qk"], p2 * 12 + 6 * e + 2 * i + s))

                    with sp.Fori(0, 2) as p2:
                        qk(p2, 0)
                        with sp.Fori(0, 3) as i:
                            for s in range(2):
                                load(j + p2 * 9 + 3 + i, s, W_FULL, one(a["d_v"], p2 * 6 + 2 * i + s))
                        qk(p2, 1)
                    with sp.Fori(0, 4) as i:
                        for s in range(2):
                            load(j + 18 + i, s, 4 * P, one(a["d_out"], 2 * i + s))
            for m in range(0, KD, 2):
                sp.wait_ge(y_final, m + 2)
                sp.dma_start(out[:, m * T:(m + 2) * T], x[:, m:m + 2, :].rearrange("p k t -> p (k t)")).then_inc(out_stored, 16)
            sp.wait_ge(out_stored, 64)

        @block.gpsimd
        def _(pool):
            nc.gpsimd.memset(ones[:, :], 1.0).then_inc(consts_made, 1)
            nc.gpsimd.memset(pick[:, :], 0.0)
            pool.drain()
            for i in range(8):
                nc.gpsimd.memset(pick[:, 9 * i:9 * i + 1], 1.0).then_inc(consts_made, 1)
            def add_up(n0, values=None):
                for m in range(1, KD - 2):
                    hold(pool, sq_ready, n0 + m + 1)
                    if values is not None:
                        nc.gpsimd.tensor_tensor(sum1[:, :], values[:, 0, :] if m == 1 else sum1[:, :], values[:, m, :], ALU.add)
                    nc.gpsimd.tensor_tensor(sum2[:, :], sq[:, 0, :] if m == 1 else sum2[:, :], sq[:, m % 2, :], ALU.add)
                    pool.drain().then_inc(sq_used, 2 if m == 1 else 1)

            with pool.Fori(0, L) as l:
                hold(pool, kr_ready, l + 1)
                for h in range(4):
                    nc.gpsimd.tensor_copy(kc[64:96, h, :], krope[64:96, :]).then_inc(kr_copied, 1)
                add_up(l * 16, x)
                hold(pool, gt_copied, l + 1)
                pool.dma_start(gates_dram, gates_t[:, :]).then_inc(gates_stored, 16)
                hold(pool, gates_stored, l * 16 + 16)
                with pool.Fori(0, E) as e:
                    hold(pool, gb_used, l * E + e + 1)
                    pool.dma_start(gb[:, :].rearrange("p (a t) -> p a t", a=1), gates_dram[bass.ds(e, 1), :].partition_broadcast(P)).then_inc(gb_landed, 16)
                add_up(l * 16 + 8, y)
            add_up(SQ["ffn0"])
            hold(pool, place_free, L + 1)
            pool.dma_start(dcol[:, :], a["dcol"]).then_inc(pos_landed, 16)
            pool.dma_start(sum1[:, :].bitcast(I32).rearrange("p (a t) -> p a t", a=1), a["pos"].partition_broadcast(P)).then_inc(pos_landed, 16)
            for name in ("ffn0_out", "pool", "pool_out", "ffn1", "ffn1_out", "ffn2"):
                add_up(SQ[name])
            for i, ms in enumerate(KEY_TILES):
                hold(pool, hk_split, ms[-1] + 1)
                for t, d in ((hs_hi, keys_dram[0]), (hs_lo, keys_dram[1])):
                    pool.dma_start(d[:, ms[0] * T:(ms[-1] + 1) * T], t[:, GK - KD + ms[0]:GK - KD + ms[-1] + 1, :]
                                   .rearrange("p k t -> p (k t)")).then_inc(hk_stored[i], 16)
            for i in range(len(KEY_TILES)):
                hold(pool, hk_stored[i], 32)
            add_up(SQ["ffn2_out"])
            hold(pool, acc_full, 2 * (AS["ffn2"] + 30))
            for t, d in ((ks_hi, keys_dram[0]), (ks_lo, keys_dram[1])):
                pool.dma_start(flat(t), d).then_inc(hk_landed, 16)
            add_up(SQ["dilated"])
            hold(pool, place_free, L + 3)
            pool.dma_start(flat(mask_d), a["mask_d"]).then_inc(mask_landed, 16)
            for name in ("dilated_out", "ffn3", "ffn3_out"):
                add_up(SQ[name])

        @block.tensor
        def _(pe):
            def three(o, lh, ll, rh, rl_, start, stop):
                pe.matmul(o, lh, rh, start=start, stop=False)
                pe.matmul(o, lh, rl_, start=False, stop=False)
                return pe.matmul(o, ll, rh, start=False, stop=stop)

            def begin(jp, s, ap, b):
                pe.wait_ge(w_split, 2 * jp + s + 1 + RING)
                pe.wait_ge(acc_free[b], ap + 1)

            def job(jp, s, ap, b, hi, lo, K=KD, M=P, waits=None, before=None):
                begin(jp, s, ap, b)
                for k in range(K):
                    if before is not None:
                        before(k)
                    if waits is not None:
                        pe.wait_ge(waits[0], waits[1] + k + 1)
                    last = three(ps[0:M, b, :], w_hi[:, s, k * M:k * M + M], w_lo[:, s, k * M:k * M + M],
                                 hi[:, k, :], lo[:, k, :], k == 0, k == K - 1)
                last.then_inc(acc_full, 1)

            def turn(n, b, N, bank):
                pe.wait_ge(v_evacuated, n + 1)
                for t in range(NT):
                    last = pe.transpose(ps[:, bank, t * N:t * N + N], rot[0:N, b, t * P:t * P + P], ident[0:N, 0:N])
                last.then_inc(v_turned, 1)

            def stats(n, tables):
                pe.wait_ge(stat_in, n + 1)
                for i, t in enumerate(tables):
                    for q in range(NT):
                        last = pe.matmul(ps[:, STAT, 4 * i + q:4 * i + q + 1], t[:, q * P:q * P + P], ones[:, 0:1],
                                         start=True, stop=True)
                last.then_inc(stat_full, 1)

            def norm_sums(n0, values=None):
                for m in (None, KD - 2, KD - 1):
                    if m is None:
                        pe.wait_ge(sq_used, n0 + KD)
                    else:
                        pe.wait_ge(sq_ready, n0 + m + 1)
                    for q in range(NT):
                        at = slice(q * P, q * P + P)
                        if values is not None:
                            pe.matmul(ps[:, STAT, 0:8], sum1[:, at] if m is None else values[:, m, at],
                                      pick[:, 8 * q + 32:8 * q + 40], start=m is None and q == 0, stop=False)
                        last = pe.matmul(ps[:, STAT, 0:8], sum2[:, at] if m is None else sq[:, m % 2, at],
                                         pick[:, 8 * q:8 * q + 8], start=m is None and q == 0 and values is None,
                                         stop=m == KD - 1 and q == NT - 1)
                    if m is not None:
                        last.then_inc(sq_used, 1)

            def with_stats(n0, tile_job, values=None):
                for m in range(KD):
                    tile_job(m)
                norm_sums(n0, values)

            def spread(n, banks):
                pe.wait_ge(rstd_ready, n + 1)
                for i, b in enumerate(banks):
                    for q in range(NT):
                        last = pe.matmul(ps[:, b, q * P:q * P + P],
                                         small[:, 4 * i + q:4 * i + q + 1].to_broadcast([P, P]), ident[:, :],
                                         start=True, stop=True)
                last.then_inc(rb_full, 1)

            def scores(un, n, F):
                b = F["banks"][n % len(F["banks"])]
                q = un["q"] if isinstance(un["q"], list) else [un["q"]]
                for i, (k, at) in enumerate(un["keys"]):
                    w = k.shape[-1]
                    last = pe.matmul(ps[:, b + at // T, at % T:at % T + w], q[i], k, start=True, stop=True)
                last.then_inc(s_full, 1)

            def transposes(un, n, c0, probs, bank, ring):
                pe.wait_ge(p_norm, c0 + n + 1)
                for i in range(un["W"] // P):
                    last = pe.transpose(ps[:, bank + i // 4, (i % 4) * P:(i % 4) * P + P], probs[:, n % ring, i * P:i * P + P],
                                        ident[:, :])
                last.then_inc(pt_full, 1)

            def mix(un, n, c0, probs_t, o):
                pe.wait_ge(pt_copied, c0 + n + 1)
                if n >= 2:
                    pe.wait_ge(o_split, c0 + n - 1)
                nb = un["W"] // P
                for i in range(nb):
                    last = pe.matmul(o, un["v"][i], probs_t[:, i * P:i * P + P], start=(i == 0), stop=(i == nb - 1))
                last.then_inc(o_full, 1)

            def attend(U, c0, F, probs, t_bank, probs_t, o_of):
                N = len(U)
                for n in range(F["scores"]):
                    scores(U[n], n, F)
                for n in range(N + F["mix"]):
                    ahead = n + F["scores"]
                    if n < N and F is WIDE:
                        transposes(U[n], n, c0, probs, t_bank(n), F["ring"])
                    if ahead < N:
                        if ahead >= len(F["banks"]):
                            pe.wait_ge(masked, c0 + ahead - len(F["banks"]) + 1)
                        scores(U[ahead], ahead, F)
                    if n < N and F is DEEP:
                        transposes(U[n], n, c0, probs, t_bank(n), F["ring"])
                    m = n - F["mix"]
                    if m >= 0:
                        mix(U[m], m, c0, probs_t(m), o_of(U[m], m))

            pe.wait_ge(consts_made, 9)
            with pe.Fori(0, L) as l:
                j, c = l * JL, l * AL
                for i in range(4):
                    job(j + i // 2, i % 2, c + i // 2, i % 2, xs_hi, xs_lo, M=64 if i == 3 else P,
                        waits=(xs_ready, l * 16) if i == 0 else None)
                job(j + 2, 0, c + 2, 0, xs_hi, xs_lo)
                job(j + 2, 1, c + 2, 1, xs_hi, xs_lo, M=68)
                pe.wait_ge(const_landed, 144)
                turn(2 * l, 0, P, 5)
                turn(2 * l + 1, 1, 68, 6)
                stats(l, [sum2, sum1])
                with pe.Fori(0, 5) as i:
                    for s in range(2):
                        job(j + 3 + i, s, c + 3 + i, s, xs_hi, xs_lo)
                spread(3 * l, [RB, MB])
                job(j + 8, 0, c + 8, 0, xs_hi, xs_lo)
                pe.wait_ge(w_split, 2 * (j + 8) + 2 + RING)
                for i in range(4):
                    pe.wait_ge(acc_free[(i + 1) % 2], c + 8 + (i + 1) // 2 + 1)
                    for k in range(2):
                        if i == 0:
                            pe.wait_ge(c_ready, l * 3 + k + 1)
                        m = i * 2 * P + k * P
                        last = three(ps[:, (i + 1) % 2, :], w_hi[:, 1, m:m + P], w_lo[:, 1, m:m + P],
                                     cs_hi[:, k, :], cs_lo[:, k, :], k == 0, k == 1)
                    last.then_inc(acc_full, 1)
                pe.wait_ge(c_ready, l * 3 + 3)
                for i in range(2):
                    pe.wait_ge(acc_free[(i + 1) % 2], c + 10 + (i + 1) // 2 + 1)
                    m = 8 * P + i * P
                    three(ps[:, (i + 1) % 2, :], w_hi[:, 1, m:m + P], w_lo[:, 1, m:m + P],
                          cs_hi[:, 2, :], cs_lo[:, 2, :], True, True).then_inc(acc_full, 1)
                for i in range(2):
                    pe.wait_ge(acc_free[(i + 1) % 2], c + 11 + (i + 1) // 2 + 1)
                    for t in (2 * i, 2 * i + 1):
                        last = three(ps[:, (i + 1) % 2, 256 * (t % 2):256 * (t % 2) + 256],
                                     cs_hi[:, 2, t * P:t * P + P], cs_lo[:, 2, t * P:t * P + P],
                                     w_hi[:, 1, 10 * P:12 * P], w_lo[:, 1, 10 * P:12 * P], True, True)
                    last.then_inc(acc_full, 1)
                pe.wait_ge(heads_ready, l * N_ROPE + N_ROPE)
                for n, (qt, h) in enumerate(IX):
                    if n >= 2:
                        pe.wait_ge(ix_relu, l * len(IX) + n - 1)
                    r = slice(64 * (h % 2), 64 * (h % 2) + 64)
                    pe.matmul(ps[:, 2 + n % 2, 0:(qt + 1) * P], heads[r, 8 + h // 2, qt * P:qt * P + P],
                              heads[r, 10, 0:(qt + 1) * P], start=True, stop=True).then_inc(ix_full, 1)
                pe.wait_ge(ix_relu, l * len(IX) + len(IX))
                pe.wait_ge(act_copied, l * COPIES + COPIES)
                pe.wait_ge(qc_ready, l * 4 + 4)
                pe.wait_ge(kr_copied, l * 4 + 4)
                u0_ = l * UNITS
                attend(UN, u0_, DEEP, prob, lambda n: 4 + n % 2, lambda n: probt[:, n % 2, :],
                       lambda un, n: ps[un["row"]:un["row"] + 64, 6 + n % 2, 0:P])
                hold(pe, o_split, u0_ + UNITS)
                with_stats(l * 16, lambda m: job(j + 9 + m // 2, m % 2, c + 12 + (m + 1) // 2, 1 - m % 2, xs_hi, xs_lo), x)
                spread(3 * l + 1, [RB, MB])
                pe.wait_ge(wr_ready, 1)
                pe.wait_ge(acc_free[1], c + 17)
                for k in range(KD):
                    pe.wait_ge(xs_ready, l * 16 + 8 + k + 1)
                    last = three(ps[0:E, 1, :], wr_hi[:, k * E:k * E + E], wr_lo[:, k * E:k * E + E],
                                 xs_hi[:, k, :], xs_lo[:, k, :], k == 0, k == KD - 1)
                last.then_inc(acc_full, 1)
                hold(pe, logits_copied, l + 1)
                for t in range(NT):
                    last = pe.transpose(ps[:, STAT, t * E:t * E + E], gates_t[:, t * P:t * P + P], ident[0:E, 0:E])
                last.then_inc(logits_full, 1)
                jm, cm = j + J_MOE // 2, c + A_MOE // 2

                def gate_up(q, i):
                    for s in range(2):
                        job(jm + q * 12 + i, s, cm + q * 12 + i, s, xs_hi, xs_lo)

                gate_up(0, 0)
                pe.wait_ge(gates_ready, l + 1)
                for t in range(NT):
                    last = pe.transpose(ps[0:E, STAT, t * P:t * P + P], rt[:, 0, t * E:t * E + E], ident[:, :])
                last.then_inc(gt_full, 1)
                with pe.Fori(0, 3) as q:
                    with pe.Fori(1, 8) as i:
                        gate_up(q, i)
                    with pe.Fori(0, 4) as i:
                        for s in range(2):
                            job(jm + q * 12 + 8 + i, s, cm + q * 12 + 8 + i, s, hs_hi, hs_lo,
                                waits=(h_ready, l * 32 + q * 8) if s == 0 else None)
                    gate_up(q + 1, 0)
                with pe.Fori(1, 8) as i:
                    gate_up(3, i)
                with_stats(l * 16 + 8, lambda m: job(jm + 44 + m // 2, m % 2, cm + 44 + m // 2, m % 2, hs_hi, hs_lo,
                                                     waits=(h_ready, l * 32 + 24) if m == 0 else None), y)
                spread(3 * l + 2, [RB, MB])

            def first_jobs(name, j, c):
                job(j, 0, c, 0, xs_hi, xs_lo, waits=(xs_ready, FILL[name] * 8), before=lambda k: norm_sums(SQ[name]) if k == KD - 1 else None)
                job(j, 1, c, 1, xs_hi, xs_lo, before=lambda k: spread(NORM[name], [RB]) if k == 4 else None)

            def dense(name):
                j, c, n = JS[name], AS[name], int(name[3])
                first_jobs(name, j, c)
                for g in range(2):
                    with pe.Fori(1 - g, GK) as i:
                        for s in range(2):
                            job(j + 15 * g + i, s, c + 15 * g + i, s, xs_hi, xs_lo)
                    h_tiles = (h_ready, 64 + n * 22 + g * GK)
                    if g == 0:
                        with pe.Fori(0, 4) as i:
                            for s in range(2):
                                job(j + 11 + i, s, c + 11 + i, s, hs_hi, hs_lo, K=GK, waits=h_tiles if s == 0 else None)
                with_stats(SQ[name + "_out"],
                           lambda m: job(j + 26 + m // 2, m % 2, c + 26 + m // 2, m % 2, hs_hi, hs_lo, K=GK,
                                         waits=h_tiles if m == 0 else None))
                spread(NORM[name + "_out"], [RB])

            def pooling():
                j, c = JS["pool"], AS["pool"]
                first_jobs("pool", j, c)
                with pe.Fori(1, 4) as i:
                    for s in range(2):
                        job(j + i, s, c + i, s, xs_hi, xs_lo)
                for g in range(4):
                    pe.wait_ge(k_ready, 2 * g + 2)
                    for s in range(2):
                        job(j + 4 + g, s, c + 4 + g, s, po_hi[:, 2 * g:2 * g + 2, :], po_lo[:, 2 * g:2 * g + 2, :], K=2)
                with_stats(SQ["pool_out"], lambda m: job(j + 8 + m // 2, m % 2, c + 8 + m // 2, m % 2, xs_hi, xs_lo,
                                                         waits=(xs_ready, FILL["pool_out"] * 8) if m == 0 else None))
                spread(NORM["pool_out"], [RB])

            def dilated():
                j, c = JS["dilated"], AS["dilated"]

                def two_pairs(p2):
                    n_rope, n_unit, n_v = L * N_ROPE + p2 * 12, L * UNITS + p2 * 16, p2 * 6
                    for e in range(2):
                        jp, cp = j + p2 * 9 + 6 * e, c + p2 * 9 + 6 * e
                        pe.wait_ge(o_split, n_unit + 8 * e)
                        for i in range(6):
                            if p2 + e + i == 0:
                                first_jobs("dilated", j, c)
                            elif p2 + e > 0 or i > 1:
                                hi, lo = (xs_hi, xs_lo) if i < 3 else (ks_hi, ks_lo)
                                if i == 3:
                                    pe.wait_ge(hk_landed, 32)
                                job(jp + i // 2, i % 2, cp + i // 2, i % 2, hi, lo)
                        for i in range(7 if e == 0 else 0):
                            if i < 6:
                                job(jp + 3 + i // 2, i % 2, cp + 3 + i // 2, i % 2, ks_hi, ks_lo)
                            if i >= 3:
                                pe.wait_ge(act_copied, L * COPIES + n_v + i - 2)
                            if i >= 1:
                                turn(2 * L + n_v + i - 1, (i - 1) % 2, P, 6 + (i - 1) % 2)
                        pe.wait_ge(heads_ready, n_rope + 6 * e + 6)
                        pe.wait_ge(act_copied, L * COPIES + n_v + 6)
                        attend(UD[e], n_unit + 8 * e, WIDE, dprob, lambda n: 6, lambda n: dprobt[:, :],
                               lambda un, n: ps[un["row"]:un["row"] + 64, n % 2, 0:P])

                for p2 in range(2):
                    two_pairs(p2)
                pe.wait_ge(o_split, L * UNITS + 32)
                with_stats(SQ["dilated_out"],
                           lambda m: job(j + 18 + m // 2, m % 2, c + 18 + m // 2, m % 2, dm_hi, dm_lo, K=4))
                spread(NORM["dilated_out"], [RB])

            dense("ffn0")
            pooling()
            dense("ffn1")
            dense("ffn2")
            dilated()
            dense("ffn3")

        @block.scalar
        def _(act):
            copy = lambda o, i: nc.scalar.activation(o, i, ACT.Copy)

            def split(jp, s, n, free_at=None):
                act.wait_ge(w_landed[s], 16 * jp + 16)
                if free_at is not None:
                    act.wait_ge(acc_full, free_at)
                copy(w_hi[:, s, 0:n], stage[:, s, 0:n]).then_inc(w_hi_done, 1)

            def square(n, s, t):
                act.wait_ge(sq_used, n + 1)
                nc.scalar.activation(sq[:, s:s + 1, :], t, ACT.Square).then_inc(sq_ready, 1)

            def take_x(name):
                for m in range(KD):
                    if X_NEW[name] is not None:
                        act.wait_ge(x_new, X_NEW[name] + m + 1)
                    else:
                        act.wait_ge(xs_ready, 8 * (FILL[name] - 1) + m + 1)
                    t, hi = x[:, m, :], xs_hi[:, m, :]
                    if name == "dilated":
                        t, hi = by_class(t), by_class(hi, True)
                    nc.scalar.activation(hi, t, ACT.Identity, scale=ngain[:, GAIN[name], m:m + 1]).then_inc(xs_hi_done, 1)
                    square(SQ[name] + m, m % 2, x[:, m:m + 1, :])

            def layer_norm(f, g):
                for m in range(KD):
                    act.wait_ge(tile_ready, 8 * f + m + 1)
                    for o in (x[:, m, :], xs_hi[:, m, :]):
                        last = nc.scalar.activation(o, norm_tile(m), ACT.Identity, bias=lng[:, g + 1, m:m + 1],
                                                    scale=lng[:, g, m:m + 1])
                    last.then_inc(xs_hi_done, 1)

            def rotate(c2, b, full):
                act.wait_ge(acc_full, c2 + 1)
                for h in range(4):
                    last = copy(rot[32 * h:32 * h + 32, b, :], ps[32 * (h ^ 1):32 * (h ^ 1) + 32, b, :])
                last.then_inc(rot_ready, 1)

            def exps(un, n, c0, probs, ring):
                b = n % ring
                act.wait_ge(masked, c0 + n + 1)
                if un["sink"] is not None:
                    nc.scalar.activation(col[:, b, 2:3], nsink[:, un["sink"]:un["sink"] + 1], ACT.Exp,
                                         bias=col[:, b, 0:1], scale=-1.0)
                nc.scalar.activation(probs[:, b, 0:un["W"]], probs[:, b, 0:un["W"]], ACT.Exp, bias=col[:, b, 0:1],
                                     scale=-1.0, accum_out=col[:, b, 1:2]).then_inc(p_exp, 1)

            def attend(U, c0, F, probs, probs_t, t_bank, o_of, hi_of):
                N = len(U)
                for n in range(F["exps"]):
                    exps(U[n], n, c0, probs, F["ring"])
                for n in range(N + F["o_hi"]):
                    if n + F["exps"] < N:
                        exps(U[n + F["exps"]], n + F["exps"], c0, probs, F["ring"])
                    m = n - F["o_hi"]
                    if m >= 0:
                        act.wait_ge(o_full, c0 + m + 1)
                        copy(hi_of(U[m]), o_of(U[m], m)).then_inc(o_hi_done, 1)
                    if n < N:
                        W = U[n]["W"]
                        act.wait_ge(pt_full, c0 + n + 1)
                        if n >= 1 + F["mix"]:
                            act.wait_ge(o_full, c0 + n - F["mix"])
                        tb = t_bank(n)
                        src = ps[:, tb, 0:W] if W <= T else ps[:, tb:tb + 2, :].rearrange("p b t -> p (b t)")[:, 0:W]
                        copy(probs_t(n)[:, 0:W], src).then_inc(pt_copied, 1)

            def silu_pair(jp, ap, n, s0, s1, scaled=None):
                split(jp + 1, 0, s0, 2 * ap + 1)
                if scaled is not None:
                    act.wait_ge(gate_scaled, scaled + 1)
                    nc.scalar.activation(sg[:, :], tmp[:, 0, :], ACT.Silu).then_inc(sg_ready, 1)
                else:
                    act.wait_ge(sg_used, n + 1)
                    nc.scalar.activation(sg[:, :], ps[:, 0, :], ACT.Silu).then_inc(sg_ready, 1)
                    act.drain().then_inc(acc_free[0], 1)
                split(jp + 1, 1, s1, 2 * ap + 2)

            def down_squares(n0, j1, c1, n_w, n_next, Y=y):
                with act.Fori(0, 3) as i:
                    for s in range(2):
                        split(j1 + i, s, n_w, 2 * (c1 + i) + s + 1)
                        act.wait_ge(acc_free[s], c1 + 2 + i)
                        square(n0 + 2 * i + s, s, Y[:, bass.ds(2 * i + s, 1), :])
                if n_next is not None:
                    split(j1 + 3, 0, n_next, 2 * (c1 + 3) + 1)
                for s in range(2):
                    act.wait_ge(acc_free[s], c1 + 5)
                    square(n0 + 6 + s, s, Y[:, 6 + s:7 + s, :])
                if n_next is not None:
                    split(j1 + 3, 1, n_next, 2 * (c1 + 3) + 2)

            for m in range(KD):
                if m % 4 == 0:
                    act.wait_ge(x_landed[m // 4], 16)
                copy(xs_hi[:, m, :], x[:, m, :]).then_inc(xs_hi_done, 1)
                if m % 4 == 3:
                    split(0, m // 4, W_FULL)
            act.wait_ge(const_landed, 144)
            copy(wr_hi[:, :], wr[:, :]).then_inc(wr_hi_done, 1)
            with act.Fori(0, L) as l:
                j, c = l * JL, l * AL
                act.preload_act_table(ACT.Exp)
                for i in range(3):
                    split(j + 1 + i // 2, i % 2, (W_FULL, W_KR, W_VA)[i], 2 * c + i + 1)
                    act.wait_ge(acc_full, 2 * c + i + 1)
                    copy(cfeat[:, i, :], ps[:, i % 2, :]).then_inc(c_copied, 1)
                    act.drain().then_inc(acc_free[i % 2], 1)
                act.wait_ge(acc_full, 2 * c + 4)
                split(j + 2, 1, W_VB, 2 * c + 4)
                for s, N in ((0, P), (1, 68)):
                    act.wait_ge(acc_full, 2 * c + 5 + s)
                    copy(rot[0:N, s, :], ps[0:N, s, :]).then_inc(v_evacuated, 1)
                    act.drain().then_inc(acc_free[s], 1)
                    split(j + 3, s, W_FULL, 2 * c + 5 + s)
                for s, N, o in ((0, P, va), (1, 68, vb)):
                    act.wait_ge(v_turned, 2 * l + s + 1)
                    copy(flat(o), ps[:, 5 + s, 0:NT * N]).then_inc(act_copied, 1)
                with act.Fori(0, 4) as i:
                    for s in range(2):
                        split(j + 4 + i, s, W_FULL, 2 * (c + 3 + i) + s + 1)
                        rotate(2 * (c + 3 + i) + s, s, True)
                for s in range(2):
                    split(j + 8, s, (W_FULL, W_UP)[s], 2 * (c + 7) + s + 1)
                    rotate(2 * (c + 7) + s, s, True)
                for i in range(3):
                    act.wait_ge(c_tile, 3 * l + i + 1)
                    copy(cs_hi[:, i, :], cfeat[:, i, :]).then_inc(c_hi_done, 1)
                split(j + 9, 0, W_FULL, 2 * c + 17)
                rotate(2 * c + 16, 0, True)
                for i in range(4):
                    act.wait_ge(acc_full, 2 * c + 18 + i)
                    copy(qc[0:64, i, :], ps[0:64, (i + 1) % 2, :]).then_inc(act_copied, 1)
                for i in range(2):
                    act.wait_ge(acc_full, 2 * c + 22 + i)
                    copy(kc[0:64, 2 * i, :], ps[0:64, (i + 1) % 2, :]).then_inc(act_copied, 1)
                    copy(kc[0:64, 2 * i + 1, :], ps[64:128, (i + 1) % 2, :]).then_inc(act_copied, 1)
                    act.drain().then_inc(acc_free[(i + 1) % 2], 1)
                for i in range(2):
                    act.wait_ge(acc_full, 2 * c + 24 + i)
                    copy(vc[:, 2 * i:2 * i + 2, :].rearrange("p a b -> p (a b)"), ps[:, (i + 1) % 2, :]).then_inc(act_copied, 1)
                    act.drain().then_inc(acc_free[(i + 1) % 2], 1)
                split(j + 9, 1, W_FULL, 2 * c + 25)
                for n, (qt, h) in enumerate(IX):
                    act.wait_ge(ix_full, l * len(IX) + n + 1)
                    if n >= 2:
                        act.wait_ge(ix_used, l * len(IX) + n - 1)
                    nc.scalar.activation(rl[:, n % 2, 0:(qt + 1) * P], ps[:, 2 + n % 2, 0:(qt + 1) * P], ACT.Relu,
                                         scale=1.0 / 16).then_inc(ix_relu, 1)
                attend(UN, l * UNITS, DEEP, prob, lambda n: probt[:, n % 2, :], lambda n: 4 + n % 2,
                       lambda un, n: ps[un["row"]:un["row"] + 64, 6 + n % 2, 0:P],
                       lambda un: xs_hi[un["row"]:un["row"] + 64, un["tile"], un["at"]:un["at"] + P])
                for m in range(KD):
                    split(j + 10 + m // 2, m % 2, W_FULL, 2 * (c + 12) + m + 2)
                    act.wait_ge(acc_free[1 - m % 2], c + 14 + (m + 1) // 2)
                    square(l * 16 + m, m % 2, x[:, m:m + 1, :])
                layer_norm(2 * l + 1, 0)
                act.wait_ge(acc_full, 2 * c + 34)
                copy(gates_t[:, :], ps[0:E, 1, :]).then_inc(logits_copied, 1)
                act.drain().then_inc(acc_free[1], 1)
                act.wait_ge(logits_full, l + 1)
                nc.scalar.activation(rt[:, 1, :], ps[:, STAT, 0:NT * E], ACT.Tanh, scale=0.5).then_inc(r_tanh, 1)
                act.wait_ge(gt_full, l + 1)
                copy(gates_t[:, :], ps[0:E, STAT, :]).then_inc(gt_copied, 1)
                act.preload_act_table(ACT.Silu)
                jm, cm = j + J_MOE // 2, c + A_MOE // 2

                def gate_up(q):
                    with act.Fori(0, 8) as i:
                        silu_pair(jm + q * 12 + i, cm + q * 12 + i, l * 32 + q * 8 + i, W_FULL, W_FULL)

                with act.Fori(0, 3) as q:
                    gate_up(q)
                    with act.Fori(0, 4) as i:
                        for s in range(2):
                            split(jm + q * 12 + 9 + i, s, W_FULL, 2 * (cm + q * 12 + 8 + i) + s + 1)
                gate_up(3)
                down_squares(l * 16 + 8, jm + 45, cm + 44, W_FULL, W_FULL)
                layer_norm(2 * l + 2, 2)

            def dense(name, last=False):
                j, c, n = JS[name], AS[name], int(name[3])
                take_x(name)
                act.preload_act_table(ACT.Silu)
                for g in range(2):
                    jg, c_g, n_g = j + 15 * g, c + 15 * g, 64 + 22 * n + GK * g
                    i0 = 0
                    if name == "ffn2" and g == 0:
                        i0 = len(KEY_TILES)
                        for i in range(i0):
                            silu_pair(jg + i, c_g + i, n_g + i, W_FULL, W_FULL, n_g - 64 + i)
                            for m in KEY_TILES[i]:
                                act.wait_ge(hk_ready, m + 1)
                                copy(by_class(hs_hi[:, GK - KD + m, :], True), by_class(y[:, m, :])).then_inc(hk_hi_done, 1)
                    with act.Fori(i0, GK - 1) as i:
                        silu_pair(jg + i, c_g + i, n_g + i, W_FULL, W_FULL, n_g - 64 + i)
                    silu_pair(jg + 10, c_g + 10, n_g + 10, W_DOWN, W_DOWN, n_g - 64 + 10)
                    if g == 0:
                        with act.Fori(0, 3) as i:
                            for s in range(2):
                                split(jg + 12 + i, s, W_DOWN, 2 * (c_g + 11 + i) + s + 1)
                        for s in range(2):
                            split(jg + 15, s, W_FULL, 2 * (c_g + 14) + s + 1)
                        if name == "ffn0":
                            for i in range(2):
                                act.wait_ge(tab_in, i + 1)
                                nc.scalar.activation(dtab[:, i, :], dtab[:, i, :], ACT.Sin).then_inc(tab_done, 1)
                            act.preload_act_table(ACT.Silu)
                down_squares(SQ[name + "_out"], j + 27, c + 26, W_DOWN, None if last else W_FULL)

            dense("ffn0")
            j, c = JS["pool"], AS["pool"]
            take_x("pool")
            for m in range(8):
                n_w = W_FULL if m < 6 else 2 * P
                split(j + 1 + m // 2, m % 2, n_w, 2 * c + m + 1)
                act.wait_ge(c_tile, 3 * L + m + 1)
                copy(po_hi[:, m, :], tmp[:, m % 2, :]).then_inc(k_hi_done, 1)
            for m in range(8):
                n_w = 2 * P if m < 6 else W_FULL
                split(j + 5 + m // 2, m % 2, n_w, 2 * c + 8 + m + 1)
                act.wait_ge(tile_ready, 8 * (1 + 2 * L) + m + 1)
                copy(xs_hi[:, m, :], tmp[:, m % 2, :]).then_inc(xs_hi_done, 1)
            down_squares(SQ["pool_out"], j + 9, c + 8, W_FULL, W_FULL)
            dense("ffn1")
            dense("ffn2")
            j, c = JS["dilated"], AS["dilated"]
            take_x("dilated")
            act.preload_act_table(ACT.Exp)
            with act.Fori(0, 2) as p2:
                for e in range(2):
                    jp, cp = j + p2 * 9 + 6 * e, c + p2 * 9 + 6 * e
                    for i in range(6):
                        split(jp + 1 + i // 2, i % 2, W_FULL, 2 * cp + i + 1)
                        rotate(2 * cp + i, i % 2, True)
                    for i in range(7 if e == 0 else 0):
                        if i < 6:
                            act.wait_ge(acc_full, 2 * cp + 7 + i)
                            copy(rot[:, i % 2, :], ps[:, i % 2, :]).then_inc(v_evacuated, 1)
                            act.drain().then_inc(acc_free[i % 2], 1)
                            split(jp + 4 + i // 2, i % 2, W_FULL, 2 * cp + 7 + i)
                        if i >= 1:
                            act.wait_ge(v_turned, 2 * L + p2 * 6 + i)
                            copy(dv[:, :, P * (i - 1):P * i],
                                 ps[:, 6 + (i - 1) % 2, :].rearrange("p (t n) -> p t n", t=4)).then_inc(act_copied, 1)
                    attend(UD[e], L * UNITS + p2 * 16 + 8 * e, WIDE, dprob, lambda n: dprobt[:, :], lambda n: 6,
                           lambda un, n: ps[un["row"]:un["row"] + 64, n % 2, 0:P],
                           lambda un: dm_hi[un["row"]:un["row"] + 64, bass.ds(2 * p2 + e, 1), un["at"]:un["at"] + P])
            down_squares(SQ["dilated_out"], j + 19, c + 18, 4 * P, W_FULL, yd)
            dense("ffn3", last=True)
        @block.vector
        def _(v):
            V = nc.vector
            tt, ts, stt = V.tensor_tensor, V.tensor_scalar, V.scalar_tensor_tensor

            def split(jp, s, n):
                v.wait_ge(w_hi_done, 2 * jp + s + 1)
                tt(w_lo[:, s, 0:n], stage[:, s, 0:n], w_hi[:, s, 0:n].bitcast(F32), ALU.subtract).then_inc(w_split, 1)

            def norm_columns(n, kind, n0, half=False):
                if kind == "c":
                    v.drain().then_inc(stat_in, 1)
                    v.wait_ge(stat_full, n0 + 1)
                else:
                    v.wait_ge(sq_used, n0 + KD + 2)
                r, mean, var, t = small[:, 0:8], small[:, 8:12], small[:, 16:24], small[:, 24:32]
                w = 8 if kind == "c" else 4
                if kind == "ln":
                    ts(mean, ps[:, STAT, 4:8], 1.0 / D, None, ALU.mult)
                    v.drain()
                    tt(t[:, 0:4], mean, mean, ALU.mult)
                    v.drain()
                    stt(var[:, 0:4], ps[:, STAT, 0:4], 1.0 / D, t[:, 0:4], ALU.mult, ALU.subtract)
                    v.drain()
                    ts(var[:, 0:4], var[:, 0:4], LN_EPS, None, ALU.add)
                elif kind == "rms":
                    ts(var[:, 0:4], ps[:, STAT, 0:4], 1.0 / D, RMS_EPS, ALU.mult, ALU.add)
                else:
                    ts(var[:, 0:4], ps[:, STAT, 0:4], 1.0 / 256, RMS_EPS, ALU.mult, ALU.add)
                    ts(var[:, 4:8], ps[:, STAT, 4:8], 1.0 / 128, RMS_EPS, ALU.mult, ALU.add)
                v.drain()
                r, var, t = r[:, 0:w], var[:, 0:w], t[:, 0:w]
                ts(t.bitcast(I32), var.bitcast(I32), 1, None, ALU.logical_shift_right)
                v.drain()
                ts(r.bitcast(I32), t.bitcast(I32), -1.0, float(0x5F3759DF), ALU.mult, ALU.add)
                v.drain()
                for _ in range(3):
                    stt(t, r, -0.5, r, ALU.mult, ALU.mult)
                    v.drain()
                    tt(t, t, var, ALU.mult)
                    v.drain()
                    stt(r, t, 1.5, r, ALU.add, ALU.mult)
                    v.drain()
                if half:
                    ts(r, r, 0.5, None, ALU.mult)
                if kind == "ln":
                    stt(small[:, 4:8], mean, -1.0, r, ALU.mult, ALU.mult)
                v.drain().then_inc(rstd_ready, 1)

            def norm(n, kind, n0, half=False, meanwhile=None):
                norm_columns(n, kind, n0, half)
                if meanwhile is not None:
                    meanwhile()
                hold(v, rb_full, n + 1)

            def layer_norm(n, f, src, n0, meanwhile=None):
                norm(n, "ln", n0, meanwhile=meanwhile)
                for i in range(KD + 3):
                    if i < KD:
                        tt(norm_tile(i), src[:, i, :], ps[:, RB, :], ALU.mult)
                    if 1 <= i <= KD:
                        tt(norm_tile(i - 1), norm_tile(i - 1), ps[:, MB, :], ALU.add).then_inc(tile_ready, 1)
                    if i >= 3:
                        m = i - 3
                        v.wait_ge(xs_hi_done, 8 * f + m + 1)
                        tt(xs_lo[:, m, :], x[:, m, :], xs_hi[:, m, :].bitcast(F32), ALU.subtract).then_inc(xs_ready, 1)
                    v.drain()

            def rope(a2, r, b, dst, cos, sin):
                v.wait_ge(acc_full, a2 + 1)
                v.wait_ge(rot_ready, r + 1)
                tt(dst, ps[:, b:b + 1, :], cos, ALU.mult)
                tt(tmp[:, b:b + 1, :], rot[:, b:b + 1, :], sin, ALU.mult).then_inc(acc_free[b], 1)
                v.drain()
                tt(dst, dst, tmp[:, b:b + 1, :], ALU.add).then_inc(heads_ready, 1)

            def mask_scores(un, n, c0, F, probs):
                b, W, bank = n % F["ring"], un["W"], F["banks"][n % len(F["banks"])]
                if n >= F["ring"]:
                    v.wait_ge(pt_full, c0 + n - F["ring"] + 1)
                hold(v, s_full, c0 + n + 1)
                src = ps[:, bank, 0:W] if F is DEEP else ps[:, bank:bank + 2, :].rearrange("p b t -> p (b t)")[:, 0:W]
                m = un["mask"] if F is DEEP else mask_d[:, un["mask"], :]
                init = 3.0e38 if un["sink"] is None else nsink[:, un["sink"]:un["sink"] + 1]
                V.tensor_tensor_reduce(probs[:, b, 0:W], src, m, -un["scale"], init, ALU.add, ALU.min,
                                       col[:, b, 0:1]).then_inc(masked, 1)

            def attend(U, c0, F, probs, o_of, hi_of, lo_of, between=None):
                N = len(U)

                def low(m):
                    if 0 <= m < N:
                        v.wait_ge(o_hi_done, c0 + m + 1)
                        tt(lo_of(U[m]), o_of(U[m], m), hi_of(U[m]).bitcast(F32), ALU.subtract).then_inc(o_split, 1)

                for n in range(F["exps"]):
                    mask_scores(U[n], n, c0, F, probs)
                for n in range(N + F["o_lo"]):
                    b, select = n % F["ring"], None if between is None else between(n)
                    if n + F["exps"] < N and F is DEEP:
                        mask_scores(U[n + F["exps"]], n + F["exps"], c0, F, probs)
                    if n < N:
                        if U[n]["sink"] is not None:
                            v.wait_ge(p_exp, c0 + n + 1)
                            tt(col[:, b, 1:2], col[:, b, 1:2], col[:, b, 2:3], ALU.add)
                        v.drain()
                        if U[n]["sink"] is None:
                            v.wait_ge(p_exp, c0 + n + 1)
                        V.reciprocal(col[:, b, 3:4], col[:, b, 1:2])
                    if select is not None:
                        V.max(max8[:, :], select)
                    v.drain()
                    if n < N:
                        W = U[n]["W"]
                        ts(probs[:, b, 0:W], probs[:, b, 0:W], col[:, b, 3:4], None, ALU.mult).then_inc(p_norm, 1)
                    if select is not None:
                        V.match_replace(select, max8[:, :], select, TAKEN)
                    if n + F["exps"] < N and F is WIDE:
                        mask_scores(U[n + F["exps"]], n + F["exps"], c0, F, probs)
                    low(n - F["o_lo"])

            def out_tile(ap, s, m, Y, add):
                v.wait_ge(acc_full, 2 * ap + s + 1)
                ym = Y[:, bass.ds(m, 1), :]
                if add:
                    tt(ym, ym, ps[:, s:s + 1, :], ALU.add).then_inc(acc_free[s], 1)
                else:
                    ts(ym, ps[:, s:s + 1, :], 1.0, None, ALU.mult).then_inc(acc_free[s], 1)

            def out_tiles(j1, c1, n_w, more, Y, add, tile=None):
                tile = tile or out_tile
                with v.Fori(0, 3) as i:
                    for s in range(2):
                        split(j1 + i, s, n_w)
                        tile(c1 + i, s, 2 * i + s, Y, add)
                if more:
                    split(j1 + 3, 0, W_FULL)
                for s in range(2):
                    tile(c1 + 3, s, 6 + s, Y, add)

            def router():
                v4 = lambda i: rt[:, i, :].rearrange("p (g e) -> p g e", e=TOKG)
                scores, biased, rank, sel = rt[:, 2, :], rt[:, 3, :], rt[:, 4, :], rt[:, 5, :]
                ts(scores, rt[:, 1, :], 0.5, 0.5, ALU.mult, ALU.add)
                v.drain()
                tt(biased.rearrange("p (t e) -> p t e", e=E), scores.rearrange("p (t e) -> p t e", e=E),
                   rbias[:, :].unsqueeze(1).to_broadcast([P, NT, E]), ALU.add)
                v.drain()

                def ranks(o, vals, g):
                    other = vals.unsqueeze(2).to_broadcast([P, g, 4, 4])
                    own = vals.unsqueeze(3).to_broadcast([P, g, 4, 4])
                    gt, eq = (pairs[:, i, 0:16 * g].rearrange("p (g j i) -> p g j i", j=4, i=4) for i in range(2))
                    tt(gt, other, own, ALU.is_gt)
                    tt(eq, other, own, ALU.is_equal)
                    v.drain()
                    tt(eq, eq, tri[:, :].rearrange("p (j i) -> p j i", j=4).unsqueeze(1).to_broadcast([P, g, 4, 4]), ALU.mult)
                    v.drain()
                    tt(gt, gt, eq, ALU.add)
                    v.drain()
                    V.tensor_reduce(o, gt, AX.X, ALU.add)
                    v.drain()

                ranks(v4(4), v4(3), 16)
                ts(sel, rank, 1.5, None, ALU.is_lt)
                v.drain()
                tt(rt[:, 6, :], biased, sel, ALU.mult)
                v.drain()
                gsum, grank = rt[:, 7, 0:16], rt[:, 7, 16:32]
                V.tensor_reduce(gsum, v4(6), AX.X, ALU.add)
                v.drain()
                ranks(grank.rearrange("p (t g) -> p t g", g=4), gsum.rearrange("p (t g) -> p t g", g=4), 4)
                ts(grank, grank, 0.5, None, ALU.is_lt)
                v.drain()
                tt(v4(5), v4(5), grank.unsqueeze(2).to_broadcast([P, 16, 4]), ALU.mult)
                v.drain()
                tt(rt[:, 6, :], scores, sel, ALU.mult)
                v.drain()
                total, inv = rt[:, 7, 32:36], rt[:, 7, 36:40]
                V.tensor_reduce(total, rt[:, 6, :].rearrange("p (t e) -> p t e", e=E), AX.X, ALU.add)
                v.drain()
                V.reciprocal(inv, total)
                v.drain()
                tt(rt[:, 0, :].rearrange("p (t e) -> p t e", e=E), rt[:, 6, :].rearrange("p (t e) -> p t e", e=E),
                   inv.unsqueeze(2).to_broadcast([P, NT, E]), ALU.mult).then_inc(gates_ready, 1)

            def scale_gate(ap):
                v.wait_ge(acc_full, 2 * ap + 1)
                tt(tmp[:, 0, :], ps[:, 0, :], rstd[:, :], ALU.mult).then_inc(acc_free[0], 1)
                v.drain().then_inc(gate_scaled, 1)

            def hidden(ap, n, k, gate=None, last_of_gate=False, scaled=False):
                v.drain()
                if scaled:
                    v.wait_ge(acc_full, 2 * ap + 2)
                    tt(hh[:, :], ps[:, 1, :], rstd[:, :], ALU.mult).then_inc(acc_free[1], 1)
                    v.drain()
                    v.wait_ge(sg_ready, n + 1)
                    tt(hh[:, :], sg[:, :], hh[:, :], ALU.mult)
                else:
                    v.wait_ge(sg_ready, n + 1)
                    v.wait_ge(acc_full, 2 * ap + 2)
                    tt(hh[:, :], sg[:, :], ps[:, 1, :], ALU.mult).then_inc(acc_free[1], 1)
                v.drain().then_inc(sg_used, 1)
                if gate is not None:
                    v.wait_ge(gb_landed, gate)
                    tt(hh[:, :], hh[:, :], gb[:, :], ALU.mult)
                    v.drain()
                    if last_of_gate:
                        v.drain().then_inc(gb_used, 1)
                h3 = hh[:, :].rearrange("p (a t) -> p a t", a=1)
                ts(hs_hi[:, bass.ds(k, 1), :], h3, 1.0, None, ALU.mult)
                v.drain()
                tt(hs_lo[:, bass.ds(k, 1), :], h3, hs_hi[:, bass.ds(k, 1), :].bitcast(F32), ALU.subtract).then_inc(h_ready, 1)

            v.sem_inc(w_split, RING)
            for b in range(RING):
                v.sem_inc(acc_free[b], 1)
            for s_ in (gb_used, sg_used, place_free):
                v.sem_inc(s_, 1)
            v.sem_inc(sq_used, 2)
            v.sem_inc(tile_ready, KD)
            for m in range(KD):
                v.wait_ge(xs_hi_done, m + 1)
                tt(xs_lo[:, m, :], x[:, m, :], xs_hi[:, m, :].bitcast(F32), ALU.subtract).then_inc(xs_ready, 1)
                if m % 4 == 3:
                    split(0, m // 4, W_FULL)
            v.wait_ge(const_landed, 144)
            v.wait_ge(wr_hi_done, 1)
            tt(wr_lo[:, :], wr[:, :], wr_hi[:, :].bitcast(F32), ALU.subtract).then_inc(wr_ready, 1)
            with v.Fori(0, L) as l:
                j, c = l * JL, l * AL
                v.wait_ge(layer_landed, l * 48 + 48)
                ts(nsink[:, :], nsink[:, :], -1.0, None, ALU.mult)
                for i in range(3):
                    split(j + 1 + i // 2, i % 2, (W_FULL, W_KR, W_VA)[i])
                    v.wait_ge(c_copied, 3 * l + i + 1)
                    tt((sum2[:, :], sq[:, 0, :], sum1[:, :])[i], cfeat[:, i, :], cfeat[:, i, :], ALU.mult)
                    if i == 1:
                        v.drain()
                        tt(sum2[:, :], sum2[:, :], sq[:, 0, :], ALU.add)
                split(j + 2, 1, W_VB)
                v.wait_ge(acc_full, 2 * c + 4)
                tt(krope[64:96, :], ps[0:32, 1, :], tabc[0:32, :], ALU.mult)
                tt(tmp[64:96, 1, :], ps[32:64, 1, :], tabc[32:64, :], ALU.mult).then_inc(acc_free[1], 1)
                v.drain()
                tt(krope[64:96, :], krope[64:96, :], tmp[64:96, 1, :], ALU.add).then_inc(kr_ready, 1)
                split(j + 3, 0, W_FULL)
                split(j + 3, 1, W_FULL)
                norm_columns(3 * l, "c", l)
                cos, sin = tabs[:, 0:1, :], tabs[:, 1:2, :]
                with v.Fori(0, 4) as i:
                    for s in range(2):
                        split(j + 4 + i, s, W_FULL)
                        rope(2 * (c + 3 + i) + s, l * N_ROPE + 2 * i + s, s, heads[:, bass.ds(2 * i + s, 1), :], cos, sin)
                for s in range(2):
                    split(j + 8, s, (W_FULL, W_UP)[s])
                    rope(2 * (c + 7) + s, l * N_ROPE + 8 + s, s, heads[:, 8 + s:9 + s, :], cos, sin)
                v.wait_ge(rb_full, 3 * l + 1)
                for i in range(3):
                    stt(cfeat[:, i, :], cfeat[:, i, :], cg[:, i:i + 1], ps[:, (RB, RB, MB)[i], :], ALU.mult, ALU.mult)\
                        .then_inc(c_tile, 1)
                for i in range(3):
                    v.wait_ge(c_hi_done, 3 * l + i + 1)
                    tt(cs_lo[:, i, :], cfeat[:, i, :], cs_hi[:, i, :].bitcast(F32), ALU.subtract).then_inc(c_ready, 1)
                split(j + 9, 0, W_FULL)
                rope(2 * c + 16, l * N_ROPE + 10, 0, heads[:, 10:11, :], cos, sin)
                for i in range(4):
                    b = (i + 1) % 2
                    v.wait_ge(acc_full, 2 * c + 18 + i)
                    v.wait_ge(act_copied, l * COPIES + 3 + i)
                    tt(qc[64:96, i, :], ps[64:96, b, :], tabc[64:96, :], ALU.mult)
                    tt(tmp[64:96, b, :], ps[96:128, b, :], tabc[96:128, :], ALU.mult).then_inc(acc_free[b], 1)
                    v.drain()
                    tt(qc[64:96, i, :], qc[64:96, i, :], tmp[64:96, b, :], ALU.add).then_inc(qc_ready, 1)
                split(j + 9, 1, W_FULL)
                for n, (qt, h) in enumerate(IX):
                    work, src, wcol = maskb[:, qt, 0:(qt + 1) * P], rl[:, n % 2, 0:(qt + 1) * P], vb[:, qt, 64 + h:65 + h]
                    v.drain()
                    v.wait_ge(ix_relu, l * len(IX) + n + 1)
                    if h == 0:
                        ts(work, src, wcol, None, ALU.mult).then_inc(ix_used, 1)
                    else:
                        stt(work, src, wcol, work, ALU.mult, ALU.add).then_inc(ix_used, 1)
                v.drain()
                for qt in range(1, NT):
                    work = maskb[:, qt, 0:(qt + 1) * P]
                    stt(work, mask_c[:, (3 - qt) * P:T], CAUSAL / MASKED, work, ALU.mult, ALU.add)
                V.tensor_copy(maskb[:, 0, 0:P], mask_c[:, 3 * P:T])
                rounds = [maskb[:, qt, 0:(qt + 1) * P] for qt in range(1, NT) for i in range(TOPK // 8)]
                B_MASKED = 48 - DEEP["exps"]

                def between(n):
                    if n < B_MASKED:
                        return rounds[n]
                    if n == B_MASKED:
                        for work in rounds[n:]:
                            v.drain()
                            V.max(max8[:, :], work)
                            v.drain()
                            V.match_replace(work, max8[:, :], work, TAKEN)
                        v.drain()
                        for qt in range(1, NT):
                            work = maskb[:, qt, 0:(qt + 1) * P]
                            ts(work, work, TAKEN * 0.99, MASKED, ALU.is_gt, ALU.mult)
                        v.drain()

                attend(UN, l * UNITS, DEEP, prob, lambda un, n: ps[un["row"]:un["row"] + 64, 6 + n % 2, 0:P],
                       lambda un: xs_hi[un["row"]:un["row"] + 64, un["tile"], un["at"]:un["at"] + P],
                       lambda un: xs_lo[un["row"]:un["row"] + 64, un["tile"], un["at"]:un["at"] + P], between)
                for m in range(KD):
                    split(j + 10 + m // 2, m % 2, W_FULL)
                    v.wait_ge(acc_full, 2 * (c + 12) + m + 2)
                    b = 1 - m % 2
                    stt(x[:, m, :], x[:, m, :], ALPHA, ps[:, b, :], ALU.mult, ALU.add).then_inc(acc_free[b], 1)
                layer_norm(3 * l + 1, 2 * l + 1, x, l * 16)
                v.wait_ge(r_tanh, l + 1)
                router()
                ts(flat(y), flat(x), ALPHA, None, ALU.mult)
                v.drain()
                jm, cm = j + J_MOE // 2, c + A_MOE // 2

                def experts(q):
                    with v.Fori(0, 4) as e:
                        for f in range(2):
                            for s in range(2):
                                split(jm + q * 12 + 1 + 2 * e + f, s, W_FULL)
                            hidden(cm + q * 12 + 2 * e + f, l * 32 + q * 8 + 2 * e + f, 2 * e + f,
                                   gate=(l * 16 + q * 4 + e) * 16 + 16, last_of_gate=(f == 1))

                with v.Fori(0, 3) as q:
                    experts(q)
                    with v.Fori(0, 4) as i:
                        for s in range(2):
                            split(jm + q * 12 + 9 + i, s, W_FULL)
                            out_tile(cm + q * 12 + 8 + i, s, 2 * i + s, y, True)
                experts(3)
                out_tiles(jm + 45, cm + 44, W_FULL, True, y, True)
                layer_norm(3 * l + 2, 2 * l + 2, y, l * 16 + 8, lambda: split(jm + 48, 1, W_FULL))
                v.drain().then_inc(place_free, 1)

            def low_part(name, m):
                v.wait_ge(xs_hi_done, 8 * FILL[name] + m + 1)
                t, hi, lo = x[:, m, :], xs_hi[:, m, :].bitcast(F32), xs_lo[:, m, :]
                if name == "dilated":
                    t, hi, lo = by_class(t), by_class(hi, True), by_class(lo, True)
                stt(lo, t, ngain[:, GAIN[name], m:m + 1], hi, ALU.mult, ALU.subtract).then_inc(xs_ready, 1)

            def statistics(name):
                norm(NORM[name], "rms", SQ[name])
                V.tensor_copy(rstd[:, :], ps[:, RB, :])
                v.drain()

            def residual(name, t, half, meanwhile, after):
                norm(NORM[name], "rms", SQ[name], half, meanwhile)
                for m in range(KD + (3 if after else 1)):
                    if m < KD:
                        stt(tmp[:, m % 2, :], t[:, m, :], ngain[:, GAIN[name], m:m + 1], ps[:, RB, :], ALU.mult, ALU.mult)
                    if 1 <= m <= KD:
                        tt(x[:, m - 1, :], x[:, m - 1, :], tmp[:, (m - 1) % 2, :], ALU.add).then_inc(x_new if after else y_final, 1)
                    if after and m >= 3:
                        low_part(after, m - 3)
                    v.drain()
                if after:
                    statistics(after)

            def dense(name, after, last=False):
                j, c, n = JS[name], AS[name], int(name[3])
                for g in range(2):
                    jg, c_g = j + 15 * g, c + 15 * g
                    n_g = 64 + 22 * n + GK * g

                    def hidden_tile(i):
                        split(jg + 1 + i, 0, W_FULL)
                        scale_gate(c_g + i)
                        split(jg + 1 + i, 1, W_FULL)
                        hidden(c_g + i, n_g + i, i, scaled=True)

                    def gate_up(i0, i1):
                        with v.Fori(i0, i1) as i:
                            hidden_tile(i)

                    if name == "ffn2" and g == 0:
                        for i, ms in enumerate(KEY_TILES):
                            hidden_tile(i)
                            keys_input(ms)
                        for i, ms in enumerate(KEY_TILES):
                            v.wait_ge(hk_stored[i], 32)
                            gate_up(GK - KD + ms[0], min(GK - KD + ms[-1] + 1, GK - 1))
                    else:
                        gate_up(0, GK - 1)
                    if name == "ffn0" and g == 0:
                        angles()
                    split(jg + GK, 0, W_DOWN)
                    scale_gate(c_g + GK - 1)
                    split(jg + GK, 1, W_DOWN)
                    hidden(c_g + GK - 1, n_g + GK - 1, GK - 1, scaled=True)
                    if name == "ffn0" and g == 0:
                        reduce_angles(0)
                    if name == "ffn0" and g == 1:
                        v.wait_ge(tab_done, 2)
                        ts(dtab[:, 1, :], dtab[:, 1, :], dcol[:, 1:2], None, ALU.mult)
                    out_tiles(jg + 12, c_g + GK, W_DOWN, not (last and g == 1), y, g == 1)
                    if g == 0:
                        split(jg + 15, 1, W_FULL)
                        if name == "ffn0":
                            reduce_angles(1)
                if name == "ffn0":
                    v.drain().then_inc(place_free, 1)
                residual(name + "_out", y, True, None if last else lambda: split(j + 30, 1, W_FULL), after)

            def angles():
                v.wait_ge(pos_landed, 32)
                ang, turns = sum2[:, :], sq[:, 0, :]
                V.tensor_copy(turns, sum1[:, :].bitcast(I32))
                v.drain()
                ts(ang, turns, dcol[:, 0:1], None, ALU.mult)
                v.drain()

            def reduce_angles(i):
                shift, ang, turns = (0.25, 0.0)[i], sum2[:, :], sq[:, 0, :]
                ts(turns, ang, 1.0 / (2 * np.pi), shift, ALU.mult, ALU.add)
                v.drain()
                ts(turns, turns, 12582912.0, None, ALU.add)
                v.drain()
                ts(turns, turns, 12582912.0, None, ALU.subtract)
                v.drain()
                o = dtab[:, i, :]
                for part in TWO_PI:
                    stt(o, turns, -part, ang if part == TWO_PI[0] else o, ALU.mult, ALU.add)
                    v.drain()
                if i == 0:
                    ts(o, o, float(np.pi / 2), None, ALU.add)
                    v.drain()
                ts(o, o, PI_BELOW, -PI_BELOW, ALU.min, ALU.max).then_inc(tab_in, 1)
                v.drain()

            def keys_input(ms):
                for m in ms:
                    stt(y[:, m, :], x[:, m, :], ngain[:, GAIN["keys"], m:m + 1], rstd[:, :], ALU.mult, ALU.mult).then_inc(hk_ready, 1)
                for m in ms:
                    v.wait_ge(hk_hi_done, m + 1)
                    k = GK - KD + m
                    tt(by_class(hs_lo[:, k, :], True), by_class(y[:, m, :]), by_class(hs_hi[:, k, :], True).bitcast(F32),
                       ALU.subtract).then_inc(hk_split, 1)

            for m in range(KD):
                low_part("ffn0", m)
            statistics("ffn0")
            dense("ffn0", "pool")

            j, c = JS["pool"], AS["pool"]
            V.memset(u0[:, 0:16], 0.0)
            V.memset(uw[:, 0, 0:16], 0.0)
            V.memset(uw[:, 1, 0:16], 0.0)
            v.wait_ge(late_landed, 32)
            for m in range(KD):
                g = m // 2
                split(j + 1 + m // 2, m % 2, W_FULL if m < 6 else 2 * P)
                v.wait_ge(acc_full, 2 * c + m + 1)
                v.drain()
                tt(u0[:, 16:16 + T], ps[:, m % 2, :], rstd[:, :], ALU.mult).then_inc(acc_free[m % 2], 1)
                if m >= 2:
                    v.wait_ge(k_hi_done, m - 1)
                src = u0
                for i in range(g + 1):
                    dst = uw[:, i % 2, :]
                    v.drain()
                    tt(dst[:, 16:16 + T], src[:, 16:16 + T], src[:, 16 - (1 << i):16 + T - (1 << i)], ALU.add)
                    src = dst
                v.drain()
                t = tmp[:, m % 2, :]
                stt(t, src[:, 16:16 + T], 1.0 / (2 << g), u0[:, 16:16 + T], ALU.mult, ALU.subtract)
                v.drain()
                tt(t[:, 0:16], src[:, 16:32], cnt[:, g, :], ALU.mult)
                v.drain()
                tt(t[:, 0:16], t[:, 0:16], u0[:, 16:32], ALU.subtract).then_inc(c_tile, 1)
                v.wait_ge(k_hi_done, m + 1)
                v.drain()
                tt(po_lo[:, m, :], t, po_hi[:, m, :].bitcast(F32), ALU.subtract).then_inc(k_ready, 1)
            for m in range(KD):
                split(j + 5 + m // 2, m % 2, 2 * P if m < 6 else W_FULL)
                v.wait_ge(acc_full, 2 * c + 8 + m + 1)
                v.drain()
                ts(tmp[:, m % 2, :], ps[:, m % 2, :], pgain[:, m:m + 1], None, ALU.mult).then_inc(tile_ready, 1)
                v.wait_ge(xs_hi_done, 8 * FILL["pool_out"] + m + 1)
                v.sem_inc(acc_free[m % 2], 1)
                tt(xs_lo[:, m, :], tmp[:, m % 2, :], xs_hi[:, m, :].bitcast(F32), ALU.subtract).then_inc(xs_ready, 1)
            out_tiles(j + 9, c + 8, W_FULL, True, y, False)
            residual("pool_out", y, False, lambda: split(j + 12, 1, W_FULL), "ffn1")
            dense("ffn1", "ffn2")

            j, c = JS["dilated"], AS["dilated"]
            dense("ffn2", "dilated")
            v.drain().then_inc(place_free, 1)
            cos, sin = dtab[:, 0:1, :], dtab[:, 1:2, :]
            q_tab = [t[:, :].rearrange("p (a t) -> p a t", a=1) for t in (sum1, sum2)]
            for i in range(2):
                tt(by_class((sum1, sum2)[i][:, :], True), by_class(dtab[:, i, :], True), by_class(ps[:, RB, :]), ALU.mult)
            v.drain()

            with v.Fori(0, 2) as p2:
                for e in range(2):
                    jp, cp = j + p2 * 9 + 6 * e, c + p2 * 9 + 6 * e
                    for i in range(6):
                        split(jp + 1 + i // 2, i % 2, W_FULL)
                        rope(2 * cp + i, L * N_ROPE + p2 * 12 + 6 * e + i, i % 2, dq[:, i:i + 1, :],
                             *(q_tab if i < 3 else (cos, sin)))
                    for i in range(6 if e == 0 else 0):
                        split(jp + 4 + i // 2, i % 2, W_FULL)
                    v.wait_ge(mask_landed, 16)
                    attend(UD[e], L * UNITS + p2 * 16 + 8 * e, WIDE, dprob,
                           lambda un, n: ps[un["row"]:un["row"] + 64, n % 2, 0:P],
                           lambda un: dm_hi[un["row"]:un["row"] + 64, bass.ds(2 * p2 + e, 1), un["at"]:un["at"] + P],
                           lambda un: dm_lo[un["row"]:un["row"] + 64, bass.ds(2 * p2 + e, 1), un["at"]:un["at"] + P])

            def back_in_order(ap, s, m, Y, add):
                v.wait_ge(acc_full, 2 * ap + s + 1)
                ts(Y[:, bass.ds(m, 1), :].rearrange("p a (i c) -> p a c i", c=4),
                   ps[:, s:s + 1, :].rearrange("p a (c i) -> p a c i", c=4), 1.0, None, ALU.mult).then_inc(acc_free[s], 1)

            out_tiles(j + 19, c + 18, 4 * P, True, yd, False, back_in_order)
            residual("dilated_out", yd, False, lambda: split(j + 22, 1, W_FULL), "ffn3")
            dense("ffn3", None, last=True)



def tiles(w):
    k = w.shape[0] // P
    return w.reshape(k, P, -1).transpose(1, 0, 2).reshape(P, -1)


def columns(w):
    return np.stack([tiles(w[:, i:i + P]) for i in range(0, w.shape[1], P)])


def rope_rows(rows, dim, positions):
    inv = (1.0 / (np.float32(10000.0) ** (np.arange(0, dim, 2, dtype=np.float32) / dim))).astype(np.float32)
    return positions.astype(np.float32)[None, :] * inv[rows][:, None]


def first_constants():
    pos = np.arange(T)
    row = np.arange(P)
    ang = rope_rows(row % 32, HD, pos)
    sign = np.where(row % 64 < 32, -1.0, 1.0).astype(np.float32)[:, None]
    tab = np.stack([np.cos(ang), np.sin(ang) * sign], axis=1)
    angc = rope_rows(row % 16, 32, pos)
    signc = np.where(row % 32 < 16, -1.0, 1.0).astype(np.float32)[:, None]
    tabc = np.where((row % 64 < 32)[:, None], np.cos(angc), np.sin(angc) * signc)
    q, k = np.arange(P)[:, None], np.arange(2 * P)[None, :]
    diff = q + P - k
    mask_a = np.where((diff >= 0) & (diff < P), 0.0, MASKED)
    mask_c = np.zeros((P, T))
    mask_c[:, 3 * P:] = np.where(np.arange(P)[None, :] <= q, 0.0, MASKED)
    j, i = np.arange(4)[:, None], np.arange(4)[None, :]
    tri = np.broadcast_to((i < j).reshape(1, 16), (P, 16))
    t_all = (4 * np.arange(P)[None, :] + np.arange(4)[:, None]).reshape(-1)
    mask_d = np.full((P, 4, T + 2 * P), MASKED)
    for c in range(4):
        d = (4 * np.arange(P) + c)[:, None] - t_all[None, :]
        mask_d[:, c, :T] = np.where((d >= 0) & (d <= P), 0.0, MASKED)
        d = np.arange(P)[:, None] - np.arange(P)[None, :]
        mask_d[:, c, T:T + P] = np.where(d >= 0, 0.0, MASKED)
        mask_d[:, c, T + P:] = np.where((d >= 0) & (d % 4 == 0), 0.0, MASKED)
    inv = (np.float32(10000.0) ** (-np.arange(0, HD, 2, dtype=np.float32) / HD)).astype(np.float32)
    dcol = np.stack([inv[row % 32], sign[:, 0]], axis=1)
    w = np.array([2, 4, 8, 16])[:, None]
    cnt = np.broadcast_to((1.0 / np.minimum(np.arange(16)[None, :] + 1, w)).reshape(1, 64), (P, 64))
    f = lambda v: np.ascontiguousarray(v, dtype=np.float32)
    return dict(tab=f(tab).reshape(P, -1), tabc=f(tabc), mask_a=f(mask_a), mask_c=f(mask_c), tri=f(tri),
                ident=np.eye(P, dtype=np.float32), mask_d=f(mask_d).reshape(P, -1), dcol=f(dcol), p_cnt=f(cnt))


def lay_out(i):
    cat = np.concatenate
    out = first_constants()
    out["xT"] = tiles(i["x"][0].T)
    w_in, w_kr, w_vb, w_up, w_out = [], [], [], [], []
    for l in range(L):
        o = np.cumsum([0, 512, 128, 128, 256, 64, 64, 256, 64, 4, 256, 128, 32])
        aq, ak, av, bq, bk, bv, iq, ik, iw, cq, ckv, ckr = (i["w_in"][l][:, o[n]:o[n + 1]] for n in range(12))
        pair = [aq[:, 64 * h:64 * h + 64] for t in range(4) for h in (t, 4 + t)]
        w_in.append(columns(cat([cq, ckv, av] + pair + [ak, bq, bk, bk, iq, ik, ik], axis=1)))
        w_kr.append(tiles(cat([ckr, ckr[:, 16:], ckr[:, :16]], axis=1)))
        w_vb.append(tiles(cat([bv, iw], axis=1)))
        uq, ukv = i["w_uq"][l], i["w_ukv"][l]
        q = [tiles(cat([uq[:, 96 * h:96 * h + 96], uq[:, 96 * h + 80:96 * h + 96], uq[:, 96 * h + 64:96 * h + 80]], axis=1))
             for h in range(4)]
        k = [ukv[:, P * h:P * h + 64] for h in range(4)]
        v = [ukv[:, P * h + 64:P * h + P] for h in range(4)]
        w_up.append(cat(q + k + v, axis=1))
        wo = i["w_out"][l]
        rows = [wo[64 * h:64 * h + 64] for t in range(4) for h in (t, 4 + t)]
        w_out.append(columns(cat(rows + [wo[512:]], axis=0)))
    stack = lambda v: np.ascontiguousarray(np.stack(v))
    out["w_in"], out["w_out"] = np.concatenate(w_in), np.concatenate(w_out)
    out["w_kr"], out["w_vb"], out["w_up"] = stack(w_kr), stack(w_vb), stack(w_up)
    out["w_router"] = tiles(i["w_router"])
    out["rbias"] = i["router_bias"].reshape(1, E)
    out["nsink"] = i["attn_sinks"]
    cols = lambda v: v.reshape(-1, P).T
    out["c_g"] = stack([cat([cols(i["c_q_norm_g"][l]), cols(i["c_kv_norm_g"][l])], axis=1) for l in range(L)])
    out["ln"] = stack([cat([cols(i[n][l]) for n in ("ln1_g", "ln1_b", "ln2_g", "ln2_b")], axis=1) for l in range(L)])
    gu = stack([i["w_gate"], i["w_up"]]).reshape(2, L, E, KD, P, 2, P)
    out["w_gu"] = gu.transpose(1, 2, 5, 0, 4, 3, 6).reshape(-1, P, D)
    dn = i["w_down"].reshape(L, 4, 8, P, KD, P)
    out["w_dn"] = dn.transpose(0, 1, 4, 3, 2, 5).reshape(-1, P, 8 * P)
    out["ngain"] = cat([cols(g) for g in i["norm_gain_2"].reshape(12, D)] + [cols(i["kv_norm_gain_2"])], axis=1)
    F = i["ffn_w_gate_2"].shape[-1]
    gu = stack([i["ffn_w_gate_2"], i["ffn_w_up_2"]]).reshape(2, 4, KD, P, F // P, P)
    out["f_gu"] = gu.transpose(1, 4, 0, 3, 2, 5).reshape(-1, P, D)
    dn = i["ffn_w_down_2"].reshape(4, 2, GK, P, KD, P)
    out["f_dn"] = dn.transpose(0, 1, 4, 3, 2, 5).reshape(-1, P, GK * P)
    out["next_in"] = cat([out["w_in"][15:17], out["f_gu"][0:2]])
    out["p_in"], out["p_out"] = columns(i["pool_w_in_2"][0]), columns(i["pool_w_out_2"][0])
    out["p_grp"] = np.concatenate([columns(g) for g in i["pool_w_group_2"][0]])
    out["p_scale"] = cols(i["pool_scale_2"][0])
    pairs = lambda w: [w[:, 512 * g + P * p:512 * g + P * p + P] for p in range(4) for g in range(3)]
    q, k, v = pairs(i["attn_w_q_2"][0]), pairs(i["w_k_2"]), pairs(i["w_v_2"])
    out["d_qk"] = stack([tiles(w) for p in range(4) for w in q[3 * p:3 * p + 3] + k[3 * p:3 * p + 3]])
    out["d_v"] = stack([tiles(w) for w in v])
    out["d_out"] = columns(i["attn_w_o_2"][0])
    out["pos"] = i["positions_2"].reshape(P, 4).T.reshape(1, T).astype(np.int32)
    return {n: np.ascontiguousarray(v) for n, v in out.items()}


def kernel(**inputs):
    import concourse.bacc as bacc
    from concourse.bass_utils import run_bass_kernel_spmd

    nc = bacc.Bacc("TRN2", target_bir_lowering=False, num_devices=1)
    arrays = lay_out({n: np.asarray(v) for n, v in inputs.items()})
    args = {n: nc.dram_tensor(f"in_{n}", v.shape, mybir.dt.from_np(v.dtype), kind="ExternalInput").ap()
            for n, v in arrays.items()}
    out = nc.dram_tensor("out_hT", (P, KD * T), F32, kind="ExternalOutput").ap()
    build_program(nc, args, out)
    r = run_bass_kernel_spmd(nc, [{f"in_{n}": v for n, v in arrays.items()}], core_ids=[0])
    got = np.asarray(r.results[0]["out_hT"])
    return got.reshape(P, KD, T).transpose(2, 1, 0).reshape(1, T, D)
```
